# Optimizing a Trainium2 kernel written in Bass

```python
import math
import jax, jax.numpy as jnp
from jax import lax
import numpy as np

D_MODEL = 1024
BATCH = 1
SEQ = 2048
DEPTH = 1

PLE_DIM = 256
MIX_WIDTH = D_MODEL
HGRN_WIDTH = MIX_WIDTH // 2
HGRN_KEY_DIM = 128
HGRN_HEADS = HGRN_WIDTH // HGRN_KEY_DIM
HGRN_VAL_DIM = HGRN_WIDTH // HGRN_HEADS
HGRN_CHUNK = 64
DIFF_WIDTH = MIX_WIDTH - HGRN_WIDTH
DIFF_VAL_DIM = 128
DIFF_HEADS = DIFF_WIDTH // DIFF_VAL_DIM
DIFF_HEAD_DIM = DIFF_VAL_DIM // 2
Q_BLOCK = 128
IN_COLS = 4 * HGRN_WIDTH + 3 * DIFF_WIDTH
SPLITS = (HGRN_WIDTH, 2 * HGRN_WIDTH, 3 * HGRN_WIDTH, 4 * HGRN_WIDTH,
          4 * HGRN_WIDTH + DIFF_WIDTH, 4 * HGRN_WIDTH + 2 * DIFF_WIDTH)
N_EXPERTS = 16
N_GROUPS = 4
EXPERTS_PER_GROUP = N_EXPERTS // N_GROUPS
TOP_K = 2
D_FF_EXPERT = D_MODEL // 2
MOE_BLOCK = 128
EPS = 1e-6
MIN_FORGET = 1e-6
MASK_VALUE = -1e30

kernel_name = "hymba_hgrn2_diffattn_grouped_moe_ple"

def rms_norm(x, gain):
    xf = x.astype(jnp.float32)
    y = xf * lax.rsqrt(jnp.mean(xf * xf, axis=-1, keepdims=True) + EPS)
    return (y * gain.astype(jnp.float32)).astype(x.dtype)

def hgrn2_mixer(zq, zf, zi, zg, lb, out_gain):
    b, s, _ = zq.shape
    shp = (b, s, HGRN_HEADS, HGRN_KEY_DIM)
    q = jax.nn.silu(zq.astype(jnp.float32)).reshape(shp)
    f_logit = zf.astype(jnp.float32).reshape(shp)
    lb = lb.reshape(HGRN_HEADS, HGRN_KEY_DIM)
    forget = lb + (1.0 - lb) * jax.nn.sigmoid(f_logit)
    log_f = jnp.log(jnp.maximum(forget, MIN_FORGET))
    k = (1.0 - lb) * jax.nn.sigmoid(-f_logit)
    v = zi.astype(jnp.float32).reshape(b, s, HGRN_HEADS, HGRN_VAL_DIM)
    n_chunks = s // HGRN_CHUNK

    def to_chunks(t):
        return t.reshape(b, n_chunks, HGRN_CHUNK, HGRN_HEADS, t.shape[-1]).transpose(1, 0, 3, 2, 4)

    causal = jnp.tril(jnp.ones((HGRN_CHUNK, HGRN_CHUNK), dtype=bool))[:, :, None]

    def chunk_step(state, inp):
        qc, kc, vc, lfc = inp
        cum = jnp.cumsum(lfc, axis=2)
        o_inter = jnp.einsum("bhtd,bhdv->bhtv", qc * jnp.exp(cum), state)
        rel = jnp.where(causal, cum[:, :, :, None, :] - cum[:, :, None, :, :], MASK_VALUE)
        decay = jnp.where(causal, jnp.exp(rel), 0.0)
        scores = jnp.einsum("bhtd,bhsd,bhtsd->bhts", qc, kc, decay)
        o = o_inter + jnp.einsum("bhts,bhsv->bhtv", scores, vc)
        last = cum[:, :, -1:, :]
        state = (jnp.exp(last[:, :, 0, :])[..., None] * state
                 + jnp.einsum("bhsd,bhsv->bhdv", kc * jnp.exp(last - cum), vc))
        return state, o

    state0 = jnp.zeros((b, HGRN_HEADS, HGRN_KEY_DIM, HGRN_VAL_DIM), jnp.float32)
    _, o = lax.scan(chunk_step, state0,
                    (to_chunks(q), to_chunks(k), to_chunks(v), to_chunks(log_f)))
    o = o.transpose(1, 0, 3, 2, 4).reshape(b, s, HGRN_HEADS, HGRN_VAL_DIM)
    gate = jax.nn.silu(zg.astype(jnp.float32)).reshape(b, s, HGRN_HEADS, HGRN_VAL_DIM)
    o = rms_norm(o, out_gain) * gate
    return o.reshape(b, s, HGRN_WIDTH)

def diff_attention(zq, zk, zv, q_gain, k_gain, lam_q1, lam_k1, lam_q2, lam_k2, subln, lam_init):
    b, s, _ = zq.shape
    shp = (b, s, DIFF_HEADS, 2, DIFF_HEAD_DIM)
    q = rms_norm(zq.reshape(shp), q_gain).astype(jnp.float32) * (DIFF_HEAD_DIM ** -0.5)
    k = rms_norm(zk.reshape(shp), k_gain).astype(jnp.float32)
    v = zv.astype(jnp.float32).reshape(b, s, DIFF_HEADS, DIFF_VAL_DIM)
    lam = (jnp.exp(jnp.sum(lam_q1.astype(jnp.float32) * lam_k1.astype(jnp.float32)))
           - jnp.exp(jnp.sum(lam_q2.astype(jnp.float32) * lam_k2.astype(jnp.float32)))
           + lam_init)
    n_blocks = s // Q_BLOCK
    q_blocks = q.reshape(b, n_blocks, Q_BLOCK, DIFF_HEADS, 2, DIFF_HEAD_DIM).transpose(1, 0, 2, 3, 4, 5)
    key_pos = jnp.arange(s)

    def attend_block(args):
        qb, blk = args
        scores = jnp.einsum("bqhcd,bkhcd->bhcqk", qb, k)
        q_pos = blk * Q_BLOCK + jnp.arange(Q_BLOCK)
        mask = key_pos[None, :] <= q_pos[:, None]
        probs = jax.nn.softmax(jnp.where(mask, scores, MASK_VALUE), axis=-1)
        weights = probs[:, :, 0] - lam * probs[:, :, 1]
        return jnp.einsum("bhqk,bkhv->bqhv", weights, v)

    o = lax.map(attend_block, (q_blocks, jnp.arange(n_blocks)))
    o = o.transpose(1, 0, 2, 3, 4).reshape(b, s, DIFF_HEADS, DIFF_VAL_DIM)
    o = rms_norm(o, subln) * (1.0 - lam_init)
    return o.reshape(b, s, DIFF_WIDTH)

def grouped_moe(xn, w_router, w_gate, w_up, w_down):
    b, s, d = xn.shape
    t = b * s
    xt = xn.reshape(t, d)
    aff = jax.nn.softmax(xt.astype(jnp.float32) @ w_router.astype(jnp.float32), axis=-1)
    aff_g = aff.reshape(t, N_GROUPS, EXPERTS_PER_GROUP)
    group_score = lax.top_k(aff_g, TOP_K)[0].sum(-1)
    g_sel = jnp.argmax(group_score, axis=-1)
    in_group = jnp.take_along_axis(aff_g, g_sel[:, None, None], axis=1)[:, 0]
    top_w, top_local = lax.top_k(in_group, TOP_K)
    top_e = g_sel[:, None] * EXPERTS_PER_GROUP + top_local
    top_w = top_w / jnp.sum(top_w, axis=-1, keepdims=True)
    n_assign = t * TOP_K
    flat_e = top_e.reshape(n_assign)
    order = jnp.argsort(flat_e)
    sorted_e = flat_e[order]
    sorted_tok = (order // TOP_K).astype(jnp.int32)
    sorted_w = top_w.reshape(n_assign)[order]
    counts = jnp.bincount(flat_e, length=N_EXPERTS)
    starts = jnp.cumsum(counts) - counts
    padded = (counts + MOE_BLOCK - 1) // MOE_BLOCK * MOE_BLOCK
    padded_end = jnp.cumsum(padded)
    padded_start = padded_end - padded
    dest = padded_start[sorted_e] + jnp.arange(n_assign) - starts[sorted_e]
    n_rows = n_assign + N_EXPERTS * MOE_BLOCK
    n_blk = n_rows // MOE_BLOCK
    row_tok = jnp.full((n_rows,), t, jnp.int32).at[dest].set(sorted_tok)
    row_w = jnp.zeros((n_rows,), jnp.float32).at[dest].set(sorted_w)
    blk_e = jnp.minimum(jnp.searchsorted(padded_end, jnp.arange(n_blk) * MOE_BLOCK, side="right"),
                        N_EXPERTS - 1)
    x_rows = jnp.concatenate([xt, jnp.zeros((1, d), xt.dtype)], axis=0)[row_tok]
    x_rows = x_rows.reshape(n_blk, MOE_BLOCK, d)

    def expert_block(args):
        xb, e = args
        h = jax.nn.silu(xb @ w_gate[e]) * (xb @ w_up[e])
        return h @ w_down[e]

    y_rows = lax.map(expert_block, (x_rows, blk_e)).reshape(n_rows, d)
    y = jax.ops.segment_sum(y_rows * row_w[:, None].astype(y_rows.dtype), row_tok,
                            num_segments=t + 1)[:t]
    return y.reshape(b, s, d).astype(xn.dtype)

def setup_inputs(seed: int = 0) -> dict:
    key = jax.random.key(seed)
    ks = jax.random.split(key, 22)
    f32 = jnp.float32

    def nrm(k, shape, scale):
        return jax.random.normal(k, shape, f32) * scale

    def gain(k, shape):
        return 1.0 + 0.02 * jax.random.normal(k, shape, f32)

    res_scale = (2 * DEPTH) ** -0.5
    return {
        "x": nrm(ks[0], (BATCH, SEQ, D_MODEL), 1.0),
        "p": nrm(ks[1], (DEPTH, BATCH, SEQ, PLE_DIM), 1.0),
        "mix_norm": gain(ks[2], (DEPTH, D_MODEL)),
        "w_in": nrm(ks[3], (DEPTH, D_MODEL, IN_COLS), D_MODEL ** -0.5),
        "hgrn_lb": nrm(ks[4], (DEPTH, HGRN_WIDTH), 1.0),
        "hgrn_out_norm": gain(ks[5], (DEPTH, HGRN_VAL_DIM)),
        "q_norm": gain(ks[6], (DEPTH, DIFF_HEAD_DIM)),
        "k_norm": gain(ks[7], (DEPTH, DIFF_HEAD_DIM)),
        "lam_q1": nrm(ks[8], (DEPTH, DIFF_HEAD_DIM), 0.1),
        "lam_k1": nrm(ks[9], (DEPTH, DIFF_HEAD_DIM), 0.1),
        "lam_q2": nrm(ks[10], (DEPTH, DIFF_HEAD_DIM), 0.1),
        "lam_k2": nrm(ks[11], (DEPTH, DIFF_HEAD_DIM), 0.1),
        "diff_subln": gain(ks[12], (DEPTH, DIFF_VAL_DIM)),
        "w_out": nrm(ks[13], (DEPTH, MIX_WIDTH, D_MODEL), MIX_WIDTH ** -0.5 * res_scale),
        "ffn_norm": gain(ks[14], (DEPTH, D_MODEL)),
        "w_router": nrm(ks[15], (D_MODEL, N_EXPERTS), D_MODEL ** -0.5),
        "w_gate": nrm(ks[16], (DEPTH, N_EXPERTS, D_MODEL, D_FF_EXPERT), D_MODEL ** -0.5),
        "w_up": nrm(ks[17], (DEPTH, N_EXPERTS, D_MODEL, D_FF_EXPERT), D_MODEL ** -0.5),
        "w_down": nrm(ks[18], (DEPTH, N_EXPERTS, D_FF_EXPERT, D_MODEL), D_FF_EXPERT ** -0.5 * res_scale),
        "ple_proj": nrm(ks[19], (DEPTH, PLE_DIM, D_MODEL), PLE_DIM ** -0.5),
        "ple_norm": gain(ks[20], (DEPTH, D_MODEL)),
        "ple_gate": nrm(ks[21], (DEPTH, D_MODEL, D_MODEL), D_MODEL ** -0.5),
    }

def reference(x, p, mix_norm, w_in, hgrn_lb, hgrn_out_norm, q_norm, k_norm,
              lam_q1, lam_k1, lam_q2, lam_k2, diff_subln, w_out, ffn_norm, w_router,
              w_gate, w_up, w_down, ple_proj, ple_norm, ple_gate):
    lb_soft = jax.nn.softmax(hgrn_lb.astype(jnp.float32), axis=0)
    lower_bounds = jnp.cumsum(lb_soft, axis=0) - lb_soft[0]
    h = x
    for i in range(DEPTH):
        lam_init = 0.8 - 0.6 * math.exp(-0.3 * i)
        hn = rms_norm(h, mix_norm[i])
        z = hn @ w_in[i]
        zq, zf, zi, zg, dq, dk, dv = jnp.split(z, SPLITS, axis=-1)
        o_hgrn = hgrn2_mixer(zq, zf, zi, zg, lower_bounds[i], hgrn_out_norm[i])
        o_diff = diff_attention(dq, dk, dv, q_norm[i], k_norm[i], lam_q1[i], lam_k1[i],
                                lam_q2[i], lam_k2[i], diff_subln[i], lam_init)
        mix = jnp.concatenate([o_hgrn.astype(h.dtype), o_diff.astype(h.dtype)], axis=-1)
        h = h + mix @ w_out[i]
        h = h + grouped_moe(rms_norm(h, ffn_norm[i]), w_router, w_gate[i], w_up[i], w_down[i])
        ple = rms_norm(p[i] @ ple_proj[i], ple_norm[i])
        h = h + ple * jax.nn.sigmoid(h @ ple_gate[i])
    return h


_drawn_inputs = setup_inputs


def setup_inputs(seed=0):
    import zlib

    import numpy as np

    out = dict(_drawn_inputs(seed))
    spreads = {}
    factors = {'lam_k1': 14.012,
     'lam_q2': 14.128,
     'ple_norm': 21.498,
     'hgrn_out_norm': 4.666,
     'q_norm': 3.911,
     'k_norm': 4.181,
     'diff_subln': 4.582,
     'ffn_norm': 2.754}
    for name, (base, spread) in spreads.items():
        noise = np.random.default_rng([zlib.crc32(name.encode()), seed]).standard_normal(out[name].shape)
        drawn = base * np.exp(spread * noise) if base else spread * noise
        out[name] = __import__('jax').numpy.asarray(drawn.astype(out[name].dtype))
    for name, factor in factors.items():
        out[name] = (out[name] * factor).astype(out[name].dtype)
    return out
```

```python
from contextlib import ExitStack

import concourse.bass as bass
from concourse import mybir

F32 = mybir.dt.float32
F32R = mybir.dt.float32r
BF16 = mybir.dt.bfloat16
I32 = mybir.dt.int32

ALU = mybir.AluOpType
ACT = mybir.ActivationFunctionType
AX = mybir.AxisListType
P = 128

D = 1024
S = 2048
KD = D // P
NT = S // P
HW = 512
NH = HW // P
EPS = 1e-6


class Place:

    def __init__(self, nc, stack, stage):
        self.nc, self.stack, self.stage, self.sems, self.held = nc, stack, stage, [], None
        stack.callback(self.clear)

    def sb(self, name, shape, dt=F32):
        return self.stack.enter_context(self.nc.sbuf_tensor(f"{self.stage}_{name}", shape, dt))

    def ps(self, name, shape=(P, 512)):
        return self.stack.enter_context(self.nc.psum_tensor(f"{self.stage}_{name}", list(shape), F32))

    def clear(self):
        self.nc.clear_and_free_semaphores(self.sems)
        self.nc.all_engine_barrier()

    def hold(self, eng, sem, value):
        eng.wait_ge(sem, value)
        if not isinstance(value, int):
            if self.held is None:
                self.held = self.sem("held")
            eng.sem_inc(self.held, 1)

    def sem(self, name):
        self.sems.append(self.nc.alloc_semaphore(f"{self.stage}_{name}"))
        return self.sems[-1]


GT = 4
GW = GT * P
NG = NT // GT
SLICES = [(2 * HW, HW, "zi"), (3 * HW, HW, "zg"), (4 * HW, HW, "dq"), (5 * HW, HW, "dk"), (6 * HW, HW, "dv"),
          (0, HW, "zq"), (HW, HW // 2, "zf0"), (HW + HW // 2, HW // 2, "zf1")]
NSL = len(SLICES)


def project_in(nc, x, mix_norm, w_in, ident_in, hgrn_q, hgrn_f, hgrn_k, tok):
    groups = [[(s, j) for j in range(GT if s < 5 else w // P)] for s, (_, w, _) in enumerate(SLICES)]
    NGRP = sum(len(g) for g in groups)
    upto = [sum(len(g) for g in groups[:s + 1]) for s in range(NSL)]
    NST = 8
    with ExitStack() as stack:
        at = Place(nc, stack, "in")
        ident = at.sb("ident", [P, P])
        gain = at.sb("gain", [P, KD])
        eps = at.sb("eps", [P, 1])
        xs = at.sb("xs", [P, 2, D])
        xn = at.sb("xn", [P, D])
        ss = at.sb("ss", [P, GT])
        lnms = at.sb("lnms", [P, GT])
        rstd = at.sb("rstd", [P, GT])
        xT = at.sb("xT", [P, KD, GW])
        hhi = at.sb("hhi", [P, KD, GW], F32R)
        hlo = at.sb("hlo", [P, KD, GW], F32R)
        wraw = at.sb("wraw", [P, 2, KD, HW])
        whi = at.sb("whi", [P, 2, KD, HW], F32R)
        wlo = at.sb("wlo", [P, 2, KD, HW], F32R)
        st = at.sb("st", [P, NST, GW])
        psT = [at.ps(f"psT{i}") for i in range(2)]
        psM = [at.ps(f"psM{i}") for i in range(4)]
        NM = len(psM)

        consts_in = at.sem("consts_in")
        x_in = [at.sem(f"x_in{i}") for i in range(2)]
        w_in_sem = [at.sem(f"w_in{i}") for i in range(2)]
        eps_set = at.sem("eps_set")
        squares = at.sem("squares")
        logs = at.sem("logs")
        rstd_ok = at.sem("rstd_ok")
        xn_ok = at.sem("xn_ok")
        xT_ps = at.sem("xT_ps")
        xT_ok = at.sem("xT_ok")
        hi_ok = at.sem("hi_ok")
        lo_ok = at.sem("lo_ok")
        whi_ok = at.sem("whi_ok")
        wlo_ok = at.sem("wlo_ok")
        mm_ok = at.sem("mm_ok")
        sig_ok = at.sem("sig_ok")
        out_ok = at.sem("out_ok")
        out_ok2 = at.sem("out_ok2")
        stored = [at.sem(f"stored{i}") for i in range(NST)]

        stores = []
        for s in range(NSL):
            for (_, j) in groups[s]:
                n = upto[s] - len(groups[s]) + j
                for part in range(2 if s >= 6 else 1):
                    stores.append((s, j, n, part))
        NSTO = len(stores)
        slot = {(s, j, part): k % NST for k, (s, j, n, part) in enumerate(stores)}
        ordinal = {(s, j, part): k for k, (s, j, n, part) in enumerate(stores)}
        assert NSTO % NST == 0 and NGRP % NM == 0, (NSTO, NGRP)
        PER = NSTO // NST

        def x_row(g, t):
            return x[bass.ds((g * GT + t) * P, P), :]

        def by_vector(s, j):
            return s in (1, 5) or (s in (0, 2, 3, 4) and j % 2 == 0)

        order = {}
        nv = ns = 0
        for (s, j, n, part) in stores:
            if by_vector(s, j):
                nv += 1
                order[(s, j, part)] = (out_ok, nv)
            else:
                ns += 1
                order[(s, j, part)] = (out_ok2, ns)
        writer_total = {False: nv, True: ns}

        def writer(s, j, part):
            return order[(s, j, part)]

        def slot_free(eng, g, s, j, part):
            m = ordinal[(s, j, part)] // NST
            if not (isinstance(g, int) and g == 0 and m == 0):
                eng.wait_ge(stored[slot[(s, j, part)]], (g * PER + m) * 16)

        with nc.Block() as block:
            @block.sync
            def _(sp):
                sp.dma_start(ident[:], ident_in).then_inc(consts_in, 16)
                sp.dma_start(gain[:], mix_norm.rearrange("a (k p) -> p (a k)", p=P), allow_slow_non_contiguous=True).then_inc(consts_in, 16)

                def load_x(g, t, n):
                    sp.wait_ge(xn_ok, n - 1) if not isinstance(n, int) or n >= 2 else None
                    sp.dma_start(xs[:, t % 2, :], x_row(g, t)).then_inc(x_in[t % 2], 16)

                def load_w(g, s):
                    c0, w, _ = SLICES[s]
                    if not (isinstance(g, int) and g == 0 and s < 2):
                        sp.wait_ge(whi_ok, g * NSL + s - 1)
                        sp.wait_ge(wlo_ok, g * NSL + s - 1)
                    sp.dma_start(wraw[:, s % 2, :, 0:w], w_in[:, c0:c0 + w].rearrange("(k p) n -> p k n", p=P)) \
                        .then_inc(w_in_sem[s % 2], 16)

                for t in range(GT):
                    load_x(0, t, t)
                    if t == 1:
                        load_w(0, 0)
                for s in range(1, 3):
                    load_w(0, s)
                sp.wait_ge(xn_ok, GT)

                def group(g, last):
                    for s in range(3, NSL):
                        load_w(g, s)
                        if not last and s - 3 < GT:
                            load_x(g + 1, s - 3, (g + 1) * GT + s - 3)
                    if not last:
                        for s in range(3):
                            load_w(g + 1, s)

                group(0, False)
                with sp.Fori(1, NG - 1) as g:
                    group(g, False)
                group(NG - 1, True)

            @block.gpsimd
            def _(pool):
                def group(g):
                    for (s, j, n, part) in stores:
                        k = slot[(s, j, part)]
                        sem, cnt = writer(s, j, part)
                        at.hold(pool, sem, g * writer_total[sem is out_ok2] + cnt)
                        if s < 5:
                            dst = tok[bass.ds((g * GT + j) * P, P), s * HW:(s + 1) * HW]
                        elif s == 5:
                            dst = hgrn_q[j * P:(j + 1) * P, bass.ds(g * GW, GW)]
                        else:
                            r = (s - 6) * (HW // 2) + j * P
                            dst = (hgrn_f, hgrn_k)[part][r:r + P, bass.ds(g * GW, GW)]
                        pool.dma_start(dst, st[:, k, :]).then_inc(stored[k], 16)

                with pool.Fori(0, NG) as g:
                    group(g)
                for k in range(NST):
                    pool.wait_ge(stored[k], 16 * PER * NG)

            @block.scalar
            def _(act):
                def norm_stats(g, t):
                    n = g * GT + t
                    act.wait_ge(x_in[t % 2], (g * (GT // 2) + t // 2 + 1) * 16)
                    if not (isinstance(g, int) and g == 0 and t == 0):
                        act.wait_ge(xT_ps, n * 2)
                    act.activation(xn[:], xs[:, t % 2, :], ACT.Square, accum_out=ss[:, t:t + 1]).then_inc(squares, 1)
                    act.wait_ge(squares, n + 1)
                    act.activation(lnms[:, t:t + 1], ss[:, t:t + 1], ACT.Ln, bias=eps[:], scale=1.0 / D).then_inc(logs, 1)
                    act.wait_ge(logs, n + 1)
                    act.activation(rstd[:, t:t + 1], lnms[:, t:t + 1], ACT.Exp, scale=-0.5).then_inc(rstd_ok, 1)
                    act.wait_ge(rstd_ok, n + 1)
                    act.activation(xn[:], xs[:, t % 2, :], ACT.Copy, scale=rstd[:, t:t + 1]).then_inc(xn_ok, 1)

                def split_h(g, t):
                    act.wait_ge(xT_ok, (g * GT + t + 1) * 2)
                    if not (isinstance(g, int) and g == 0) and t == 0:
                        act.wait_ge(mm_ok, g * NGRP)
                    act.activation(hhi[:, :, t * P:(t + 1) * P], xT[:, :, t * P:(t + 1) * P], ACT.Copy).then_inc(hi_ok, 1)

                def split_w(g, s):
                    w = SLICES[s][1]
                    act.wait_ge(w_in_sem[s % 2], (g * (NSL // 2) + s // 2 + 1) * 16)
                    if not (isinstance(g, int) and g == 0 and s < 2):
                        before = g * NGRP + (upto[s - 2] if s >= 2 else upto[s - 2 + NSL] - NGRP)
                        act.wait_ge(mm_ok, before)
                    act.activation(whi[:, s % 2, :, 0:w], wraw[:, s % 2, :, 0:w], ACT.Copy).then_inc(whi_ok, 1)

                def evacuate(g, s):
                    for (_, j) in groups[s]:
                        n = upto[s] - len(groups[s]) + j
                        src = psM[n % NM]
                        if s in (1, 5):
                            act.wait_ge(mm_ok, g * NGRP + n + 1)
                            slot_free(act, g, s, j, 0)
                            act.activation(st[:, slot[(s, j, 0)], :], src[:], ACT.Sigmoid).then_inc(sig_ok, 1)
                        elif s >= 6:
                            act.wait_ge(mm_ok, g * NGRP + n + 1)
                            for part in range(2):
                                slot_free(act, g, s, j, part)
                                act.activation(st[:, slot[(s, j, part)], :], src[:], ACT.Sigmoid,
                                               scale=(1.0, -1.0)[part]).then_inc(out_ok2, 1)
                        elif not by_vector(s, j):
                            act.wait_ge(mm_ok, g * NGRP + n + 1)
                            slot_free(act, g, s, j, 0)
                            act.activation(st[:, slot[(s, j, 0)], :], src[:], ACT.Copy).then_inc(out_ok2, 1)

                act.wait_ge(eps_set, 1)
                for t in range(GT):
                    norm_stats(0, t)
                split_w(0, 0)

                def body(g, last):
                    for t in range(GT):
                        split_h(g, t)
                    for s in range(NSL):
                        if s + 1 < NSL:
                            split_w(g, s + 1)
                        elif not last:
                            split_w(g + 1, 0)
                        if 2 <= s < 2 + GT and not last:
                            norm_stats(g + 1, s - 2)
                        evacuate(g, s)

                body(0, False)
                with act.Fori(1, NG - 1) as g:
                    body(g, False)
                body(NG - 1, True)

            @block.vector
            def _(dve):
                dve.memset(eps[:], EPS).then_inc(eps_set, 1)
                dve.wait_ge(consts_in, 32)

                def take_xT(g, t):
                    for half in range(2):
                        dve.wait_ge(xT_ps, (g * GT + t) * 2 + half + 1)
                        if not (isinstance(g, int) and g == 0) and t == 0 and half == 0:
                            dve.wait_ge(hi_ok, g * GT)
                            dve.wait_ge(lo_ok, g * GT)
                        k0 = half * KD // 2
                        dve.tensor_tensor(xT[:, k0:k0 + KD // 2, t * P:(t + 1) * P],
                                          psT[half][:].rearrange("p (k t) -> p k t", k=KD // 2),
                                          gain[:, k0:k0 + KD // 2].unsqueeze(2).to_broadcast([P, KD // 2, P]),
                                          ALU.mult).then_inc(xT_ok, 1)

                def split_h(g, t):
                    dve.wait_ge(hi_ok, g * GT + t + 1)
                    dve.tensor_tensor(hlo[:, :, t * P:(t + 1) * P], xT[:, :, t * P:(t + 1) * P],
                                      hhi[:, :, t * P:(t + 1) * P].bitcast(F32), ALU.subtract).then_inc(lo_ok, 1)

                def split_w(g, s):
                    w = SLICES[s][1]
                    dve.wait_ge(whi_ok, g * NSL + s + 1)
                    dve.tensor_tensor(wlo[:, s % 2, :, 0:w], wraw[:, s % 2, :, 0:w],
                                      whi[:, s % 2, :, 0:w].bitcast(F32), ALU.subtract).then_inc(wlo_ok, 1)

                def evacuate(g, s):
                    for (_, j) in groups[s]:
                        n = upto[s] - len(groups[s]) + j
                        src = psM[n % NM]
                        if s in (1, 5):
                            i = j if s == 1 else GT + j
                            dve.wait_ge(sig_ok, g * 2 * GT + i + 1)
                            o = st[:, slot[(s, j, 0)], :]
                            dve.tensor_tensor(o, src[:], o, ALU.mult).then_inc(out_ok, 1)
                        elif by_vector(s, j):
                            dve.wait_ge(mm_ok, g * NGRP + n + 1)
                            slot_free(dve, g, s, j, 0)
                            dve.tensor_copy(st[:, slot[(s, j, 0)], :], src[:]).then_inc(out_ok, 1)

                for t in range(GT):
                    take_xT(0, t)
                split_w(0, 0)

                def body(g, last):
                    for t in range(GT):
                        split_h(g, t)
                    for s in range(NSL):
                        if s + 1 < NSL:
                            split_w(g, s + 1)
                        elif not last:
                            split_w(g + 1, 0)
                        if 3 <= s < 3 + GT and not last:
                            take_xT(g + 1, s - 3)
                        evacuate(g, s)

                body(0, False)
                with dve.Fori(1, NG - 1) as g:
                    body(g, False)
                body(NG - 1, True)

            @block.tensor
            def _(pe):
                pe.wait_ge(consts_in, 32)

                def transpose_x(g, t):
                    pe.wait_ge(xn_ok, g * GT + t + 1)
                    for half in range(2):
                        if not (isinstance(g, int) and g == 0 and t == 0):
                            pe.wait_ge(xT_ok, (g * GT + t) * 2 - 1 + half)
                        for i in range(KD // 2):
                            k = half * KD // 2 + i
                            last = pe.transpose(psT[half][:, i * P:(i + 1) * P], xn[:, k * P:(k + 1) * P], ident[:])
                        last.then_inc(xT_ps, 1)

                def bank_free(g, s, j):
                    n = upto[s] - len(groups[s]) + j - NM
                    back = n < 0
                    if back and isinstance(g, int) and g == 0:
                        return
                    if back:
                        n += NGRP
                    s2 = next(i for i in range(NSL) if n < upto[i])
                    j2 = n - (upto[s2] - len(groups[s2]))
                    sem, cnt = writer(s2, j2, 1 if s2 >= 6 else 0)
                    total = writer_total[sem is out_ok2]
                    pe.wait_ge(sem, g * total + (cnt - total if back else cnt))

                def multiply(g, s):
                    pe.wait_ge(wlo_ok, g * NSL + s + 1)
                    pe.wait_ge(whi_ok, g * NSL + s + 1)
                    b = s % 2
                    for (_, j) in groups[s]:
                        n = upto[s] - len(groups[s]) + j
                        if s == 0:
                            pe.wait_ge(hi_ok, g * GT + j + 1)
                            pe.wait_ge(lo_ok, g * GT + j + 1)
                        bank_free(g, s, j)
                        out = psM[n % NM][:]
                        cut = slice(j * P, (j + 1) * P)
                        for k in range(KD):
                            if s < 5:
                                three = ((hhi[:, k, cut], whi[:, b, k, :]), (hhi[:, k, cut], wlo[:, b, k, :]),
                                         (hlo[:, k, cut], whi[:, b, k, :]))
                            else:
                                three = ((whi[:, b, k, cut], hhi[:, k, :]), (whi[:, b, k, cut], hlo[:, k, :]),
                                         (wlo[:, b, k, cut], hhi[:, k, :]))
                            for i, (l, r) in enumerate(three):
                                last = pe.matmul(out, l, r, start=(k == 0 and i == 0), stop=(k == KD - 1 and i == 2))
                        last.then_inc(mm_ok, 1)

                for t in range(GT):
                    transpose_x(0, t)

                def body(g, last):
                    for s in range(NSL):
                        if 3 <= s < 3 + GT and not last:
                            transpose_x(g + 1, s - 3)
                        multiply(g, s)

                body(0, False)
                with pe.Fori(1, NG - 1) as g:
                    body(g, False)
                body(NG - 1, True)


CH = 64
MIN_FORGET = 1e-6
HALVES = (32, 16, 8, 4)
LV = 2 + len(HALVES)


def recurrence(nc, hgrn_q, hgrn_f, hgrn_k, tok, hgrn_lb, out_norm, ident_in, masks_in, resets_in, mix):
    with ExitStack() as stack:
        at = Place(nc, stack, "rec")
        ident = at.sb("ident", [P, P])
        masks = at.sb("masks", [P, LV, P], I32)
        resets = at.sb("resets", [P, NH * P])
        lb_in = at.sb("lb_in", [P, NH])
        lbs = at.sb("lbs", [P, 5, NH])
        gain = at.sb("gain", [P, P])
        eps = at.sb("eps", [P, 1])
        W4 = [P, 2, NH, P]
        q, f, k, v, g = (at.sb(n, W4) for n in ("q", "f", "k", "v", "g"))
        fm, fl, lf, cum = (at.sb(n, [P, NH, P]) for n in ("fm", "fl", "lf", "cum"))
        d64, dB = at.sb("d64", [P, NH, P]), at.sb("dB", [P, NH, P])
        dH = at.sb("dH", [P, len(HALVES), NH, P])
        e0, eK = at.sb("e0", [P, NH, P]), at.sb("eK", [P, NH, P])
        eH = at.sb("eH", [P, len(HALVES), NH, P])
        eBq, eBk = at.sb("eBq", [P, NH, P]), at.sb("eBk", [P, NH, P])
        ql = at.sb("ql", [P, 2, LV, NH, P])
        kl = at.sb("kl", [P, 2, LV, NH, P])
        qI, kD = at.sb("qI", W4), at.sb("kD", W4)
        eL = at.sb("eL", [P, 2, NH])
        sT = at.sb("sT", W4)
        kDT = at.sb("kDT", W4)
        state = at.sb("state", [P, 2, NH, P])
        osq = at.sb("osq", [P, NH, P])
        oss, oln, ors = (at.sb(n, [P, NH]) for n in ("oss", "oln", "ors"))
        gg = at.sb("gg", W4)
        on = at.sb("on", [P, NH, P])
        o = at.sb("o", W4)
        psA = [at.ps(f"psA{i}", (P, NH, P)) for i in range(3)]
        psK = at.ps("psK", (P, NH, P))
        psU = at.ps("psU", (P, NH, P))
        psO = [at.ps(f"psO{i}", (P, NH, P)) for i in range(2)]
        NA = len(psA)

        consts_in, init = at.sem("consts_in"), at.sem("init")
        lb_ok = at.sem("lb_ok")
        tile_in = [at.sem(f"tile_in{i}") for i in range(2)]
        names = ("fm_ok km_ok fl_ok0 fl_ok lf_ok cum_ok d64_ok dB_ok dH_ok e0_ok eK_ok eH_ok eB_ok q0_ok k0_ok qH_ok kH_ok qB_ok kB_ok "
                 "qI_ok kD_ok eL_ok qIc_ok kDc_ok kDT_ps kDT_ok lv_ps lv_ok upd_ps state_ok o_ps osq_ok oss_ok oln_ok ors_ok gg_ok on_ok o_ok").split()
        s = {n: at.sem(n) for n in names}
        stored = [at.sem(f"stored{i}") for i in range(2)]

        def later(t, n=1):
            return not isinstance(t, int) or t >= n

        def done(eng, name, t, n=1, per=1):
            if eng in (nc.sync, nc.gpsimd) or name == "lv_ps" and eng is nc.vector:
                at.hold(eng, s[name], t * per + n)
            else:
                eng.wait_ge(s[name], t * per + n)

        def second(x, H):
            return x.rearrange("p h (b t) -> p (h b) t", t=2 * H)[:, :, H:2 * H]

        def first_(x, H):
            return x.rearrange("p h (b t) -> p (h b) t", t=2 * H)[:, :, 0:H]

        def from_middle(x, H, at_):
            b = x.rearrange("p h (b t) -> p (h b) t", t=2 * H)
            return b, b[:, :, at_:at_ + 1].to_broadcast([P, NH * P // (2 * H), 2 * H])

        def tiles(eng, body):
            body(0, 0)
            body(1, 1)
            with eng.Fori(1, NT // 2) as pair:
                body(pair * 2, 0)
                body(pair * 2 + 1, 1)

        def staggered(eng, front, back):
            front(0, 0)
            front(1, 1)
            back(0, 0)
            with eng.Fori(1, NT // 2) as pair:
                front(pair * 2, 0)
                back(pair * 2 - 1, 1)
                front(pair * 2 + 1, 1)
                back(pair * 2, 0)
            back(NT - 1, 1)

        def psA_of(t, b, i):
            return psA[i % NA]

        with nc.Block() as block:
            @block.sync
            def _(sp):
                for dst, src in ((ident, ident_in), (masks, masks_in), (resets, resets_in)):
                    sp.dma_start(dst[:], src).then_inc(consts_in, 16)
                sp.dma_start(lb_in[:], hgrn_lb.rearrange("a (h d) -> d (a h)", d=P), allow_slow_non_contiguous=True).then_inc(consts_in, 16)
                sp.dma_start(gain[:], out_norm.broadcast_to([P, P])).then_inc(consts_in, 16)

                def load(t, b):
                    if later(t, 2):
                        done(sp, "lv_ps", t - 2, LV, LV)
                        done(sp, "fm_ok", t - 2)
                        done(sp, "o_ps", t - 2)
                        done(sp, "gg_ok", t - 2)
                    for dst, src in ((q, hgrn_q), (f, hgrn_f), (k, hgrn_k)):
                        sp.dma_start(dst[:, b], src.rearrange("(h d) t -> d h t", d=P)[:, :, bass.ds(t * P, P)]).then_inc(tile_in[b], 16)
                    for dst, c0 in ((v, 0), (g, HW)):
                        sp.dma_start(dst[:, b].rearrange("p h c -> p (h c)"), tok[bass.ds(t * P, P), c0:c0 + HW]).then_inc(tile_in[b], 16)

                tiles(sp, load)

            def tile_loaded(eng, t, b):
                at.hold(eng, tile_in[b], (t - b + 2) * 40)

            @block.gpsimd
            def _(pool):
                pool.wait_ge(lb_ok, 5)

                def front(t, b):
                    tile_loaded(pool, t, b)
                    if later(t):
                        done(pool, "fl_ok0", t - 1)
                    oml = lbs[:, 4].unsqueeze(2).to_broadcast([P, NH, P])
                    pool.tensor_tensor(fm[:], f[:, b], oml, ALU.mult).then_inc(s["fm_ok"], 1)
                    pool.tensor_tensor(k[:, b], k[:, b], oml, ALU.mult).then_inc(s["km_ok"], 1)
                    for i, H in enumerate(HALVES):
                        done(pool, "cum_ok", t)
                        if later(t):
                            done(pool, "eH_ok", t - 1, 2 * i + 2, 2 * len(HALVES))
                        a, m = from_middle(cum[:], H, H - 1)
                        pool.tensor_tensor(dH[:, i].rearrange("p h (b t) -> p (h b) t", t=2 * H), a, m, ALU.subtract).then_inc(s["dH_ok"], 1)
                    for i, H in enumerate(HALVES):
                        done(pool, "eH_ok", t, 2 * i + 2, 2 * len(HALVES))
                        done(pool, "km_ok", t)
                        if later(t, 2):
                            done(pool, "lv_ps", t - 2, LV, LV)
                        pool.tensor_tensor(first_(kl[:, b, 1 + i], H), first_(k[:, b], H), first_(eH[:, i], H), ALU.mult).then_inc(s["kH_ok"], 1)

                def back(t, b):
                    done(pool, "o_ok", t)
                    pool.dma_start(mix[bass.ds(t * P, P), 0:HW], o[:, b].rearrange("p h c -> p (h c)")).then_inc(stored[b], 16)

                staggered(pool, front, back)
                for b in range(2):
                    pool.wait_ge(stored[b], 16 * NT // 2)

            @block.scalar
            def _(act):
                act.preload_act_table_set("natural_log_exp_and_others")
                act.wait_ge(lb_ok, 1)
                act.activation(lbs[:, 1], lbs[:, 0], ACT.Exp).then_inc(lb_ok, 1)
                act.wait_ge(init, 1)

                def front(t, b):
                    done(act, "fl_ok", t)
                    if later(t):
                        done(act, "cum_ok", t - 1)
                    act.activation(lf[:], fl[:], ACT.Ln).then_inc(s["lf_ok"], 1)
                    done(act, "cum_ok", t)
                    if later(t):
                        done(act, "q0_ok", t - 1)
                        done(act, "kD_ok", t - 1)
                        done(act, "eL_ok", t - 1)
                        done(act, "qI_ok", t - 1)
                    act.activation(e0[:], cum[:], ACT.Exp).then_inc(s["e0_ok"], 1)
                    done(act, "d64_ok", t)
                    if later(t):
                        done(act, "k0_ok", t - 1)
                    act.activation(eK[:], d64[:], ACT.Exp).then_inc(s["eK_ok"], 1)
                    for i, H in enumerate(HALVES):
                        done(act, "dH_ok", t, i + 1, len(HALVES))
                        if later(t):
                            done(act, "qH_ok", t - 1, i + 1, len(HALVES))
                            done(act, "kH_ok", t - 1, i + 1, len(HALVES))
                        act.activation(second(eH[:, i], H), second(dH[:, i], H), ACT.Exp).then_inc(s["eH_ok"], 1)
                        act.activation(first_(eH[:, i], H), first_(dH[:, i], H), ACT.Exp, scale=-1.0).then_inc(s["eH_ok"], 1)
                    done(act, "dB_ok", t)
                    if later(t):
                        done(act, "qB_ok", t - 1)
                        done(act, "kB_ok", t - 1)
                    act.activation(eBq[:], dB[:], ACT.Exp).then_inc(s["eB_ok"], 1)
                    act.activation(eBk[:], dB[:], ACT.Exp, scale=-1.0).then_inc(s["eB_ok"], 1)
                    done(act, "q0_ok", t)
                    done(act, "k0_ok", t)
                    if later(t, 2):
                        done(act, "o_ps", t - 2)
                        done(act, "kDT_ps", t - 2)
                    act.activation(qI[:, b, :, 0:CH], ql[:, b, 0, :, 0:CH], ACT.Copy).then_inc(s["qIc_ok"], 1)
                    act.activation(kD[:, b, :, CH:P], kl[:, b, 0, :, CH:P], ACT.Copy).then_inc(s["kDc_ok"], 1)

                def back(t, b):
                    done(act, "kDT_ps", t)
                    if later(t, 2):
                        done(act, "upd_ps", t - 2)
                    act.activation(kDT[:, b], psK[:], ACT.Copy).then_inc(s["kDT_ok"], 1)
                    done(act, "o_ps", t)
                    if later(t):
                        done(act, "oss_ok", t - 1)
                    act.activation(osq[:], psO[b][:], ACT.Square).then_inc(s["osq_ok"], 1)
                    done(act, "oss_ok", t)
                    act.activation(oln[:], oss[:], ACT.Ln, bias=eps[:], scale=1.0 / P).then_inc(s["oln_ok"], 1)
                    done(act, "oln_ok", t)
                    if later(t):
                        done(act, "on_ok", t - 1)
                    act.activation(ors[:], oln[:], ACT.Exp, scale=-0.5).then_inc(s["ors_ok"], 1)

                staggered(act, front, back)

            @block.vector
            def _(dve):
                for n, (x, val) in enumerate(((eps[:], EPS), (state[:, 1], 0.0), (sT[:], 0.0), (ql[:], 0.0), (kl[:], 0.0))):
                    dve.memset(x, val).then_inc(init, 1)
                dve.wait_ge(consts_in, 80)
                dve.wait_ge(init, 5)
                dve.tensor_tensor(lbs[:, 0], lb_in[:], lb_in[:], ALU.subtract).then_inc(lb_ok, 1)
                dve.wait_ge(lb_ok, 2)
                dve.reciprocal(lbs[:, 2], lbs[:, 1]).then_inc(lb_ok, 1)
                dve.wait_ge(lb_ok, 3)
                dve.tensor_tensor(lbs[:, 2], lbs[:, 1], lbs[:, 2], ALU.mult).then_inc(init, 1)
                dve.wait_ge(init, 6)
                dve.tensor_tensor(lbs[:, 3], lbs[:, 2], lbs[:, 2], ALU.subtract).then_inc(lb_ok, 1)
                dve.wait_ge(lb_ok, 4)
                dve.tensor_scalar(lbs[:, 4], lbs[:, 3], -1.0, 1.0, ALU.mult, ALU.add).then_inc(lb_ok, 1)

                def front(t, b):
                    tile_loaded(dve, t, b)
                    done(dve, "fm_ok", t)
                    if later(t):
                        done(dve, "lf_ok", t - 1)
                    dve.tensor_tensor(fl[:], fm[:], lbs[:, 3].unsqueeze(2).to_broadcast([P, NH, P]), ALU.add).then_inc(s["fl_ok0"], 1)
                    done(dve, "fl_ok0", t)
                    dve.tensor_scalar(fl[:], fl[:], MIN_FORGET, None, ALU.max).then_inc(s["fl_ok"], 1)
                    done(dve, "lf_ok", t)
                    if later(t):
                        done(dve, "dH_ok", t - 1, len(HALVES), len(HALVES))
                        done(dve, "e0_ok", t - 1)
                        done(dve, "dB_ok", t - 1)
                    dve.tensor_tensor_scan(cum[:].rearrange("p h t -> p (h t)"), resets[:], lf[:].rearrange("p h t -> p (h t)"),
                                           0.0, ALU.mult, ALU.add).then_inc(s["cum_ok"], 1)
                    done(dve, "cum_ok", t)
                    if later(t):
                        done(dve, "eK_ok", t - 1)
                        done(dve, "eB_ok", t - 1, 2, 2)
                    a, m = from_middle(cum[:], CH // 2, CH - 1)
                    dve.tensor_tensor(d64[:].rearrange("p h (b t) -> p (h b) t", t=CH), m, a, ALU.subtract).then_inc(s["d64_ok"], 1)
                    a, m = from_middle(cum[:], 2, 1)
                    dve.tensor_tensor(dB[:].rearrange("p h (b t) -> p (h b) t", t=4), a, m, ALU.subtract).then_inc(s["dB_ok"], 1)
                    done(dve, "e0_ok", t)
                    if later(t, 2):
                        done(dve, "lv_ps", t - 2, LV, LV)
                    dve.tensor_tensor(ql[:, b, 0], q[:, b], e0[:], ALU.mult).then_inc(s["q0_ok"], 1)
                    done(dve, "eK_ok", t)
                    done(dve, "km_ok", t)
                    dve.tensor_tensor(kl[:, b, 0], k[:, b], eK[:], ALU.mult).then_inc(s["k0_ok"], 1)
                    if later(t, 2):
                        done(dve, "state_ok", t - 2)
                        done(dve, "o_ps", t - 2)
                        done(dve, "kDT_ps", t - 2)
                    dve.tensor_tensor(eL[:, b], e0[:, :, CH - 1], e0[:, :, P - 1], ALU.mult).then_inc(s["eL_ok"], 1)
                    done(dve, "k0_ok", t)
                    dve.tensor_tensor(qI[:, b, :, CH:P], ql[:, b, 0, :, CH:P], e0[:, :, CH - 1:CH].to_broadcast([P, NH, CH]), ALU.mult).then_inc(s["qI_ok"], 1)
                    dve.tensor_tensor(kD[:, b, :, 0:CH], kl[:, b, 0, :, 0:CH], e0[:, :, P - 1:P].to_broadcast([P, NH, CH]), ALU.mult).then_inc(s["kD_ok"], 1)
                    for i, H in enumerate(HALVES):
                        done(dve, "eH_ok", t, 2 * i + 1, 2 * len(HALVES))
                        dve.tensor_tensor(second(ql[:, b, 1 + i], H), second(q[:, b], H), second(eH[:, i], H), ALU.mult).then_inc(s["qH_ok"], 1)
                    done(dve, "eB_ok", t, 2, 2)
                    dve.tensor_tensor(ql[:, b, LV - 1], q[:, b], eBq[:], ALU.mult).then_inc(s["qB_ok"], 1)
                    dve.tensor_tensor(kl[:, b, LV - 1], k[:, b], eBk[:], ALU.mult).then_inc(s["kB_ok"], 1)
                    if later(t, 2):
                        done(dve, "o_ok", t - 2)
                    dve.tensor_tensor(gg[:, b], g[:, b], gain[:].unsqueeze(1).to_broadcast([P, NH, P]), ALU.mult).then_inc(s["gg_ok"], 1)

                def back(t, b):
                    if later(t, 2):
                        done(dve, "o_ps", t - 2)
                    for i in range(LV):
                        if i or later(t):
                            done(dve, "lv_ok", t, i, LV)
                        done(dve, "lv_ps", t, i + 1, LV)
                        dve.copy_predicated(sT[:, b], masks[:, i].unsqueeze(1).to_broadcast([P, NH, P]), psA_of(t, b, i)[:]).then_inc(s["lv_ok"], 1)
                    done(dve, "upd_ps", t)
                    if later(t):
                        done(dve, "o_ps", t - 1)
                    for h in range(NH):
                        last = dve.scalar_tensor_tensor(state[:, b, h], state[:, 1 - b, h], eL[:, b, h:h + 1], psU[:, h],
                                                        ALU.mult, ALU.add)
                    last.then_inc(s["state_ok"], 1)
                    done(dve, "osq_ok", t)
                    if later(t):
                        done(dve, "oln_ok", t - 1)
                    dve.tensor_reduce(oss[:], osq[:], AX.X, ALU.add).then_inc(s["oss_ok"], 1)
                    done(dve, "ors_ok", t)
                    dve.tensor_tensor(on[:], psO[b][:], ors[:].unsqueeze(2).to_broadcast([P, NH, P]), ALU.mult).then_inc(s["on_ok"], 1)
                    done(dve, "on_ok", t)
                    if later(t, 2):
                        dve.wait_ge(stored[b], (t - b) * 8)
                    dve.tensor_tensor(o[:, b], on[:], gg[:, b], ALU.mult).then_inc(s["o_ok"], 1)

                staggered(dve, front, back)

            @block.tensor
            def _(pe):
                pe.wait_ge(consts_in, 80)
                pe.wait_ge(init, 5)

                def tile(t, b):
                    done(pe, "kD_ok", t)
                    done(pe, "kDc_ok", t)
                    if later(t):
                        done(pe, "kDT_ok", t - 1)
                    for h in range(NH):
                        last = pe.transpose(psK[:, h], kD[:, b, h], ident[:])
                    last.then_inc(s["kDT_ps"], 1)
                    for i in range(LV):
                        if i == 0:
                            done(pe, "k0_ok", t)
                        elif i < LV - 1:
                            done(pe, "qH_ok", t, i, len(HALVES))
                            done(pe, "kH_ok", t, i, len(HALVES))
                        else:
                            done(pe, "kB_ok", t)
                        if i >= NA:
                            done(pe, "lv_ok", t, i - NA + 1, LV)
                        elif later(t):
                            done(pe, "lv_ok", t - 1, LV, LV)
                        for h in range(NH):
                            last = pe.matmul(psA_of(t, b, i)[:, h], kl[:, b, i, h], ql[:, b, i, h], start=True, stop=True)
                        last.then_inc(s["lv_ps"], 1)
                    done(pe, "kDT_ok", t)
                    if later(t):
                        done(pe, "state_ok", t - 1)
                    for h in range(NH):
                        last = pe.matmul(psU[:, h], kDT[:, b, h], v[:, b, h], start=True, stop=True)
                    last.then_inc(s["upd_ps"], 1)
                    done(pe, "lv_ok", t, LV, LV)
                    done(pe, "qI_ok", t)
                    done(pe, "qIc_ok", t)
                    if later(t, 2):
                        done(pe, "on_ok", t - 2)
                    for h in range(NH):
                        pe.matmul(psO[b][:, h], qI[:, b, h], state[:, 1 - b, h], start=True, stop=False)
                        last = pe.matmul(psO[b][:, h], sT[:, b, h], v[:, b, h], start=False, stop=True)
                    last.then_inc(s["o_ps"], 1)

                tiles(pe, tile)


HD = 64
CK = 512
LAM_INIT = 0.8 - 0.6 * 1.0


def attention(nc, tok, q_norm, k_norm, lam_q1, lam_k1, lam_q2, lam_k2, subln, ident_in, causal_in, mix):
    units = [[min(CK, (i + 1) * P - j * CK) for j in range(i // 4 + 1)] for i in range(NT)]
    first = [sum(len(u) for u in units[:i]) for i in range(NT)]
    CH = sum(len(u) for u in units)
    NPREP = 2 * 2 * (S // CK)
    with ExitStack() as stack:
        at = Place(nc, stack, "att")
        ident = at.sb("ident", [P, P])
        ident_bf = at.sb("ident_bf", [P, P], BF16)
        causal_f = at.sb("causal_f", [P, P])
        causal = at.sb("causal", [P, P], BF16)
        gcol = at.sb("gcol", [P, 2])
        gain = at.sb("gain", [P, P])
        lam_in = at.sb("lam_in", [P, 4, HD])
        lam_pr = at.sb("lam_pr", [P, 2, HD])
        lam_s = at.sb("lam_s", [P, 4])
        lamvec = at.sb("lamvec", [P, 2])
        eps = at.sb("eps", [P, 1])
        qk = at.sb("qk", [P, 2, NT, P])
        v = at.sb("v", [P, 2, NT, P])
        sq = at.sb("sq", [P, NT, P])
        ms = at.sb("ms", [P, 2, 2 * NT])
        lnm = at.sb("lnm", [P, 2, 2 * NT])
        rs = at.sb("rs", [P, 2, 2 * NT])
        dup = at.sb("dup", [P, 2, NT, 2, 2, HD])
        qs = at.sb("qs", [P, 2, S], F32R)
        khi = at.sb("khi", [P, 2, S], F32R)
        klo = at.sb("klo", [P, 2, S], F32R)
        pr = at.sb("pr", [P, 2, 2, S])
        wT = at.sb("wT", [P, 2, 4, P])
        nm = at.sb("nm", [P, 2, 2, 4])
        sums = at.sb("sums", [P, 2, 2, 4])
        low = at.sb("low", [P, 2])
        dlt = at.sb("dlt", [P, 2, 4])
        ex = at.sb("ex", [P, 2, 4])
        exs = at.sb("exs", [P, 2, 4])
        tot = at.sb("tot", [P, 2])
        inv = at.sb("inv", [P, 2])
        invl = at.sb("invl", [P, 2])
        coef = at.sb("coef", [P, 2, 2, 4])
        o = at.sb("o", [P, NT, P])
        oss = at.sb("oss", [P, NT])
        oln = at.sb("oln", [P, NT])
        ors = at.sb("ors", [P, NT])
        psS = [at.ps(f"psS{i}", (P, 2, CK)) for i in range(2)]
        psW = [at.ps(f"psW{i}") for i in range(2)]
        psO = [at.ps(f"psO{i}") for i in range(2)]

        consts_in = at.sem("consts_in")
        eps_set = at.sem("eps_set")
        mask_ok = at.sem("mask_ok")
        lam_ok = at.sem("lam_ok")
        qk_in = at.sem("qk_in")
        v_in = [at.sem(f"v_in{i}") for i in range(2)]
        sq_ok = at.sem("sq_ok")
        ms_ok = at.sem("ms_ok")
        lnm_ok = at.sem("lnm_ok")
        rs_ok = at.sem("rs_ok")
        dup_ok = [at.sem("dupq_ok"), at.sem("dupk_ok")]
        prep_ps = at.sem("prep_ps")
        prep_hi = at.sem("prep_hi")
        prep_lo = at.sem("prep_lo")
        score_ps = at.sem("score_ps")
        max_ok = at.sem("max_ok")
        exp_ok = at.sem("exp_ok")
        stat_ok = at.sem("stat_ok")
        ex_ok = at.sem("ex_ok")
        scaled = at.sem("scaled")
        comb_ok = at.sem("comb_ok")
        wT_ps = at.sem("wT_ps")
        wT_ok = at.sem("wT_ok")
        pv_ok = at.sem("pv_ok")
        o_ok = at.sem("o_ok")
        fin = at.sem("fin")
        lnm2 = at.sem("lnm2")
        dl_ok = at.sem("dl_ok")
        gain_ok = at.sem("gain_ok")
        steps = at.sem("steps")
        STEPS = sum(1 if len(u) == 1 else 5 for u in units)
        stored = at.sem("stored")

        def later(h, n=1):
            return not isinstance(h, int) or h >= n

        def head_cols(part, h):
            c0 = (2 + part) * HW
            return tok[:, bass.ds(h * P + c0, P)].rearrange("(t p) c -> p t c", p=P)

        with nc.Block() as block:
            @block.sync
            def _(sp):
                for dst, src in ((ident, ident_in), (causal_f, causal_in)):
                    sp.dma_start(dst[:], src).then_inc(consts_in, 16)
                for i, g in enumerate((q_norm, k_norm)):
                    for c in range(2):
                        sp.dma_start(gcol[c * HD:(c + 1) * HD, i:i + 1], g.rearrange("a d -> d a"),
                                     allow_slow_non_contiguous=True).then_inc(consts_in, 16)
                for i, l in enumerate((lam_q1, lam_q2, lam_k1, lam_k2)):
                    sp.dma_start(lam_in[:, i, :], l.broadcast_to([P, HD])).then_inc(consts_in, 16)
                sp.dma_start(gain[:], subln.broadcast_to([P, P])).then_inc(consts_in, 16)

                def load(h, par):
                    if later(h):
                        sp.wait_ge(dup_ok[0], h)
                        sp.wait_ge(dup_ok[1], h)
                    for i in range(2):
                        sp.dma_start(qk[:, i], head_cols(i, h)).then_inc(qk_in, 16)
                    if later(h, 2):
                        sp.wait_ge(pv_ok, (h - 1) * CH)
                    sp.dma_start(v[:, par], head_cols(2, h)).then_inc(v_in[par], 16)

                load(0, 0)
                load(1, 1)
                with sp.Fori(1, NH // 2) as pair:
                    load(pair * 2, 0)
                    load(pair * 2 + 1, 1)

            @block.gpsimd
            def _(pool):
                def head(h):
                    pool.wait_ge(qk_in, (h + 1) * 32)
                    pool.wait_ge(rs_ok, h + 1)
                    if later(h):
                        pool.wait_ge(prep_ps, h * NPREP)
                    pool.tensor_tensor(dup[:, 0].rearrange("p t c u d -> p (t c) u d"),
                                       qk[:, 0].rearrange("p t (c d) -> p (t c) d", c=2).unsqueeze(2).to_broadcast([P, 2 * NT, 2, HD]),
                                       rs[:, 0].unsqueeze(2).unsqueeze(3).to_broadcast([P, 2 * NT, 2, HD]),
                                       ALU.mult).then_inc(dup_ok[0], 1)
                    for i in range(NT):
                        at.hold(pool, stat_ok, h * NT + i + 1)
                        for j, w in enumerate(units[i]):
                            pool.tensor_scalar(pr[:, i % 2, 1, j * CK:j * CK + w], pr[:, i % 2, 1, j * CK:j * CK + w],
                                               coef[:, i % 2, 1, j:j + 1], None, ALU.mult).then_inc(scaled, 1)
                    at.hold(pool, fin, (h + 1) * 5)
                    pool.dma_start(mix[:, bass.ds(h * P + HW, P)].rearrange("(t p) c -> p t c", p=P), o[:]).then_inc(stored, 16)

                head(0)
                with pool.Fori(1, NH) as h:
                    head(h)
                pool.wait_ge(stored, 16 * NH)

            @block.scalar
            def _(act):
                act.wait_ge(eps_set, 1)
                act.wait_ge(lam_ok, 2)
                act.activation(lam_s[:, 2:4], lam_s[:, 0:2], ACT.Exp).then_inc(lam_ok, 1)

                def head(h):
                    for i in range(2):
                        act.wait_ge(qk_in, (h + 1) * 32)
                        if i or later(h):
                            act.wait_ge(ms_ok, h * 2 + i)
                        act.activation(sq[:], qk[:, i], ACT.Square).then_inc(sq_ok, 1)
                    act.wait_ge(ms_ok, h * 2 + 2)
                    act.activation(lnm[:], ms[:], ACT.Ln, bias=eps[:], scale=1.0 / HD).then_inc(lnm_ok, 1)
                    act.wait_ge(lnm_ok, h + 1)
                    act.activation(rs[:], lnm[:], ACT.Exp, scale=-0.5).then_inc(rs_ok, 1)
                    for n in range(NPREP):
                        i, c, a = n // (NPREP // 2), n // (NPREP // 4) % 2, n % (S // CK)
                        act.wait_ge(prep_ps, h * NPREP + n + 1)
                        if n == 0:
                            pass
                        act.activation((qs, khi)[i][:, c, a * CK:(a + 1) * CK], psW[n % 2][:], ACT.Copy,
                                       scale=gcol[:, i:i + 1]).then_inc(prep_hi, 1)
                    for i in range(NT + 1):
                        if i < NT:
                            for j, w in enumerate(units[i]):
                                n = first[i] + j
                                act.wait_ge(max_ok, h * CH + n + 1)
                                if i >= 2 or later(h):
                                    m = h * NT + i - 1
                                    prev = h * CH + (first[i - 2] + len(units[i - 2]) if i >= 2 else first[NT - 2 + i] + len(units[NT - 2 + i]) - CH)
                                    act.wait_ge(wT_ps, prev)
                                for c in range(2):
                                    act.activation(pr[:, i % 2, c, j * CK:j * CK + w], psS[n % 2][:, c, 0:w], ACT.Exp,
                                                   bias=nm[:, i % 2, c, j:j + 1],
                                                   accum_out=sums[:, i % 2, c, j:j + 1]).then_inc(exp_ok, 1)
                        if i >= 1:
                            for j, w in enumerate(units[i - 1]):
                                n = first[i - 1] + j
                                act.wait_ge(wT_ps, h * CH + n + 1)
                                if n >= 2 or later(h):
                                    act.wait_ge(pv_ok, h * CH + n - 1)
                                act.activation(wT[:, n % 2, 0:w // P, :], psW[n % 2][:, 0:w].rearrange("p (k q) -> p k q", q=P),
                                               ACT.Copy).then_inc(wT_ok, 1)
                            act.wait_ge(pv_ok, h * CH + first[i - 1] + len(units[i - 1]))
                            if i == 1 and later(h):
                                act.wait_ge(stored, h * 16)
                            act.activation(o[:, i - 1, :], psO[(i - 1) % 2][:, 0:P], ACT.Copy).then_inc(o_ok, 1)
                        if i < NT and len(units[i]) > 1:
                            act.wait_ge(dl_ok, h * (NT - 4) + i - 3)
                            nj = len(units[i])
                            act.activation(ex[:, :, 0:nj], dlt[:, :, 0:nj], ACT.Exp).then_inc(ex_ok, 1)
                    act.wait_ge(o_ok, h * NT + NT)
                    act.activation(sq[:], o[:], ACT.Square).then_inc(fin, 1)
                    act.wait_ge(fin, h * 5 + 2)
                    act.activation(oln[:], oss[:], ACT.Ln, bias=eps[:], scale=1.0 / P).then_inc(lnm2, 1)
                    act.wait_ge(lnm2, h + 1)
                    act.activation(ors[:], oln[:], ACT.Exp, scale=-0.5).then_inc(fin, 1)

                head(0)
                with act.Fori(1, NH) as h:
                    head(h)

            @block.vector
            def _(dve):
                dve.memset(eps[:], EPS).then_inc(eps_set, 1)
                dve.wait_ge(consts_in, 16 * 11)
                dve.tensor_copy(ident_bf[:], ident[:]).then_inc(mask_ok, 1)
                dve.tensor_copy(causal[:], causal_f[:]).then_inc(mask_ok, 1)
                dve.tensor_scalar(gcol[:, 0:1], gcol[:, 0:1], HD ** -0.5, None, ALU.mult).then_inc(gain_ok, 1)
                dve.tensor_scalar(gain[:], gain[:], 1.0 - LAM_INIT, None, ALU.mult).then_inc(gain_ok, 1)
                dve.tensor_tensor(lam_pr[:], lam_in[:, 0:2], lam_in[:, 2:4], ALU.mult).then_inc(lam_ok, 1)
                dve.wait_ge(lam_ok, 1)
                dve.tensor_reduce(lam_s[:, 0:2], lam_pr[:], AX.X, ALU.add).then_inc(lam_ok, 1)
                dve.memset(lamvec[:, 0:1], 1.0).then_inc(gain_ok, 1)
                dve.wait_ge(lam_ok, 3)
                dve.scalar_tensor_tensor(lamvec[:, 1:2], lam_s[:, 3:4], LAM_INIT, lam_s[:, 2:3],
                                         ALU.subtract, ALU.subtract).then_inc(gain_ok, 1)
                dve.wait_ge(gain_ok, 4)

                def head(h):
                    for i in range(2):
                        dve.wait_ge(sq_ok, h * 2 + i + 1)
                        dve.tensor_reduce(ms[:, i], sq[:].rearrange("p t (c d) -> p (t c) d", c=2), AX.X, ALU.add).then_inc(ms_ok, 1)
                    dve.wait_ge(rs_ok, h + 1)
                    dve.tensor_tensor(dup[:, 1].rearrange("p t c u d -> p (t c) u d"),
                                      qk[:, 1].rearrange("p t (c d) -> p (t c) d", c=2).unsqueeze(2).to_broadcast([P, 2 * NT, 2, HD]),
                                      rs[:, 1].unsqueeze(2).unsqueeze(3).to_broadcast([P, 2 * NT, 2, HD]),
                                      ALU.mult).then_inc(dup_ok[1], 1)
                    for n in range(NPREP):
                        i, c, a = n // (NPREP // 2), n // (NPREP // 4) % 2, n % (S // CK)
                        dve.wait_ge(prep_hi, h * NPREP + n + 1)
                        cut = slice(a * CK, (a + 1) * CK)
                        lo, hi, r = ((qs, qs), (klo, khi))[i] + (slice(HD, P) if i == 0 else slice(0, P),)
                        dve.scalar_tensor_tensor(lo[r, c, cut], psW[n % 2][r, :], gcol[r, i:i + 1], hi[r, c, cut].bitcast(F32),
                                                 ALU.mult, ALU.subtract).then_inc(prep_lo, 1)

                    def stat(ins):
                        step[0] += 1
                        ins.then_inc(steps, 1)
                        dve.wait_ge(steps, h * STEPS + step[0])

                    step = [0]
                    for i in range(NT):
                        nj = len(units[i])
                        u = i % 2
                        for j, w in enumerate(units[i]):
                            n = first[i] + j
                            dve.wait_ge(score_ps, h * CH + n + 1)
                            dve.tensor_reduce(nm[:, u, :, j:j + 1], psS[n % 2][:, :, 0:w], AX.X, ALU.max,
                                              negate=True).then_inc(max_ok, 1)
                        dve.wait_ge(max_ok, h * CH + first[i] + nj)
                        if nj > 1:
                            stat(dve.tensor_reduce(low[:], nm[:, u, :, 0:nj], AX.X, ALU.min))
                            dve.tensor_tensor(dlt[:, :, 0:nj], low[:].unsqueeze(2).to_broadcast([P, 2, nj]), nm[:, u, :, 0:nj],
                                              ALU.subtract).then_inc(dl_ok, 1)
                            dve.wait_ge(ex_ok, h * (NT - 4) + i - 3)
                            dve.wait_ge(exp_ok, (h * CH + first[i] + nj) * 2)
                            stat(dve.tensor_tensor(exs[:, :, 0:nj], ex[:, :, 0:nj], sums[:, u, :, 0:nj], ALU.mult))
                            stat(dve.tensor_reduce(tot[:], exs[:, :, 0:nj], AX.X, ALU.add))
                            stat(dve.reciprocal(inv[:], tot[:]))
                            stat(dve.tensor_tensor(invl[:], inv[:], lamvec[:], ALU.mult))
                            dve.tensor_tensor(coef[:, u, :, 0:nj], ex[:, :, 0:nj],
                                              invl[:].unsqueeze(2).to_broadcast([P, 2, nj]), ALU.mult).then_inc(stat_ok, 1)
                        else:
                            dve.wait_ge(exp_ok, (h * CH + first[i] + nj) * 2)
                            stat(dve.reciprocal(inv[:], sums[:, u, :, 0]))
                            dve.tensor_tensor(coef[:, u, :, 0], inv[:], lamvec[:], ALU.mult).then_inc(stat_ok, 1)
                        dve.wait_ge(stat_ok, h * NT + i + 1)
                        for j, w in enumerate(units[i]):
                            dve.wait_ge(scaled, h * CH + first[i] + j + 1)
                            cut = slice(j * CK, j * CK + w)
                            dve.scalar_tensor_tensor(pr[:, u, 0, cut], pr[:, u, 0, cut], coef[:, u, 0, j:j + 1], pr[:, u, 1, cut],
                                                     ALU.mult, ALU.add).then_inc(comb_ok, 1)
                    dve.wait_ge(fin, h * 5 + 1)
                    dve.tensor_reduce(oss[:], sq[:], AX.X, ALU.add).then_inc(fin, 1)
                    dve.wait_ge(fin, h * 5 + 3)
                    dve.tensor_tensor(o[:], o[:], ors[:].unsqueeze(2).to_broadcast([P, NT, P]), ALU.mult).then_inc(fin, 1)
                    dve.wait_ge(fin, h * 5 + 4)
                    dve.tensor_tensor(o[:], o[:], gain[:].unsqueeze(1).to_broadcast([P, NT, P]), ALU.mult).then_inc(fin, 1)

                head(0)
                with dve.Fori(1, NH) as h:
                    head(h)

            @block.tensor
            def _(pe):
                pe.wait_ge(consts_in, 16 * 11)
                pe.wait_ge(mask_ok, 2)

                def head(h):
                    nonzero = later(h)
                    for n in range(NPREP):
                        i, c, a = n // (NPREP // 2), n // (NPREP // 4) % 2, n % (S // CK)
                        if n % (NPREP // 2) == 0:
                            pe.wait_ge(dup_ok[i], h + 1)
                        if n >= 2:
                            pe.wait_ge(prep_lo, h * NPREP + n - 1)
                        elif nonzero:
                            pe.wait_ge(wT_ok, h * CH)
                        for k in range(4):
                            last = pe.transpose(psW[n % 2][:, k * P:(k + 1) * P],
                                                dup[:, i, a * 4 + k, c].rearrange("p u d -> p (u d)"), ident[:])
                        last.then_inc(prep_ps, 1)
                    for i in range(NT + 1):
                        if i < NT:
                            for j, w in enumerate(units[i]):
                                n = first[i] + j
                                if i == 0:
                                    pe.wait_ge(prep_lo, (h + 1) * NPREP)
                                if n >= 2 or nonzero:
                                    pe.wait_ge(exp_ok, (h * CH + n - 1) * 2)
                                diag = j == len(units[i]) - 1
                                for c in range(2):
                                    out = psS[n % 2][:, c, 0:w]
                                    q = qs[:, c, i * P:(i + 1) * P]
                                    pe.matmul(out, q, khi[:, c, j * CK:j * CK + w], start=True, stop=False)
                                    last = pe.matmul(out, q, klo[:, c, j * CK:j * CK + w], start=False, stop=not diag)
                                    if diag:
                                        last = pe.matmul(psS[n % 2][:, c, w - P:w], ident_bf[:], causal[:], start=False, stop=True)
                                last.then_inc(score_ps, 1)
                        if i >= 1:
                            for j, w in enumerate(units[i - 1]):
                                n = first[i - 1] + j
                                pe.wait_ge(comb_ok, h * CH + n + 1)
                                if n >= 2:
                                    pe.wait_ge(wT_ok, h * CH + n - 1)
                                for k in range(w // P):
                                    last = pe.transpose(psW[n % 2][:, k * P:(k + 1) * P],
                                                        pr[:, (i - 1) % 2, 0, j * CK + k * P:j * CK + (k + 1) * P], ident[:])
                                last.then_inc(wT_ps, 1)
                                if j >= 1:
                                    pv(h, i - 1, j - 1)
                            pv(h, i - 1, len(units[i - 1]) - 1)

                def pv(h, i, j):
                    n = first[i] + j
                    nonzero = later(h)
                    pe.wait_ge(wT_ok, h * CH + n + 1)
                    if j == 0 and (i >= 2 or nonzero):
                        pe.wait_ge(o_ok, h * NT + i - 1)
                    if i == 0:
                        pe.wait_ge(v_in[par[0]], vcount(h))
                    for k in range(units[i][j] // P):
                        t = j * 4 + k
                        last = pe.matmul(psO[i % 2][:, 0:P], wT[:, n % 2, k, :], v[:, par[0], t, :],
                                         start=(t == 0), stop=(t == i))
                    last.then_inc(pv_ok, 1)

                def vcount(h):
                    return (h - par[0] + 2) * 8

                par = [0]
                head(0)
                par[0] = 1
                head(1)
                with pe.Fori(1, NH // 2) as pair:
                    par[0] = 0
                    head(pair * 2)
                    par[0] = 1
                    head(pair * 2 + 1)


NE = 16
NGR = 4
GE = NE // NGR
HALF = D // 2


def project_out(nc, mix, x, w_out, ffn_norm, w_router, ident_in, h1, xn_rows, logits):
    with ExitStack() as stack:
        at = Place(nc, stack, "out")
        ident = at.sb("ident", [P, P])
        gain = at.sb("gain", [P, D])
        eps = at.sb("eps", [P, 1])
        wraw = at.sb("wraw", [P, 2, HALF])
        whi = at.sb("whi", [P, KD, D], F32R)
        wlo = at.sb("wlo", [P, KD, D], F32R)
        wr = at.sb("wr", [P, KD, NE])
        m = at.sb("m", [P, 2, D])
        xs = at.sb("xs", [P, 2, D])
        mhi = at.sb("mhi", [P, 2, KD, P], F32R)
        mlo = at.sb("mlo", [P, 2, KD, P], F32R)
        h = at.sb("h", [P, 2, D])
        sq = at.sb("sq", [P, D])
        ss, lnm, rs = (at.sb(n, [P, 2]) for n in ("ss", "lnm", "rs"))
        xr = at.sb("xr", [P, 2, D])
        xn = at.sb("xn", [P, 2, D])
        xT = at.sb("xT", [P, KD, P])
        lg = at.sb("lg", [P, NT, NE])
        zero = at.sb("zero", [1, D])
        psT = [at.ps(f"psT{i}", (P, 4, P)) for i in range(2)]
        psM = [at.ps(f"psM{i}", (P, 2, HALF)) for i in range(2)]
        psR = at.ps("psR", (P, 4, P))
        psL = at.ps("psL")

        consts_in, zero_ok, zero_out, eps_set = (at.sem(n) for n in ("consts_in", "zero_ok", "zero_out", "eps_set"))
        w_in = [at.sem(f"w_in{i}") for i in range(2)]
        whi_ok, wlo_ok = at.sem("whi_ok"), at.sem("wlo_ok")
        m_in = [at.sem(f"m_in{i}") for i in range(2)]
        x_in = [at.sem(f"x_in{i}") for i in range(2)]
        s = {n: at.sem(n) for n in ("mT_ps mhi_ok mlo_ok mm_ok h_ok sq_ok lnm_ok rs_ok xr_ok xn_ok xT_ps xT_ok lg_ps lg_ok").split()}
        h_out = [at.sem(f"h_out{i}") for i in range(2)]
        n_out = [at.sem(f"n_out{i}") for i in range(2)]
        lg_out = at.sem("lg_out")

        def later(t, n=1):
            return not isinstance(t, int) or t >= n

        def done(eng, name, t, n=1, per=1):
            if eng in (nc.sync, nc.gpsimd):
                at.hold(eng, s[name], t * per + n)
            else:
                eng.wait_ge(s[name], t * per + n)

        def landed(eng, sem, t, b):
            at.hold(eng, sem[b], (t - b + 2) * 8)

        def tiles(eng, body):
            body(0, 0)
            body(1, 1)
            with eng.Fori(1, NT // 2) as pair:
                body(pair * 2, 0)
                body(pair * 2 + 1, 1)

        def staggered(eng, front, back):
            front(0, 0)
            front(1, 1)
            back(0, 0)
            with eng.Fori(1, NT // 2) as pair:
                front(pair * 2, 0)
                back(pair * 2 - 1, 1)
                front(pair * 2 + 1, 1)
                back(pair * 2, 0)
            back(NT - 1, 1)

        with nc.Block() as block:
            @block.sync
            def _(sp):
                sp.dma_start(ident[:], ident_in).then_inc(consts_in, 16)
                sp.dma_start(gain[:], ffn_norm.broadcast_to([P, D])).then_inc(consts_in, 16)
                sp.dma_start(wr[:], w_router.rearrange("(k p) e -> p k e", p=P)).then_inc(consts_in, 16)

                def load_m(t, b):
                    if later(t, 2):
                        done(sp, "mT_ps", t - 2, 2, 2)
                    sp.dma_start(m[:, b], mix[bass.ds(t * P, P), :]).then_inc(m_in[b], 16)

                def load_x(t, b):
                    if later(t, 2):
                        done(sp, "h_ok", t - 2)
                    sp.dma_start(xs[:, b], x[bass.ds(t * P, P), :]).then_inc(x_in[b], 16)

                load_m(0, 0)
                for i in range(2 * KD):
                    if i >= 2:
                        sp.wait_ge(whi_ok, i - 1)
                        sp.wait_ge(wlo_ok, i - 1)
                    sp.dma_start(wraw[:, i % 2], w_out[i // 2 * P:(i // 2 + 1) * P, (i % 2) * HALF:(i % 2 + 1) * HALF]) \
                        .then_inc(w_in[i % 2], 16)
                load_x(0, 0)
                load_m(1, 1)
                load_x(1, 1)
                with sp.Fori(1, NT // 2) as pair:
                    for b in range(2):
                        load_m(pair * 2 + b, b)
                        load_x(pair * 2 + b, b)

            @block.gpsimd
            def _(pool):
                pool.memset(zero[:], 0.0).then_inc(zero_ok, 1)
                pool.wait_ge(zero_ok, 1)
                pool.dma_start(xn_rows[S:S + 1, :], zero[:]).then_inc(zero_out, 16)
                pool.wait_ge(consts_in, 48)

                def tile(t, b):
                    done(pool, "h_ok", t)
                    pool.dma_start(h1[bass.ds(t * P, P), :], h[:, b]).then_inc(h_out[b], 16)
                    done(pool, "xr_ok", t)
                    if later(t, 2):
                        at.hold(pool, n_out[b], (t - b) * 8)
                        done(pool, "xT_ps", t - 2, 2, 2)
                    pool.tensor_tensor(xn[:, b], xr[:, b], gain[:], ALU.mult).then_inc(s["xn_ok"], 1)
                    done(pool, "xn_ok", t)
                    pool.dma_start(xn_rows[bass.ds(t * P, P), :], xn[:, b]).then_inc(n_out[b], 16)

                tiles(pool, tile)
                pool.wait_ge(s["lg_ok"], NT)
                pool.dma_start(logits, lg[:].rearrange("p t e -> p (t e)")).then_inc(lg_out, 16)
                pool.wait_ge(lg_out, 16)
                pool.wait_ge(zero_out, 16)
                for b in range(2):
                    pool.wait_ge(h_out[b], NT // 2 * 16)
                    pool.wait_ge(n_out[b], NT // 2 * 16)

            @block.scalar
            def _(act):
                act.preload_act_table_set("natural_log_exp_and_others")
                for i in range(2 * KD):
                    act.wait_ge(w_in[i % 2], 16 * (i // 2 + 1))
                    act.activation(whi[:, i // 2, (i % 2) * HALF:(i % 2 + 1) * HALF], wraw[:, i % 2], ACT.Copy).then_inc(whi_ok, 1)
                act.wait_ge(eps_set, 1)

                def front(t, b):
                    for i in range(2):
                        done(act, "mT_ps", t, i + 1, 2)
                        if i == 0 and later(t, 2):
                            done(act, "mm_ok", t - 2)
                        act.activation(mhi[:, b, i * 4:(i + 1) * 4], psT[i][:], ACT.Copy).then_inc(s["mhi_ok"], 1)

                def back(t, b):
                    done(act, "h_ok", t)
                    if later(t):
                        done(act, "sq_ok", t - 1)
                    act.activation(sq[:], h[:, b], ACT.Square, accum_out=ss[:, b:b + 1]).then_inc(s["sq_ok"], 1)
                    done(act, "sq_ok", t)
                    act.activation(lnm[:, b:b + 1], ss[:, b:b + 1], ACT.Ln, bias=eps[:], scale=1.0 / D).then_inc(s["lnm_ok"], 1)
                    done(act, "lnm_ok", t)
                    act.activation(rs[:, b:b + 1], lnm[:, b:b + 1], ACT.Exp, scale=-0.5).then_inc(s["rs_ok"], 1)
                    done(act, "rs_ok", t)
                    if later(t, 2):
                        done(act, "xn_ok", t - 2)
                    act.activation(xr[:, b], h[:, b], ACT.Copy, scale=rs[:, b:b + 1]).then_inc(s["xr_ok"], 1)
                    for i in range(2):
                        done(act, "xT_ps", t, i + 1, 2)
                        if later(t):
                            done(act, "lg_ps", t - 1)
                        act.activation(xT[:, i * 4:(i + 1) * 4], psR[:], ACT.Copy).then_inc(s["xT_ok"], 1)

                staggered(act, front, back)

            @block.vector
            def _(dve):
                dve.memset(eps[:], EPS).then_inc(eps_set, 1)
                for i in range(2 * KD):
                    dve.wait_ge(whi_ok, i + 1)
                    cut = slice((i % 2) * HALF, (i % 2 + 1) * HALF)
                    dve.tensor_tensor(wlo[:, i // 2, cut], wraw[:, i % 2], whi[:, i // 2, cut].bitcast(F32), ALU.subtract).then_inc(wlo_ok, 1)

                def front(t, b):
                    for i in range(2):
                        done(dve, "mhi_ok", t, i + 1, 2)
                        dve.tensor_tensor(mlo[:, b, i * 4:(i + 1) * 4], psT[i][:], mhi[:, b, i * 4:(i + 1) * 4].bitcast(F32),
                                          ALU.subtract).then_inc(s["mlo_ok"], 1)

                def back(t, b):
                    done(dve, "mm_ok", t)
                    landed(dve, x_in, t, b)
                    if later(t, 2):
                        done(dve, "xr_ok", t - 2)
                        dve.wait_ge(h_out[b], (t - b) * 8)
                    dve.tensor_tensor(h[:, b], psM[b][:].rearrange("p a n -> p (a n)"), xs[:, b], ALU.add).then_inc(s["h_ok"], 1)
                    done(dve, "lg_ps", t)
                    dve.tensor_copy(lg[:, bass.ds(t, 1), :], psL[:, 0:NE].unsqueeze(1)).then_inc(s["lg_ok"], 1)

                staggered(dve, front, back)

            @block.tensor
            def _(pe):
                pe.wait_ge(consts_in, 48)

                def front(t, b):
                    landed(pe, m_in, t, b)
                    for i in range(2):
                        if later(t):
                            done(pe, "mlo_ok", t - 1, i + 1, 2)
                        for j in range(4):
                            last = pe.transpose(psT[i][:, j], m[:, b, (i * 4 + j) * P:(i * 4 + j + 1) * P], ident[:])
                        last.then_inc(s["mT_ps"], 1)

                def middle(t, b):
                    done(pe, "mlo_ok", t, 2, 2)
                    if isinstance(t, int) and t == 0:
                        pe.wait_ge(wlo_ok, 2 * KD)
                    if later(t, 2):
                        done(pe, "h_ok", t - 2)
                    for n in range(2):
                        cut = slice(n * HALF, (n + 1) * HALF)
                        for k in range(KD):
                            for i, (l, r) in enumerate(((mhi, whi), (mhi, wlo), (mlo, whi))):
                                last = pe.matmul(psM[b][:, n], l[:, b, k], r[:, k, cut], start=(k == 0 and i == 0),
                                                 stop=(k == KD - 1 and i == 2))
                    last.then_inc(s["mm_ok"], 1)

                def router(t, b):
                    done(pe, "xn_ok", t)
                    for i in range(2):
                        if i or later(t):
                            done(pe, "xT_ok", t - 1 + i, 2 - i, 2)
                        for j in range(4):
                            last = pe.transpose(psR[:, j], xn[:, b, (i * 4 + j) * P:(i * 4 + j + 1) * P], ident[:])
                        last.then_inc(s["xT_ps"], 1)
                    done(pe, "xT_ok", t, 2, 2)
                    if later(t):
                        done(pe, "lg_ok", t - 1)
                    for k in range(KD):
                        last = pe.matmul(psL[:, 0:NE], xT[:, k], wr[:, k], start=(k == 0), stop=(k == KD - 1))
                    last.then_inc(s["lg_ps"], 1)

                front(0, 0)
                middle(0, 0)
                front(1, 1)
                with pe.Fori(1, NT // 2) as pair:
                    middle(pair * 2 - 1, 1)
                    front(pair * 2, 0)
                    router(pair * 2 - 2, 0)
                    middle(pair * 2, 0)
                    front(pair * 2 + 1, 1)
                    router(pair * 2 - 1, 1)
                middle(NT - 1, 1)
                router(NT - 2, 0)
                router(NT - 1, 1)


NB = 2 * S // P + NE
NROW = NB * P


def route(nc, logits, below_in, upper_in, firsts_in, blocks_in, tokens_in, row_tok, dest_out, wgt_out, plan_out):
    with ExitStack() as stack:
        at = Place(nc, stack, "route")
        NG2 = NT * NGR
        lg = at.sb("lg", [P, NT, NE])
        below = at.sb("below", [P, GE, GE])
        upper = at.sb("upper", [P, 2, P])
        firsts = at.sb("firsts", [P, NE, NT])
        blocks = at.sb("blocks", [P, NB])
        tokens = at.sb("tokens", [P, NT], I32)
        pad = at.sb("pad", [P, NB], I32)
        mx, sm, inv = (at.sb(n, [P, NT]) for n in ("mx", "sm", "inv"))
        aff, tmp, first, second, sel, pre, dst = (at.sb(n, [P, NT, NE]) for n in ("aff", "tmp", "first", "second", "sel", "pre", "dst"))
        cmp1, cmp2 = (at.sb(n, [P, NG2, GE, GE]) for n in ("cmp1", "cmp2"))
        rank = at.sb("rank", [P, NG2, GE])
        gs = at.sb("gs", [P, NT, NGR])
        grank, gtop = at.sb("grank", [P, NT, NGR]), at.sb("gtop", [P, NT, NGR])
        totT, incl, excl = (at.sb(n, [P, NE, NT]) for n in ("totT", "incl", "excl"))
        cnt_i, nb_i, ends_i = (at.sb(n, [P, NE], I32) for n in ("cnt_i", "nb_i", "ends_i"))
        cnt, nb, ends, starts, ones = (at.sb(n, [P, NE]) for n in ("cnt", "nb", "ends", "starts", "ones"))
        dest_f = at.sb("dest_f", [P, 2, NT])
        dest = at.sb("dest", [P, 2, NT], I32)
        wgt = at.sb("wgt", [P, 2, NT])
        over = at.sb("over", [P, NB, NE])
        be = at.sb("be", [P, NB])
        plan = at.sb("plan", [P, 2 * NB + NE], I32)
        ps = at.ps("ps")
        consts_in, lg_in, pad_out, out = (at.sem(n) for n in ("consts_in", "lg_in", "pad_out", "out"))
        step, exp_ok, tok_ok, count_ps, dest_ok, plan_ok, pad_ok = (at.sem(n) for n in ("step", "exp_ok", "tok_ok", "count_ps", "dest_ok", "plan_ok", "pad_ok"))
        scattered = at.sem("scattered")

        def over_last(x, n):
            return x.unsqueeze(len(x.shape)).to_broadcast([*x.shape, n])

        with nc.Block() as block:
            @block.sync
            def _(sp):
                sp.dma_start(lg[:].rearrange("p t e -> p (t e)"), logits).then_inc(lg_in, 16)
                for dst_, src in ((below, below_in), (upper, upper_in), (firsts, firsts_in), (blocks, blocks_in), (tokens, tokens_in)):
                    sp.dma_start(dst_[:], src).then_inc(consts_in, 16)
                sp.wait_ge(pad_ok, 1)
                sp.dma_start(row_tok.rearrange("(p b) o -> p (b o)", p=P), pad[:]).then_inc(pad_out, 16)
                sp.wait_ge(plan_ok, 1)
                sp.dma_start(dest_out, dest[:].rearrange("p a t -> p (a t)")).then_inc(out, 16)
                sp.dma_start(wgt_out, wgt[:].rearrange("p a t -> p (a t)")).then_inc(out, 16)
                sp.dma_start(plan_out, plan[:]).then_inc(out, 16)
                sp.wait_ge(out, 48)

            @block.scalar
            def _(act):
                act.wait_ge(exp_ok, 1)
                act.activation(aff[:], tmp[:], ACT.Exp).then_inc(exp_ok, 1)

            @block.tensor
            def _(pe):
                pe.wait_ge(consts_in, 80)
                pe.wait_ge(tok_ok, 1)
                for i in range(2):
                    last = pe.matmul(ps[:, i * 256:(i + 1) * 256], upper[:, i], sel[:].rearrange("p t e -> p (t e)"), start=True, stop=True)
                last.then_inc(count_ps, 1)

            @block.gpsimd
            def _(pool):
                pool.memset(pad[:], S).then_inc(pad_ok, 1)
                pool.wait_ge(dest_ok, 1)
                pool.wait_ge(pad_out, 16)
                pool.wait_ge(consts_in, 80)
                for t in range(NT):
                    for a in range(2):
                        pool.indirect_dma_start(row_tok, bass.IndirectOffsetOnAxis(ap=dest[:, a, t:t + 1], axis=0),
                                                tokens[:, t:t + 1], None).then_inc(scattered, 16)
                pool.wait_ge(scattered, 2 * NT * 16)

            @block.vector
            def _(dve):
                count = [0]

                def link(ins):
                    count[0] += 1
                    ins.then_inc(step, 1)
                    dve.wait_ge(step, count[0])

                dve.wait_ge(lg_in, 16)
                dve.wait_ge(consts_in, 80)
                TT, TS = dve.tensor_tensor, dve.tensor_scalar
                link(dve.tensor_reduce(mx[:], lg[:], AX.X, ALU.max))
                TT(tmp[:], lg[:], over_last(mx[:], NE), ALU.subtract).then_inc(exp_ok, 1)
                dve.wait_ge(exp_ok, 2)
                link(dve.tensor_reduce(sm[:], aff[:], AX.X, ALU.add))
                link(dve.reciprocal(inv[:], sm[:]))
                link(TT(aff[:], aff[:], over_last(inv[:], NE), ALU.mult))

                def ranks(x, out_, n):
                    e, j = over_last(x, n), x.unsqueeze(2).to_broadcast([P, x.shape[1], n, n])
                    c1, c2 = cmp1[:, 0:x.shape[1]], cmp2[:, 0:x.shape[1]]
                    link(TT(c1, j, e, ALU.is_equal))
                    link(TT(c1, c1, below[:].unsqueeze(1).to_broadcast([P, x.shape[1], n, n]), ALU.mult))
                    link(TT(c2, j, e, ALU.is_gt))
                    link(TT(c1, c1, c2, ALU.add))
                    link(dve.tensor_reduce(out_, c1, AX.X, ALU.add))

                def by_group(x):
                    return x.rearrange("p t (g e) -> p (t g) e", e=GE)

                ranks(by_group(aff[:]), rank[:], GE)
                link(TS(by_group(tmp[:]), rank[:], 1.5, None, ALU.is_lt))
                link(TT(tmp[:], aff[:], tmp[:], ALU.mult))
                link(dve.tensor_reduce(gs[:].rearrange("p t g -> p (t g)"), by_group(tmp[:]), AX.X, ALU.add))
                ranks(gs[:], grank[:], NGR)
                link(TS(gtop[:], grank[:], 0.5, None, ALU.is_lt))
                top = over_last(gtop[:].rearrange("p t g -> p (t g)"), GE)
                link(TS(by_group(first[:]), rank[:], 0.5, None, ALU.is_lt))
                link(TT(by_group(first[:]), by_group(first[:]), top, ALU.mult))
                link(TS(by_group(second[:]), rank[:], 1.0, None, ALU.is_equal))
                link(TT(by_group(second[:]), by_group(second[:]), top, ALU.mult))
                TT(sel[:], first[:], second[:], ALU.add).then_inc(tok_ok, 1)
                dve.wait_ge(tok_ok, 1)
                for a, x in enumerate((first, second)):
                    link(TT(tmp[:], aff[:], x[:], ALU.mult))
                    link(dve.tensor_reduce(wgt[:, a], tmp[:], AX.X, ALU.add))
                link(TT(sm[:], wgt[:, 0], wgt[:, 1], ALU.add))
                link(dve.reciprocal(inv[:], sm[:]))
                link(TT(wgt[:], wgt[:], inv[:].unsqueeze(1).to_broadcast([P, 2, NT]), ALU.mult))
                dve.wait_ge(count_ps, 1)
                link(dve.tensor_copy(totT[:].rearrange("p e t -> p t e"), ps[:, 256:512].rearrange("p (t e) -> p t e", e=NE)))
                link(dve.tensor_tensor_scan(incl[:].rearrange("p e t -> p (e t)"), firsts[:].rearrange("p e t -> p (e t)"),
                                            totT[:].rearrange("p e t -> p (e t)"), 0.0, ALU.mult, ALU.add))
                link(TT(excl[:], incl[:], totT[:], ALU.subtract))
                link(TS(cnt[:], incl[:, :, NT - 1], P - 1.0, None, ALU.add))
                link(dve.tensor_copy(cnt_i[:], cnt[:]))
                link(TS(nb_i[:], cnt_i[:], 7, None, ALU.arith_shift_right))
                link(dve.tensor_copy(nb[:], nb_i[:]))
                link(dve.memset(ones[:], 1.0))
                link(dve.tensor_tensor_scan(ends[:], ones[:], nb[:], 0.0, ALU.mult, ALU.add))
                link(TT(starts[:], ends[:], nb[:], ALU.subtract))
                link(TS(starts[:], starts[:], float(P), None, ALU.mult))
                link(TT(dst[:], ps[:, 0:256].rearrange("p (t e) -> p t e", e=NE), excl[:].rearrange("p e t -> p t e"), ALU.add))
                link(TT(dst[:], dst[:], starts[:].unsqueeze(1).to_broadcast([P, NT, NE]), ALU.add))
                for a, x in enumerate((first, second)):
                    link(TT(tmp[:], dst[:], x[:], ALU.mult))
                    link(dve.tensor_reduce(dest_f[:, a], tmp[:], AX.X, ALU.add))
                dve.tensor_copy(dest[:], dest_f[:]).then_inc(dest_ok, 1)
                link(TT(over[:], ends[:].unsqueeze(1).to_broadcast([P, NB, NE]), over_last(blocks[:], NE), ALU.is_le))
                link(dve.tensor_reduce(be[:], over[:], AX.X, ALU.add))
                link(TS(be[:], be[:], NE - 1.0, None, ALU.min))
                link(dve.tensor_copy(plan[:, NB:2 * NB], be[:]))
                link(TS(plan[:, 0:NB], plan[:, NB:2 * NB], 1, None, ALU.bitwise_and))
                link(TS(be[:], be[:], 1.0, 3 * 16.0, ALU.add, ALU.mult))
                link(dve.tensor_copy(plan[:, NB:2 * NB], be[:]))
                link(TS(ends[:], ends[:], 1.0, None, ALU.add))
                dve.wait_ge(dest_ok, 1)
                dve.tensor_copy(plan[:, 2 * NB:], ends[:]).then_inc(plan_ok, 1)


FF = 512
KF = FF // P


def experts(nc, xn_rows, row_tok, plan_in, w_gate, w_up, w_down, ident_in, y_rows):
    with ExitStack() as stack:
        at = Place(nc, stack, "moe")
        ident = at.sb("ident", [P, P])
        rows = at.sb("rows", [P, NB], I32)
        plan = at.sb("plan", [P, 2 * NB + NE], I32)
        idx = [at.sb(f"idx{i}", [P, 1], I32) for i in range(2)]
        wg = at.sb("wg", [P, 2, KD, FF])
        wu = at.sb("wu", [P, 2, KD, FF])
        wd = at.sb("wd", [P, 2, KF, D])
        x = at.sb("x", [P, 2, D])
        xT = at.sb("xT", [P, 2, KD, P])
        sg = at.sb("sg", [P, FF])
        gg = at.sb("gg", [P, FF])
        hh = at.sb("hh", [P, FF])
        hT = at.sb("hT", [P, 2, KF, P])
        y = at.sb("y", [P, 2, D])
        psT = [at.ps(f"psT{i}", (P, 4, P)) for i in range(2)]
        psG, psU, psH = at.ps("psG"), at.ps("psU"), at.ps("psH")
        psY = at.ps("psY", (P, 2, HALF))
        consts_in = at.sem("consts_in")
        w_in = at.sem("w_in")
        s = {n: at.sem(n) for n in "idx_ok xT_ps xT_ok g_ps u_ps sg_ok gg_ok hh_ok hT_ps hT_ok y_ps y_ok".split()}
        x_in = [at.sem(f"x_in{i}") for i in range(2)]
        y_out = [at.sem(f"y_out{i}") for i in range(2)]
        blocks_done = at.sem("blocks_done")

        def later(t, n=1):
            return not isinstance(t, int) or t >= n

        def done(eng, name, t, n=1, per=1):
            if eng in (nc.sync, nc.gpsimd):
                at.hold(eng, s[name], t * per + n)
            else:
                eng.wait_ge(s[name], t * per + n)

        def blocks_of(eng, body):
            body(0, 0)
            body(1, 1)
            with eng.Fori(1, NB // 2) as pair:
                body(pair * 2, 0)
                body(pair * 2 + 1, 1)

        with nc.Block() as block:
            @block.sync
            def _(sp):
                sp.dma_start(plan[:], plan_in).then_inc(consts_in, 16)
                sp.dma_start(ident[:], ident_in).then_inc(consts_in, 16)
                with nc.allow_non_contiguous_dma(reason="one row number per partition and block"):
                    sp.dma_start(rows[:], row_tok.rearrange("(b p) o -> p (b o)", p=P)).then_inc(consts_in, 16)

                def load(e, slot):
                    if later(e):
                        at.hold(sp, w_in, e * 48)
                    if later(e, 2):
                        end = sp.value_load(plan[0:1, bass.ds(e + (2 * NB - 2), 1)], min_val=1, max_val=NB + 1)
                        at.hold(sp, blocks_done, end)
                    for dst, src, k in ((wg, w_gate, KD), (wu, w_up, KD), (wd, w_down, KF)):
                        sp.dma_start(dst[:, slot], src[0, bass.ds(e, 1)].rearrange("a (k p) n -> p (a k) n", p=P)).then_inc(w_in, 16)

                load(0, 0)
                load(1, 1)
                sp.wait_ge(consts_in, 48)
                with sp.Fori(1, NE // 2) as pair:
                    load(pair * 2, 0)
                    load(pair * 2 + 1, 1)

            @block.gpsimd
            def _(pool):
                pool.wait_ge(consts_in, 48)

                def gather(t, b):
                    done(pool, "idx_ok", t)
                    if later(t, 2):
                        done(pool, "xT_ps", t - 2, 2, 2)
                    pool.indirect_dma_start(x[:, b], None, xn_rows, bass.IndirectOffsetOnAxis(ap=idx[b][:], axis=0)).then_inc(x_in[b], 16)

                def store(t, b):
                    done(pool, "y_ok", t, 2, 2)
                    pool.dma_start(y_rows[bass.ds(t * P, P), :], y[:, b]).then_inc(y_out[b], 16)

                gather(0, 0)
                gather(1, 1)
                with pool.Fori(1, NB // 2) as pair:
                    gather(pair * 2, 0)
                    store(pair * 2 - 2, 0)
                    gather(pair * 2 + 1, 1)
                    store(pair * 2 - 1, 1)
                store(NB - 2, 0)
                store(NB - 1, 1)
                for b in range(2):
                    pool.wait_ge(y_out[b], NB // 2 * 16)

            @block.scalar
            def _(act):
                def tile(t, b):
                    for i in range(2):
                        done(act, "xT_ps", t, i + 1, 2)
                        if i == 0 and later(t, 2):
                            done(act, "u_ps", t - 2)
                        act.activation(xT[:, b, i * 4:(i + 1) * 4], psT[i][:], ACT.Copy).then_inc(s["xT_ok"], 1)
                    done(act, "g_ps", t)
                    if later(t):
                        done(act, "gg_ok", t - 1)
                    act.activation(sg[:], psG[:], ACT.Sigmoid).then_inc(s["sg_ok"], 1)
                    if later(t):
                        evac_y(t - 1, 1 - b)
                    done(act, "hT_ps", t)
                    if later(t, 2):
                        done(act, "y_ps", t - 2)
                    act.activation(hT[:, b], psH[:].rearrange("p (k t) -> p k t", k=KF), ACT.Copy).then_inc(s["hT_ok"], 1)

                def evac_y(t, b):
                    done(act, "y_ps", t)
                    if later(t, 2):
                        act.wait_ge(y_out[b], (t - b) * 8)
                    act.activation(y[:, b, HALF:D], psY[:, 1], ACT.Copy).then_inc(s["y_ok"], 1)

                blocks_of(act, tile)
                evac_y(NB - 1, 1)

            @block.vector
            def _(dve):
                dve.wait_ge(consts_in, 48)

                def index(t, b):
                    if later(t, 2):
                        dve.wait_ge(x_in[b], (t - b) * 8)
                    dve.tensor_copy(idx[b][:], rows[:, bass.ds(t, 1)]).then_inc(s["idx_ok"], 1)

                def tile(t, b, ahead=True):
                    done(dve, "sg_ok", t)
                    if later(t):
                        done(dve, "hh_ok", t - 1)
                    dve.tensor_tensor(gg[:], psG[:], sg[:], ALU.mult).then_inc(s["gg_ok"], 1)
                    done(dve, "gg_ok", t)
                    done(dve, "u_ps", t)
                    if later(t):
                        done(dve, "hT_ps", t - 1)
                    dve.tensor_tensor(hh[:], psU[:], gg[:], ALU.mult).then_inc(s["hh_ok"], 1)
                    if later(t):
                        evac_y(t - 1, 1 - b)
                    if ahead:
                        index(t + 2, b)

                def evac_y(t, b):
                    done(dve, "y_ps", t)
                    if later(t, 2):
                        dve.wait_ge(y_out[b], (t - b) * 8)
                    dve.tensor_copy(y[:, b, 0:HALF], psY[:, 0]).then_inc(s["y_ok"], 1)

                index(0, 0)
                index(1, 1)
                tile(0, 0)
                tile(1, 1)
                with dve.Fori(1, NB // 2 - 1) as pair:
                    tile(pair * 2, 0)
                    tile(pair * 2 + 1, 1)
                tile(NB - 2, 0, False)
                tile(NB - 1, 1, False)
                evac_y(NB - 1, 1)

            @block.tensor
            def _(pe):
                pe.sem_inc(blocks_done, 1)
                pe.wait_ge(consts_in, 48)

                def transpose_x(t, b):
                    pe.wait_ge(x_in[b], (t - b + 2) * 8)
                    for i in range(2):
                        if later(t):
                            done(pe, "xT_ok", t - 1, i + 1, 2)
                        for j in range(4):
                            last = pe.transpose(psT[i][:, j], x[:, b, (i * 4 + j) * P:(i * 4 + j + 1) * P], ident[:])
                        last.then_inc(s["xT_ps"], 1)

                def slot_of(t):
                    return pe.value_load(plan[0:1, bass.ds(t, 1)], min_val=0, max_val=1)

                def up(t, b, slot):
                    have = pe.value_load(plan[0:1, bass.ds(t + NB, 1)], min_val=48, max_val=NE * 48)
                    pe.wait_ge(w_in, have)
                    done(pe, "xT_ok", t, 2, 2)
                    for ps, w, name, free in ((psG, wg, "g_ps", "gg_ok"), (psU, wu, "u_ps", "hh_ok")):
                        if later(t):
                            done(pe, free, t - 1)
                        for k in range(KD):
                            last = pe.matmul(ps[:], xT[:, b, k], w[:, bass.ds(slot, 1), k, :], start=(k == 0), stop=(k == KD - 1))
                        last.then_inc(s[name], 1)

                def down(t, b, slot):
                    done(pe, "hT_ok", t)
                    if later(t):
                        done(pe, "y_ok", t - 1, 2, 2)
                    for n in range(2):
                        for k in range(KF):
                            last = pe.matmul(psY[:, n], hT[:, b, k], wd[:, bass.ds(slot, 1), k, n * HALF:(n + 1) * HALF],
                                             start=(k == 0), stop=(k == KF - 1))
                    last.then_inc(s["y_ps"], 1)

                def turn_h(t, b):
                    done(pe, "hh_ok", t)
                    if later(t):
                        done(pe, "hT_ok", t - 1)
                    for k in range(KF):
                        last = pe.transpose(psH[:, k * P:(k + 1) * P], hh[:, k * P:(k + 1) * P], ident[:])
                    last.then_inc(s["hT_ps"], 1)

                def tile(t, b, ahead=True):
                    up(t, b, slot_of(t))
                    if later(t):
                        down(t - 1, 1 - b, slot_of(t - 1))
                        pe.drain().then_inc(blocks_done, 1)
                    if ahead:
                        transpose_x(t + 1, 1 - b)
                    turn_h(t, b)

                transpose_x(0, 0)
                tile(0, 0)
                tile(1, 1)
                with pe.Fori(1, NB // 2 - 1) as pair:
                    tile(pair * 2, 0)
                    tile(pair * 2 + 1, 1)
                tile(NB - 2, 0)
                tile(NB - 1, 1, False)
                down(NB - 1, 1, slot_of(NB - 1))


PD = 256
KP = PD // P


def embed(nc, h1, y_rows, dest_in, wgt_in, p_in, ple_proj, ple_norm, ple_gate, ident_in, out):
    with ExitStack() as stack:
        at = Place(nc, stack, "ple")
        ident = at.sb("ident", [P, P])
        gain = at.sb("gain", [P, D])
        eps = at.sb("eps", [P, 1])
        dest = at.sb("dest", [P, 2, NT], I32)
        wgt = at.sb("wgt", [P, 2, NT])
        idx = [[at.sb(f"idx{i}{a}", [P, 1], I32) for a in range(2)] for i in range(2)]
        wraw = at.sb("wraw", [P, 2, HALF])
        whi = at.sb("whi", [P, KD + KP, D], F32R)
        wlo = at.sb("wlo", [P, KD + KP, D], F32R)
        h = at.sb("h", [P, 2, D])
        y = at.sb("y", [P, 2, 2, D])
        pp = at.sb("pp", [P, 2, PD])
        ahi = at.sb("ahi", [P, 2, KD + KP, P], F32R)
        alo = at.sb("alo", [P, 2, KD + KP, P], F32R)
        sq = at.sb("sq", [P, D])
        ss, lnm, rs = (at.sb(n, [P, 2]) for n in ("ss", "lnm", "rs"))
        ple = at.sb("ple", [P, D])
        sg = at.sb("sg", [P, D])
        o = at.sb("o", [P, 2, D])
        psT = [at.ps(f"psT{i}", (P, 4, P)) for i in range(2)]
        psP = at.ps("psP", (P, KP, P))
        psG = at.ps("psG", (P, 2, HALF))
        psE = at.ps("psE", (P, 2, HALF))
        NW = 2 * (KD + KP)
        consts_in, eps_set = at.sem("consts_in"), at.sem("eps_set")
        w_in = [at.sem(f"w_in{i}") for i in range(2)]
        whi_ok, wlo_ok = at.sem("whi_ok"), at.sem("wlo_ok")
        s = {n: at.sem(n) for n in ("idx_ok ha_ok hb_ok aT_ps pT_ps ahi_ok phi_ok alo_ok plo_ok g_ps e_ps sq_ok lnm_ok rs_ok ple_ok pleg_ok sg_ok sp_ok o_ok").split()}
        h_in, y_in, p_sem, stored = ([at.sem(f"{n}{i}") for i in range(2)] for n in ("h_in", "y_in", "p_in", "stored"))

        def later(t, n=1):
            return not isinstance(t, int) or t >= n

        def done(eng, name, t, n=1, per=1):
            if eng in (nc.sync, nc.gpsimd):
                at.hold(eng, s[name], t * per + n)
            else:
                eng.wait_ge(s[name], t * per + n)

        def tiles(eng, body):
            body(0, 0)
            body(1, 1)
            with eng.Fori(1, NT // 2) as pair:
                body(pair * 2, 0)
                body(pair * 2 + 1, 1)

        with nc.Block() as block:
            @block.sync
            def _(sp):
                sp.dma_start(ident[:], ident_in).then_inc(consts_in, 16)
                sp.dma_start(dest[:].rearrange("p a t -> p (a t)"), dest_in).then_inc(consts_in, 16)
                sp.dma_start(wgt[:].rearrange("p a t -> p (a t)"), wgt_in).then_inc(consts_in, 16)
                sp.dma_start(gain[:], ple_norm.broadcast_to([P, D])).then_inc(consts_in, 16)

                def load(t, b):
                    if later(t, 2):
                        done(sp, "o_ok", t - 2)
                        done(sp, "pT_ps", t - 2)
                    sp.dma_start(h[:, b], h1[bass.ds(t * P, P), :]).then_inc(h_in[b], 16)
                    sp.dma_start(pp[:, b], p_in[bass.ds(t * P, P), :]).then_inc(p_sem[b], 16)

                load(0, 0)
                load(1, 1)
                for i in range(NW):
                    if i >= 2:
                        sp.wait_ge(whi_ok, i - 1)
                        sp.wait_ge(wlo_ok, i - 1)
                    k, n = i // 2, i % 2
                    src = ple_proj[k * P:(k + 1) * P] if k < KP else ple_gate[(k - KP) * P:(k - KP + 1) * P]
                    sp.dma_start(wraw[:, n], src[:, n * HALF:(n + 1) * HALF]).then_inc(w_in[n], 16)
                with sp.Fori(1, NT // 2) as pair:
                    load(pair * 2, 0)
                    load(pair * 2 + 1, 1)

            @block.gpsimd
            def _(pool):
                pool.wait_ge(consts_in, 64)

                def gather(t, b):
                    done(pool, "idx_ok", t, 2, 2)
                    if later(t, 2):
                        done(pool, "hb_ok", t - 2)
                    for a in range(2):
                        pool.indirect_dma_start(y[:, b, a], None, y_rows, bass.IndirectOffsetOnAxis(ap=idx[b][a][:], axis=0)).then_inc(y_in[b], 16)

                def finish(t, b):
                    done(pool, "ple_ok", t)
                    pool.tensor_tensor(ple[:], ple[:], gain[:], ALU.mult).then_inc(s["pleg_ok"], 1)
                    done(pool, "pleg_ok", t)
                    done(pool, "sg_ok", t)
                    pool.tensor_tensor(ple[:], ple[:], sg[:], ALU.mult).then_inc(s["sp_ok"], 1)
                    done(pool, "o_ok", t)
                    pool.dma_start(out[bass.ds(t * P, P), :], o[:, b]).then_inc(stored[b], 16)

                gather(0, 0)
                gather(1, 1)
                with pool.Fori(1, NT // 2) as pair:
                    gather(pair * 2, 0)
                    finish(pair * 2 - 2, 0)
                    gather(pair * 2 + 1, 1)
                    finish(pair * 2 - 1, 1)
                finish(NT - 2, 0)
                finish(NT - 1, 1)
                for b in range(2):
                    pool.wait_ge(stored[b], NT // 2 * 16)

            @block.scalar
            def _(act):
                for i in range(NW):
                    act.wait_ge(w_in[i % 2], 16 * (i // 2 + 1))
                    act.activation(whi[:, i // 2, (i % 2) * HALF:(i % 2 + 1) * HALF], wraw[:, i % 2], ACT.Copy).then_inc(whi_ok, 1)
                act.wait_ge(eps_set, 1)

                def front(t, b):
                    done(act, "pT_ps", t)
                    if later(t, 2):
                        done(act, "e_ps", t - 2)
                        done(act, "g_ps", t - 2)
                    act.activation(ahi[:, b, 0:KP], psP[:], ACT.Copy).then_inc(s["phi_ok"], 1)
                    for i in range(2):
                        done(act, "aT_ps", t, i + 1, 2)
                        act.activation(ahi[:, b, KP + i * 4:KP + (i + 1) * 4], psT[i][:], ACT.Copy).then_inc(s["ahi_ok"], 1)

                def back(t, b):
                    done(act, "e_ps", t)
                    if later(t):
                        done(act, "sq_ok", t - 1)
                    act.activation(sq[:], psE[:].rearrange("p a n -> p (a n)"), ACT.Square, accum_out=ss[:, b:b + 1]).then_inc(s["sq_ok"], 1)
                    done(act, "sq_ok", t)
                    act.activation(lnm[:, b:b + 1], ss[:, b:b + 1], ACT.Ln, bias=eps[:], scale=1.0 / D).then_inc(s["lnm_ok"], 1)
                    done(act, "lnm_ok", t)
                    act.activation(rs[:, b:b + 1], lnm[:, b:b + 1], ACT.Exp, scale=-0.5).then_inc(s["rs_ok"], 1)
                    done(act, "rs_ok", t)
                    if later(t):
                        done(act, "o_ok", t - 1)
                    act.activation(ple[:], psE[:].rearrange("p a n -> p (a n)"), ACT.Copy, scale=rs[:, b:b + 1]).then_inc(s["ple_ok"], 1)
                    done(act, "g_ps", t)
                    act.activation(sg[:], psG[:].rearrange("p a n -> p (a n)"), ACT.Sigmoid).then_inc(s["sg_ok"], 1)

                staggered(act, front, back)

            @block.vector
            def _(dve):
                dve.memset(eps[:], EPS).then_inc(eps_set, 1)
                dve.wait_ge(consts_in, 64)

                def index(t, b):
                    if later(t, 2):
                        dve.wait_ge(y_in[b], (t - b) * 16)
                    for a in range(2):
                        dve.tensor_copy(idx[b][a][:], dest[:, a, bass.ds(t, 1)]).then_inc(s["idx_ok"], 1)

                index(0, 0)
                index(1, 1)
                for i in range(NW):
                    dve.wait_ge(whi_ok, i + 1)
                    cut = slice((i % 2) * HALF, (i % 2 + 1) * HALF)
                    dve.tensor_tensor(wlo[:, i // 2, cut], wraw[:, i % 2], whi[:, i // 2, cut].bitcast(F32), ALU.subtract).then_inc(wlo_ok, 1)

                def add(t, b, ahead=True):
                    dve.wait_ge(h_in[b], (t - b + 2) * 8)
                    dve.wait_ge(y_in[b], (t - b + 2) * 16)
                    dve.scalar_tensor_tensor(h[:, b], y[:, b, 0], wgt[:, 0, bass.ds(t, 1)], h[:, b], ALU.mult, ALU.add).then_inc(s["ha_ok"], 1)
                    done(dve, "ha_ok", t)
                    dve.scalar_tensor_tensor(h[:, b], y[:, b, 1], wgt[:, 1, bass.ds(t, 1)], h[:, b], ALU.mult, ALU.add).then_inc(s["hb_ok"], 1)
                    if ahead:
                        index(t + 2, b)

                def split(t, b):
                    done(dve, "phi_ok", t)
                    dve.tensor_tensor(alo[:, b, 0:KP], psP[:], ahi[:, b, 0:KP].bitcast(F32), ALU.subtract).then_inc(s["plo_ok"], 1)
                    for i in range(2):
                        done(dve, "ahi_ok", t, i + 1, 2)
                        cut = slice(KP + i * 4, KP + (i + 1) * 4)
                        dve.tensor_tensor(alo[:, b, cut], psT[i][:], ahi[:, b, cut].bitcast(F32), ALU.subtract).then_inc(s["alo_ok"], 1)

                def back(t, b):
                    done(dve, "sp_ok", t)
                    if later(t, 2):
                        dve.wait_ge(stored[b], (t - b) * 8)
                    dve.tensor_tensor(o[:, b], h[:, b], ple[:], ALU.add).then_inc(s["o_ok"], 1)

                add(0, 0)
                add(1, 1)
                split(0, 0)
                split(1, 1)
                back(0, 0)
                with dve.Fori(1, NT // 2 - 1) as pair:
                    add(pair * 2, 0)
                    split(pair * 2, 0)
                    back(pair * 2 - 1, 1)
                    add(pair * 2 + 1, 1)
                    split(pair * 2 + 1, 1)
                    back(pair * 2, 0)
                add(NT - 2, 0, False)
                split(NT - 2, 0)
                back(NT - 3, 1)
                add(NT - 1, 1, False)
                split(NT - 1, 1)
                back(NT - 2, 0)
                back(NT - 1, 1)

            @block.tensor
            def _(pe):
                pe.wait_ge(consts_in, 64)

                def front(t, b):
                    pe.wait_ge(p_sem[b], (t - b + 2) * 8)
                    if later(t):
                        done(pe, "plo_ok", t - 1)
                    for j in range(KP):
                        last = pe.transpose(psP[:, j], pp[:, b, j * P:(j + 1) * P], ident[:])
                    last.then_inc(s["pT_ps"], 1)
                    done(pe, "hb_ok", t)
                    for i in range(2):
                        if later(t):
                            done(pe, "alo_ok", t - 1, i + 1, 2)
                        for j in range(4):
                            last = pe.transpose(psT[i][:, j], h[:, b, (i * 4 + j) * P:(i * 4 + j + 1) * P], ident[:])
                        last.then_inc(s["aT_ps"], 1)

                def multiply(t, b):
                    done(pe, "plo_ok", t)
                    if isinstance(t, int) and t == 0:
                        pe.wait_ge(wlo_ok, NW)
                    for ps, k0, k1, name, free in ((psE, 0, KP, "e_ps", "ple_ok"), (psG, KP, KP + KD, "g_ps", "sg_ok")):
                        if k0:
                            done(pe, "alo_ok", t, 2, 2)
                        if later(t):
                            done(pe, free, t - 1)
                        for n in range(2):
                            cut = slice(n * HALF, (n + 1) * HALF)
                            for k in range(k0, k1):
                                for i, (l, r) in enumerate(((ahi, whi), (ahi, wlo), (alo, whi))):
                                    last = pe.matmul(ps[:, n], l[:, b, k], r[:, k, cut], start=(k == k0 and i == 0),
                                                     stop=(k == k1 - 1 and i == 2))
                        last.then_inc(s[name], 1)

                front(0, 0)
                front(1, 1)
                multiply(0, 0)
                with pe.Fori(1, NT // 2) as pair:
                    front(pair * 2, 0)
                    multiply(pair * 2 - 1, 1)
                    front(pair * 2 + 1, 1)
                    multiply(pair * 2, 0)
                multiply(NT - 1, 1)


def staggered(eng, front, back):
    front(0, 0)
    front(1, 1)
    back(0, 0)
    with eng.Fori(1, NT // 2) as pair:
        front(pair * 2, 0)
        back(pair * 2 - 1, 1)
        front(pair * 2 + 1, 1)
        back(pair * 2, 0)
    back(NT - 1, 1)


def build(nc, a, out):
    def scratch(name, shape, dt=F32):
        return nc.dram_tensor(name, list(shape), dt, kind="Internal").ap()

    hgrn_q, hgrn_f, hgrn_k = (scratch(f"hgrn_{n}", (HW, S)) for n in "qfk")
    tok = scratch("tok", (S, 5 * HW))
    mix = scratch("mix", (S, D))
    h1 = scratch("h1", (S, D))
    xn_rows = scratch("xn_rows", (S + 1, D))
    logits = scratch("logits", (P, NT * NE))
    row_tok = scratch("row_tok", (NROW, 1), I32)
    dest = scratch("dest", (P, 2 * NT), I32)
    wgt = scratch("wgt", (P, 2 * NT))
    plan = scratch("plan", (P, 2 * NB + NE), I32)
    y_rows = scratch("y_rows", (NROW, D))
    x, ident = a["x"].rearrange("a s d -> (a s) d"), a["ident"]

    project_in(nc, x, a["mix_norm"], a["w_in"][0], ident, hgrn_q, hgrn_f, hgrn_k, tok)
    recurrence(nc, hgrn_q, hgrn_f, hgrn_k, tok, a["hgrn_lb"], a["hgrn_out_norm"], ident, a["masks"], a["resets"], mix)
    attention(nc, tok, a["q_norm"], a["k_norm"], a["lam_q1"], a["lam_k1"], a["lam_q2"], a["lam_k2"], a["diff_subln"],
              ident, a["causal"], mix)
    project_out(nc, mix, x, a["w_out"][0], a["ffn_norm"], a["w_router"], ident, h1, xn_rows, logits)
    route(nc, logits, a["below"], a["upper"], a["firsts"], a["blocks"], a["tokens"], row_tok, dest, wgt, plan)
    experts(nc, xn_rows, row_tok, plan, a["w_gate"], a["w_up"], a["w_down"], ident, y_rows)
    embed(nc, h1, y_rows, dest, wgt, a["p"].rearrange("a b s d -> (a b s) d"), a["ple_proj"][0], a["ple_norm"],
          a["ple_gate"][0], ident, out.rearrange("a s d -> (a s) d"))


def shape_constants():
    import numpy as np

    s, t = np.meshgrid(np.arange(P), np.arange(P), indexing="ij")
    masks = np.zeros((P, LV, P), np.int32)
    for i, half in enumerate((CH, *HALVES)):
        masks[:, i] = (s // (2 * half) == t // (2 * half)) & (s // half % 2 == 0) & (t // half % 2 == 1)
    base = HALVES[-1]
    masks[:, LV - 1] = (s // base == t // base) & (s <= t)
    resets = np.ones((P, NH * P // CH, CH), np.float32)
    resets[:, :, 0] = 0
    upper = np.stack([s < t, np.ones((P, P), bool)], 1).astype(np.float32)
    firsts = np.ones((P, NE, NT), np.float32)
    firsts[:, :, 0] = 0
    j = np.arange(GE)
    return {
        "ident": np.eye(P, dtype=np.float32),
        "causal": np.where(t > s, -1e30, 0.0).astype(np.float32),
        "masks": masks,
        "resets": resets.reshape(P, NH * P),
        "below": np.tile((j[None, :] < j[:, None]).astype(np.float32), (P, 1, 1)),
        "upper": upper,
        "firsts": firsts,
        "blocks": np.tile(np.arange(NB, dtype=np.float32), (P, 1)),
        "tokens": (np.arange(NT)[None, :] * P + np.arange(P)[:, None]).astype(np.int32),
    }


INPUTS = ("x p mix_norm w_in hgrn_lb hgrn_out_norm q_norm k_norm lam_q1 lam_k1 lam_q2 lam_k2 diff_subln w_out "
          "ffn_norm w_router w_gate w_up w_down ple_proj ple_norm ple_gate").split()


def kernel(**inputs):
    import numpy as np
    import concourse.bacc as bacc
    from concourse.bass_utils import run_bass_kernel_spmd

    nc = bacc.Bacc("TRN2", target_bir_lowering=False, num_devices=1)
    arrays = {n: np.ascontiguousarray(inputs[n]) for n in INPUTS} | shape_constants()
    aps = {n: nc.dram_tensor(n, v.shape, mybir.dt.from_np(v.dtype), kind="ExternalInput").ap() for n, v in arrays.items()}
    out = nc.dram_tensor("out", (1, S, D), F32, kind="ExternalOutput").ap()
    build(nc, aps, out)
    return run_bass_kernel_spmd(nc, [arrays], core_ids=[0]).results[0]["out"]
```

```python
from contextlib import ExitStack

import concourse.bass as bass
from concourse import mybir

F32 = mybir.dt.float32
F32R = mybir.dt.float32r
BF16 = mybir.dt.bfloat16
I32 = mybir.dt.int32

ALU = mybir.AluOpType
ACT = mybir.ActivationFunctionType
AX = mybir.AxisListType
P = 128

D = 1024
S = 2048
KD = D // P
NT = S // P
HW = 512
NH = HW // P
EPS = 1e-6


class Place:

    def __init__(self, nc, stack, stage):
        self.nc, self.stack, self.stage, self.sems, self.held = nc, stack, stage, [], None
        stack.callback(self.clear)

    def sb(self, name, shape, dt=F32):
        return self.stack.enter_context(self.nc.sbuf_tensor(f"{self.stage}_{name}", shape, dt))

    def ps(self, name, shape=(P, 512)):
        return self.stack.enter_context(self.nc.psum_tensor(f"{self.stage}_{name}", list(shape), F32))

    def clear(self):
        self.nc.clear_and_free_semaphores(self.sems)
        self.nc.all_engine_barrier()

    def hold(self, eng, sem, value):
        eng.wait_ge(sem, value)
        if not isinstance(value, int):
            if self.held is None:
                self.held = self.sem("held")
            eng.sem_inc(self.held, 1)

    def sem(self, name):
        self.sems.append(self.nc.alloc_semaphore(f"{self.stage}_{name}"))
        return self.sems[-1]


GT = 4
GW = GT * P
NG = NT // GT
SLICES = [(2 * HW, HW, "zi"), (3 * HW, HW, "zg"), (4 * HW, HW, "dq"), (5 * HW, HW, "dk"), (6 * HW, HW, "dv"),
          (0, HW, "zq"), (HW, HW // 2, "zf0"), (HW + HW // 2, HW // 2, "zf1")]
NSL = len(SLICES)


def project_in(nc, x, mix_norm, w_in, ident_in, hgrn_q, hgrn_f, hgrn_k, tok):
    groups = [[(s, j) for j in range(GT if s < 5 else w // P)] for s, (_, w, _) in enumerate(SLICES)]
    NGRP = sum(len(g) for g in groups)
    upto = [sum(len(g) for g in groups[:s + 1]) for s in range(NSL)]
    NST = 8
    with ExitStack() as stack:
        at = Place(nc, stack, "in")
        ident = at.sb("ident", [P, P])
        gain = at.sb("gain", [P, KD])
        eps = at.sb("eps", [P, 1])
        xs = at.sb("xs", [P, 2, D])
        xn = at.sb("xn", [P, D])
        ss = at.sb("ss", [P, GT])
        lnms = at.sb("lnms", [P, GT])
        rstd = at.sb("rstd", [P, GT])
        xT = at.sb("xT", [P, KD, GW])
        hhi = at.sb("hhi", [P, KD, GW], F32R)
        hlo = at.sb("hlo", [P, KD, GW], F32R)
        wraw = at.sb("wraw", [P, 2, KD, HW])
        whi = at.sb("whi", [P, 2, KD, HW], F32R)
        wlo = at.sb("wlo", [P, 2, KD, HW], F32R)
        st = at.sb("st", [P, NST, GW])
        psT = [at.ps(f"psT{i}") for i in range(2)]
        psM = [at.ps(f"psM{i}") for i in range(4)]
        NM = len(psM)

        consts_in = at.sem("consts_in")
        x_in = [at.sem(f"x_in{i}") for i in range(2)]
        w_in_sem = [at.sem(f"w_in{i}") for i in range(2)]
        eps_set = at.sem("eps_set")
        squares = at.sem("squares")
        logs = at.sem("logs")
        rstd_ok = at.sem("rstd_ok")
        xn_ok = at.sem("xn_ok")
        xT_ps = at.sem("xT_ps")
        xT_ok = at.sem("xT_ok")
        hi_ok = at.sem("hi_ok")
        lo_ok = at.sem("lo_ok")
        whi_ok = at.sem("whi_ok")
        wlo_ok = at.sem("wlo_ok")
        mm_ok = at.sem("mm_ok")
        sig_ok = at.sem("sig_ok")
        out_ok = at.sem("out_ok")
        out_ok2 = at.sem("out_ok2")
        stored = [at.sem(f"stored{i}") for i in range(NST)]

        stores = []
        for s in range(NSL):
            for (_, j) in groups[s]:
                n = upto[s] - len(groups[s]) + j
                for part in range(2 if s >= 6 else 1):
                    stores.append((s, j, n, part))
        NSTO = len(stores)
        slot = {(s, j, part): k % NST for k, (s, j, n, part) in enumerate(stores)}
        ordinal = {(s, j, part): k for k, (s, j, n, part) in enumerate(stores)}
        assert NSTO % NST == 0 and NGRP % NM == 0, (NSTO, NGRP)
        PER = NSTO // NST

        def x_row(g, t):
            return x[bass.ds((g * GT + t) * P, P), :]

        def by_vector(s, j):
            return s in (1, 5) or (s in (0, 2, 3, 4) and j % 2 == 0)

        order = {}
        nv = ns = 0
        for (s, j, n, part) in stores:
            if by_vector(s, j):
                nv += 1
                order[(s, j, part)] = (out_ok, nv)
            else:
                ns += 1
                order[(s, j, part)] = (out_ok2, ns)
        writer_total = {False: nv, True: ns}

        def writer(s, j, part):
            return order[(s, j, part)]

        def slot_free(eng, g, s, j, part):
            m = ordinal[(s, j, part)] // NST
            if not (isinstance(g, int) and g == 0 and m == 0):
                eng.wait_ge(stored[slot[(s, j, part)]], (g * PER + m) * 16)

        with nc.Block() as block:
            @block.sync
            def _(sp):
                sp.dma_start(ident[:], ident_in).then_inc(consts_in, 16)
                sp.dma_start(gain[:], mix_norm.rearrange("a (k p) -> p (a k)", p=P), allow_slow_non_contiguous=True).then_inc(consts_in, 16)

                def load_x(g, t, n):
                    sp.wait_ge(xn_ok, n - 1) if not isinstance(n, int) or n >= 2 else None
                    sp.dma_start(xs[:, t % 2, :], x_row(g, t)).then_inc(x_in[t % 2], 16)

                def load_w(g, s):
                    c0, w, _ = SLICES[s]
                    if not (isinstance(g, int) and g == 0 and s < 2):
                        sp.wait_ge(whi_ok, g * NSL + s - 1)
                        sp.wait_ge(wlo_ok, g * NSL + s - 1)
                    sp.dma_start(wraw[:, s % 2, :, 0:w], w_in[:, c0:c0 + w].rearrange("(k p) n -> p k n", p=P)) \
                        .then_inc(w_in_sem[s % 2], 16)

                for t in range(GT):
                    load_x(0, t, t)
                    if t == 1:
                        load_w(0, 0)
                for s in range(1, 3):
                    load_w(0, s)
                sp.wait_ge(xn_ok, GT)

                def group(g, last):
                    for s in range(3, NSL):
                        load_w(g, s)
                        if not last and s - 3 < GT:
                            load_x(g + 1, s - 3, (g + 1) * GT + s - 3)
                    if not last:
                        for s in range(3):
                            load_w(g + 1, s)

                group(0, False)
                with sp.Fori(1, NG - 1) as g:
                    group(g, False)
                group(NG - 1, True)

            @block.gpsimd
            def _(pool):
                def group(g):
                    for (s, j, n, part) in stores:
                        k = slot[(s, j, part)]
                        sem, cnt = writer(s, j, part)
                        at.hold(pool, sem, g * writer_total[sem is out_ok2] + cnt)
                        if s < 5:
                            dst = tok[bass.ds((g * GT + j) * P, P), s * HW:(s + 1) * HW]
                        elif s == 5:
                            dst = hgrn_q[j * P:(j + 1) * P, bass.ds(g * GW, GW)]
                        else:
                            r = (s - 6) * (HW // 2) + j * P
                            dst = (hgrn_f, hgrn_k)[part][r:r + P, bass.ds(g * GW, GW)]
                        pool.dma_start(dst, st[:, k, :]).then_inc(stored[k], 16)

                with pool.Fori(0, NG) as g:
                    group(g)
                for k in range(NST):
                    pool.wait_ge(stored[k], 16 * PER * NG)

            @block.scalar
            def _(act):
                def norm_stats(g, t):
                    n = g * GT + t
                    act.wait_ge(x_in[t % 2], (g * (GT // 2) + t // 2 + 1) * 16)
                    if not (isinstance(g, int) and g == 0 and t == 0):
                        act.wait_ge(xT_ps, n * 2)
                    act.activation(xn[:], xs[:, t % 2, :], ACT.Square, accum_out=ss[:, t:t + 1]).then_inc(squares, 1)
                    act.wait_ge(squares, n + 1)
                    act.activation(lnms[:, t:t + 1], ss[:, t:t + 1], ACT.Ln, bias=eps[:], scale=1.0 / D).then_inc(logs, 1)
                    act.wait_ge(logs, n + 1)
                    act.activation(rstd[:, t:t + 1], lnms[:, t:t + 1], ACT.Exp, scale=-0.5).then_inc(rstd_ok, 1)
                    act.wait_ge(rstd_ok, n + 1)
                    act.activation(xn[:], xs[:, t % 2, :], ACT.Copy, scale=rstd[:, t:t + 1]).then_inc(xn_ok, 1)

                def split_h(g, t):
                    act.wait_ge(xT_ok, (g * GT + t + 1) * 2)
                    if not (isinstance(g, int) and g == 0) and t == 0:
                        act.wait_ge(mm_ok, g * NGRP)
                    act.activation(hhi[:, :, t * P:(t + 1) * P], xT[:, :, t * P:(t + 1) * P], ACT.Copy).then_inc(hi_ok, 1)

                def split_w(g, s):
                    w = SLICES[s][1]
                    act.wait_ge(w_in_sem[s % 2], (g * (NSL // 2) + s // 2 + 1) * 16)
                    if not (isinstance(g, int) and g == 0 and s < 2):
                        before = g * NGRP + (upto[s - 2] if s >= 2 else upto[s - 2 + NSL] - NGRP)
                        act.wait_ge(mm_ok, before)
                    act.activation(whi[:, s % 2, :, 0:w], wraw[:, s % 2, :, 0:w], ACT.Copy).then_inc(whi_ok, 1)

                def evacuate(g, s):
                    for (_, j) in groups[s]:
                        n = upto[s] - len(groups[s]) + j
                        src = psM[n % NM]
                        if s in (1, 5):
                            act.wait_ge(mm_ok, g * NGRP + n + 1)
                            slot_free(act, g, s, j, 0)
                            act.activation(st[:, slot[(s, j, 0)], :], src[:], ACT.Sigmoid).then_inc(sig_ok, 1)
                        elif s >= 6:
                            act.wait_ge(mm_ok, g * NGRP + n + 1)
                            for part in range(2):
                                slot_free(act, g, s, j, part)
                                act.activation(st[:, slot[(s, j, part)], :], src[:], ACT.Sigmoid,
                                               scale=(1.0, -1.0)[part]).then_inc(out_ok2, 1)
                        elif not by_vector(s, j):
                            act.wait_ge(mm_ok, g * NGRP + n + 1)
                            slot_free(act, g, s, j, 0)
                            act.activation(st[:, slot[(s, j, 0)], :], src[:], ACT.Copy).then_inc(out_ok2, 1)

                act.wait_ge(eps_set, 1)
                for t in range(GT):
                    norm_stats(0, t)
                split_w(0, 0)

                def body(g, last):
                    for t in range(GT):
                        split_h(g, t)
                    for s in range(NSL):
                        if s + 1 < NSL:
                            split_w(g, s + 1)
                        elif not last:
                            split_w(g + 1, 0)
                        if 2 <= s < 2 + GT and not last:
                            norm_stats(g + 1, s - 2)
                        evacuate(g, s)

                body(0, False)
                with act.Fori(1, NG - 1) as g:
                    body(g, False)
                body(NG - 1, True)

            @block.vector
            def _(dve):
                dve.memset(eps[:], EPS).then_inc(eps_set, 1)
                dve.wait_ge(consts_in, 32)

                def take_xT(g, t):
                    for half in range(2):
                        dve.wait_ge(xT_ps, (g * GT + t) * 2 + half + 1)
                        if not (isinstance(g, int) and g == 0) and t == 0 and half == 0:
                            dve.wait_ge(hi_ok, g * GT)
                            dve.wait_ge(lo_ok, g * GT)
                        k0 = half * KD // 2
                        dve.tensor_tensor(xT[:, k0:k0 + KD // 2, t * P:(t + 1) * P],
                                          psT[half][:].rearrange("p (k t) -> p k t", k=KD // 2),
                                          gain[:, k0:k0 + KD // 2].unsqueeze(2).to_broadcast([P, KD // 2, P]),
                                          ALU.mult).then_inc(xT_ok, 1)

                def split_h(g, t):
                    dve.wait_ge(hi_ok, g * GT + t + 1)
                    dve.tensor_tensor(hlo[:, :, t * P:(t + 1) * P], xT[:, :, t * P:(t + 1) * P],
                                      hhi[:, :, t * P:(t + 1) * P].bitcast(F32), ALU.subtract).then_inc(lo_ok, 1)

                def split_w(g, s):
                    w = SLICES[s][1]
                    dve.wait_ge(whi_ok, g * NSL + s + 1)
                    dve.tensor_tensor(wlo[:, s % 2, :, 0:w], wraw[:, s % 2, :, 0:w],
                                      whi[:, s % 2, :, 0:w].bitcast(F32), ALU.subtract).then_inc(wlo_ok, 1)

                def evacuate(g, s):
                    for (_, j) in groups[s]:
                        n = upto[s] - len(groups[s]) + j
                        src = psM[n % NM]
                        if s in (1, 5):
                            i = j if s == 1 else GT + j
                            dve.wait_ge(sig_ok, g * 2 * GT + i + 1)
                            o = st[:, slot[(s, j, 0)], :]
                            dve.tensor_tensor(o, src[:], o, ALU.mult).then_inc(out_ok, 1)
                        elif by_vector(s, j):
                            dve.wait_ge(mm_ok, g * NGRP + n + 1)
                            slot_free(dve, g, s, j, 0)
                            dve.tensor_copy(st[:, slot[(s, j, 0)], :], src[:]).then_inc(out_ok, 1)

                for t in range(GT):
                    take_xT(0, t)
                split_w(0, 0)

                def body(g, last):
                    for t in range(GT):
                        split_h(g, t)
                    for s in range(NSL):
                        if s + 1 < NSL:
                            split_w(g, s + 1)
                        elif not last:
                            split_w(g + 1, 0)
                        if 3 <= s < 3 + GT and not last:
                            take_xT(g + 1, s - 3)
                        evacuate(g, s)

                body(0, False)
                with dve.Fori(1, NG - 1) as g:
                    body(g, False)
                body(NG - 1, True)

            @block.tensor
            def _(pe):
                pe.wait_ge(consts_in, 32)

                def transpose_x(g, t):
                    pe.wait_ge(xn_ok, g * GT + t + 1)
                    for half in range(2):
                        if not (isinstance(g, int) and g == 0 and t == 0):
                            pe.wait_ge(xT_ok, (g * GT + t) * 2 - 1 + half)
                        for i in range(KD // 2):
                            k = half * KD // 2 + i
                            last = pe.transpose(psT[half][:, i * P:(i + 1) * P], xn[:, k * P:(k + 1) * P], ident[:])
                        last.then_inc(xT_ps, 1)

                def bank_free(g, s, j):
                    n = upto[s] - len(groups[s]) + j - NM
                    back = n < 0
                    if back and isinstance(g, int) and g == 0:
                        return
                    if back:
                        n += NGRP
                    s2 = next(i for i in range(NSL) if n < upto[i])
                    j2 = n - (upto[s2] - len(groups[s2]))
                    sem, cnt = writer(s2, j2, 1 if s2 >= 6 else 0)
                    total = writer_total[sem is out_ok2]
                    pe.wait_ge(sem, g * total + (cnt - total if back else cnt))

                def multiply(g, s):
                    pe.wait_ge(wlo_ok, g * NSL + s + 1)
                    pe.wait_ge(whi_ok, g * NSL + s + 1)
                    b = s % 2
                    for (_, j) in groups[s]:
                        n = upto[s] - len(groups[s]) + j
                        if s == 0:
                            pe.wait_ge(hi_ok, g * GT + j + 1)
                            pe.wait_ge(lo_ok, g * GT + j + 1)
                        bank_free(g, s, j)
                        out = psM[n % NM][:]
                        cut = slice(j * P, (j + 1) * P)
                        for k in range(KD):
                            if s < 5:
                                three = ((hhi[:, k, cut], whi[:, b, k, :]), (hhi[:, k, cut], wlo[:, b, k, :]),
                                         (hlo[:, k, cut], whi[:, b, k, :]))
                            else:
                                three = ((whi[:, b, k, cut], hhi[:, k, :]), (whi[:, b, k, cut], hlo[:, k, :]),
                                         (wlo[:, b, k, cut], hhi[:, k, :]))
                            for i, (l, r) in enumerate(three):
                                last = pe.matmul(out, l, r, start=(k == 0 and i == 0), stop=(k == KD - 1 and i == 2))
                        last.then_inc(mm_ok, 1)

                for t in range(GT):
                    transpose_x(0, t)

                def body(g, last):
                    for s in range(NSL):
                        if 3 <= s < 3 + GT and not last:
                            transpose_x(g + 1, s - 3)
                        multiply(g, s)

                body(0, False)
                with pe.Fori(1, NG - 1) as g:
                    body(g, False)
                body(NG - 1, True)


CH = 64
MIN_FORGET = 1e-6
HALVES = (32, 16, 8, 4)
LV = 2 + len(HALVES)


def recurrence(nc, hgrn_q, hgrn_f, hgrn_k, tok, hgrn_lb, out_norm, ident_in, masks_in, resets_in, mix):
    with ExitStack() as stack:
        at = Place(nc, stack, "rec")
        ident = at.sb("ident", [P, P])
        masks = at.sb("masks", [P, LV, P], I32)
        resets = at.sb("resets", [P, NH * P])
        lb_in = at.sb("lb_in", [P, NH])
        lbs = at.sb("lbs", [P, 5, NH])
        gain = at.sb("gain", [P, P])
        eps = at.sb("eps", [P, 1])
        W4 = [P, 2, NH, P]
        q, f, k, v, g = (at.sb(n, W4) for n in ("q", "f", "k", "v", "g"))
        fm, fl, lf, cum = (at.sb(n, [P, NH, P]) for n in ("fm", "fl", "lf", "cum"))
        d64, dB = at.sb("d64", [P, NH, P]), at.sb("dB", [P, NH, P])
        dH = at.sb("dH", [P, len(HALVES), NH, P])
        e0, eK = at.sb("e0", [P, NH, P]), at.sb("eK", [P, NH, P])
        eH = at.sb("eH", [P, len(HALVES), NH, P])
        eBq, eBk = at.sb("eBq", [P, NH, P]), at.sb("eBk", [P, NH, P])
        ql = at.sb("ql", [P, 2, LV, NH, P])
        kl = at.sb("kl", [P, 2, LV, NH, P])
        qI, kD = at.sb("qI", W4), at.sb("kD", W4)
        eL = at.sb("eL", [P, 2, NH])
        sT = at.sb("sT", W4)
        kDT = at.sb("kDT", W4)
        state = at.sb("state", [P, 2, NH, P])
        osq = at.sb("osq", [P, NH, P])
        oss, oln, ors = (at.sb(n, [P, NH]) for n in ("oss", "oln", "ors"))
        gg = at.sb("gg", W4)
        on = at.sb("on", [P, NH, P])
        o = at.sb("o", W4)
        psA = [at.ps(f"psA{i}", (P, NH, P)) for i in range(3)]
        psK = at.ps("psK", (P, NH, P))
        psU = at.ps("psU", (P, NH, P))
        psO = [at.ps(f"psO{i}", (P, NH, P)) for i in range(2)]
        NA = len(psA)

        consts_in, init = at.sem("consts_in"), at.sem("init")
        lb_ok = at.sem("lb_ok")
        tile_in = [at.sem(f"tile_in{i}") for i in range(2)]
        names = ("fm_ok km_ok fl_ok0 fl_ok lf_ok cum_ok d64_ok dB_ok dH_ok e0_ok eK_ok eH_ok eB_ok q0_ok k0_ok qH_ok kH_ok qB_ok kB_ok "
                 "qI_ok kD_ok eL_ok qIc_ok kDc_ok kDT_ps kDT_ok lv_ps lv_ok upd_ps state_ok o_ps osq_ok oss_ok oln_ok ors_ok gg_ok on_ok o_ok").split()
        s = {n: at.sem(n) for n in names}
        stored = [at.sem(f"stored{i}") for i in range(2)]

        def later(t, n=1):
            return not isinstance(t, int) or t >= n

        def done(eng, name, t, n=1, per=1):
            if eng in (nc.sync, nc.gpsimd) or name == "lv_ps" and eng is nc.vector:
                at.hold(eng, s[name], t * per + n)
            else:
                eng.wait_ge(s[name], t * per + n)

        def second(x, H):
            return x.rearrange("p h (b t) -> p (h b) t", t=2 * H)[:, :, H:2 * H]

        def first_(x, H):
            return x.rearrange("p h (b t) -> p (h b) t", t=2 * H)[:, :, 0:H]

        def from_middle(x, H, at_):
            b = x.rearrange("p h (b t) -> p (h b) t", t=2 * H)
            return b, b[:, :, at_:at_ + 1].to_broadcast([P, NH * P // (2 * H), 2 * H])

        def tiles(eng, body):
            body(0, 0)
            body(1, 1)
            with eng.Fori(1, NT // 2) as pair:
                body(pair * 2, 0)
                body(pair * 2 + 1, 1)

        def staggered(eng, front, back):
            front(0, 0)
            front(1, 1)
            back(0, 0)
            with eng.Fori(1, NT // 2) as pair:
                front(pair * 2, 0)
                back(pair * 2 - 1, 1)
                front(pair * 2 + 1, 1)
                back(pair * 2, 0)
            back(NT - 1, 1)

        def psA_of(t, b, i):
            return psA[i % NA]

        with nc.Block() as block:
            @block.sync
            def _(sp):
                for dst, src in ((ident, ident_in), (masks, masks_in), (resets, resets_in)):
                    sp.dma_start(dst[:], src).then_inc(consts_in, 16)
                sp.dma_start(lb_in[:], hgrn_lb.rearrange("a (h d) -> d (a h)", d=P), allow_slow_non_contiguous=True).then_inc(consts_in, 16)
                sp.dma_start(gain[:], out_norm.broadcast_to([P, P])).then_inc(consts_in, 16)

                def load(t, b):
                    if later(t, 2):
                        done(sp, "lv_ps", t - 2, LV, LV)
                        done(sp, "fm_ok", t - 2)
                        done(sp, "o_ps", t - 2)
                        done(sp, "gg_ok", t - 2)
                    for dst, src in ((q, hgrn_q), (f, hgrn_f), (k, hgrn_k)):
                        sp.dma_start(dst[:, b], src.rearrange("(h d) t -> d h t", d=P)[:, :, bass.ds(t * P, P)]).then_inc(tile_in[b], 16)
                    for dst, c0 in ((v, 0), (g, HW)):
                        sp.dma_start(dst[:, b].rearrange("p h c -> p (h c)"), tok[bass.ds(t * P, P), c0:c0 + HW]).then_inc(tile_in[b], 16)

                tiles(sp, load)

            def tile_loaded(eng, t, b):
                at.hold(eng, tile_in[b], (t - b + 2) * 40)

            @block.gpsimd
            def _(pool):
                pool.wait_ge(lb_ok, 5)

                def front(t, b):
                    tile_loaded(pool, t, b)
                    if later(t):
                        done(pool, "fl_ok0", t - 1)
                    oml = lbs[:, 4].unsqueeze(2).to_broadcast([P, NH, P])
                    pool.tensor_tensor(fm[:], f[:, b], oml, ALU.mult).then_inc(s["fm_ok"], 1)
                    pool.tensor_tensor(k[:, b], k[:, b], oml, ALU.mult).then_inc(s["km_ok"], 1)
                    for i, H in enumerate(HALVES):
                        done(pool, "cum_ok", t)
                        if later(t):
                            done(pool, "eH_ok", t - 1, 2 * i + 2, 2 * len(HALVES))
                        a, m = from_middle(cum[:], H, H - 1)
                        pool.tensor_tensor(dH[:, i].rearrange("p h (b t) -> p (h b) t", t=2 * H), a, m, ALU.subtract).then_inc(s["dH_ok"], 1)
                    for i, H in enumerate(HALVES):
                        done(pool, "eH_ok", t, 2 * i + 2, 2 * len(HALVES))
                        done(pool, "km_ok", t)
                        if later(t, 2):
                            done(pool, "lv_ps", t - 2, LV, LV)
                        pool.tensor_tensor(first_(kl[:, b, 1 + i], H), first_(k[:, b], H), first_(eH[:, i], H), ALU.mult).then_inc(s["kH_ok"], 1)

                def back(t, b):
                    done(pool, "o_ok", t)
                    pool.dma_start(mix[bass.ds(t * P, P), 0:HW], o[:, b].rearrange("p h c -> p (h c)")).then_inc(stored[b], 16)

                staggered(pool, front, back)
                for b in range(2):
                    pool.wait_ge(stored[b], 16 * NT // 2)

            @block.scalar
            def _(act):
                act.preload_act_table_set("natural_log_exp_and_others")
                act.wait_ge(lb_ok, 1)
                act.activation(lbs[:, 1], lbs[:, 0], ACT.Exp).then_inc(lb_ok, 1)
                act.wait_ge(init, 1)

                def front(t, b):
                    done(act, "fl_ok", t)
                    if later(t):
                        done(act, "cum_ok", t - 1)
                    act.activation(lf[:], fl[:], ACT.Ln).then_inc(s["lf_ok"], 1)
                    done(act, "cum_ok", t)
                    if later(t):
                        done(act, "q0_ok", t - 1)
                        done(act, "kD_ok", t - 1)
                        done(act, "eL_ok", t - 1)
                        done(act, "qI_ok", t - 1)
                    act.activation(e0[:], cum[:], ACT.Exp).then_inc(s["e0_ok"], 1)
                    done(act, "d64_ok", t)
                    if later(t):
                        done(act, "k0_ok", t - 1)
                    act.activation(eK[:], d64[:], ACT.Exp).then_inc(s["eK_ok"], 1)
                    for i, H in enumerate(HALVES):
                        done(act, "dH_ok", t, i + 1, len(HALVES))
                        if later(t):
                            done(act, "qH_ok", t - 1, i + 1, len(HALVES))
                            done(act, "kH_ok", t - 1, i + 1, len(HALVES))
                        act.activation(second(eH[:, i], H), second(dH[:, i], H), ACT.Exp).then_inc(s["eH_ok"], 1)
                        act.activation(first_(eH[:, i], H), first_(dH[:, i], H), ACT.Exp, scale=-1.0).then_inc(s["eH_ok"], 1)
                    done(act, "dB_ok", t)
                    if later(t):
                        done(act, "qB_ok", t - 1)
                        done(act, "kB_ok", t - 1)
                    act.activation(eBq[:], dB[:], ACT.Exp).then_inc(s["eB_ok"], 1)
                    act.activation(eBk[:], dB[:], ACT.Exp, scale=-1.0).then_inc(s["eB_ok"], 1)
                    done(act, "q0_ok", t)
                    done(act, "k0_ok", t)
                    if later(t, 2):
                        done(act, "o_ps", t - 2)
                        done(act, "kDT_ps", t - 2)
                    act.activation(qI[:, b, :, 0:CH], ql[:, b, 0, :, 0:CH], ACT.Copy).then_inc(s["qIc_ok"], 1)
                    act.activation(kD[:, b, :, CH:P], kl[:, b, 0, :, CH:P], ACT.Copy).then_inc(s["kDc_ok"], 1)

                def back(t, b):
                    done(act, "kDT_ps", t)
                    if later(t, 2):
                        done(act, "upd_ps", t - 2)
                    act.activation(kDT[:, b], psK[:], ACT.Copy).then_inc(s["kDT_ok"], 1)
                    done(act, "o_ps", t)
                    if later(t):
                        done(act, "oss_ok", t - 1)
                    act.activation(osq[:], psO[b][:], ACT.Square).then_inc(s["osq_ok"], 1)
                    done(act, "oss_ok", t)
                    act.activation(oln[:], oss[:], ACT.Ln, bias=eps[:], scale=1.0 / P).then_inc(s["oln_ok"], 1)
                    done(act, "oln_ok", t)
                    if later(t):
                        done(act, "on_ok", t - 1)
                    act.activation(ors[:], oln[:], ACT.Exp, scale=-0.5).then_inc(s["ors_ok"], 1)

                staggered(act, front, back)

            @block.vector
            def _(dve):
                for n, (x, val) in enumerate(((eps[:], EPS), (state[:, 1], 0.0), (sT[:], 0.0), (ql[:], 0.0), (kl[:], 0.0))):
                    dve.memset(x, val).then_inc(init, 1)
                dve.wait_ge(consts_in, 80)
                dve.wait_ge(init, 5)
                dve.tensor_tensor(lbs[:, 0], lb_in[:], lb_in[:], ALU.subtract).then_inc(lb_ok, 1)
                dve.wait_ge(lb_ok, 2)
                dve.reciprocal(lbs[:, 2], lbs[:, 1]).then_inc(lb_ok, 1)
                dve.wait_ge(lb_ok, 3)
                dve.tensor_tensor(lbs[:, 2], lbs[:, 1], lbs[:, 2], ALU.mult).then_inc(init, 1)
                dve.wait_ge(init, 6)
                dve.tensor_tensor(lbs[:, 3], lbs[:, 2], lbs[:, 2], ALU.subtract).then_inc(lb_ok, 1)
                dve.wait_ge(lb_ok, 4)
                dve.tensor_scalar(lbs[:, 4], lbs[:, 3], -1.0, 1.0, ALU.mult, ALU.add).then_inc(lb_ok, 1)

                def front(t, b):
                    tile_loaded(dve, t, b)
                    done(dve, "fm_ok", t)
                    if later(t):
                        done(dve, "lf_ok", t - 1)
                    dve.tensor_tensor(fl[:], fm[:], lbs[:, 3].unsqueeze(2).to_broadcast([P, NH, P]), ALU.add).then_inc(s["fl_ok0"], 1)
                    done(dve, "fl_ok0", t)
                    dve.tensor_scalar(fl[:], fl[:], MIN_FORGET, None, ALU.max).then_inc(s["fl_ok"], 1)
                    done(dve, "lf_ok", t)
                    if later(t):
                        done(dve, "dH_ok", t - 1, len(HALVES), len(HALVES))
                        done(dve, "e0_ok", t - 1)
                        done(dve, "dB_ok", t - 1)
                    dve.tensor_tensor_scan(cum[:].rearrange("p h t -> p (h t)"), resets[:], lf[:].rearrange("p h t -> p (h t)"),
                                           0.0, ALU.mult, ALU.add).then_inc(s["cum_ok"], 1)
                    done(dve, "cum_ok", t)
                    if later(t):
                        done(dve, "eK_ok", t - 1)
                        done(dve, "eB_ok", t - 1, 2, 2)
                    a, m = from_middle(cum[:], CH // 2, CH - 1)
                    dve.tensor_tensor(d64[:].rearrange("p h (b t) -> p (h b) t", t=CH), m, a, ALU.subtract).then_inc(s["d64_ok"], 1)
                    a, m = from_middle(cum[:], 2, 1)
                    dve.tensor_tensor(dB[:].rearrange("p h (b t) -> p (h b) t", t=4), a, m, ALU.subtract).then_inc(s["dB_ok"], 1)
                    done(dve, "e0_ok", t)
                    if later(t, 2):
                        done(dve, "lv_ps", t - 2, LV, LV)
                    dve.tensor_tensor(ql[:, b, 0], q[:, b], e0[:], ALU.mult).then_inc(s["q0_ok"], 1)
                    done(dve, "eK_ok", t)
                    done(dve, "km_ok", t)
                    dve.tensor_tensor(kl[:, b, 0], k[:, b], eK[:], ALU.mult).then_inc(s["k0_ok"], 1)
                    if later(t, 2):
                        done(dve, "state_ok", t - 2)
                        done(dve, "o_ps", t - 2)
                        done(dve, "kDT_ps", t - 2)
                    dve.tensor_tensor(eL[:, b], e0[:, :, CH - 1], e0[:, :, P - 1], ALU.mult).then_inc(s["eL_ok"], 1)
                    done(dve, "k0_ok", t)
                    dve.tensor_tensor(qI[:, b, :, CH:P], ql[:, b, 0, :, CH:P], e0[:, :, CH - 1:CH].to_broadcast([P, NH, CH]), ALU.mult).then_inc(s["qI_ok"], 1)
                    dve.tensor_tensor(kD[:, b, :, 0:CH], kl[:, b, 0, :, 0:CH], e0[:, :, P - 1:P].to_broadcast([P, NH, CH]), ALU.mult).then_inc(s["kD_ok"], 1)
                    for i, H in enumerate(HALVES):
                        done(dve, "eH_ok", t, 2 * i + 1, 2 * len(HALVES))
                        dve.tensor_tensor(second(ql[:, b, 1 + i], H), second(q[:, b], H), second(eH[:, i], H), ALU.mult).then_inc(s["qH_ok"], 1)
                    done(dve, "eB_ok", t, 2, 2)
                    dve.tensor_tensor(ql[:, b, LV - 1], q[:, b], eBq[:], ALU.mult).then_inc(s["qB_ok"], 1)
                    dve.tensor_tensor(kl[:, b, LV - 1], k[:, b], eBk[:], ALU.mult).then_inc(s["kB_ok"], 1)
                    if later(t, 2):
                        done(dve, "o_ok", t - 2)
                    dve.tensor_tensor(gg[:, b], g[:, b], gain[:].unsqueeze(1).to_broadcast([P, NH, P]), ALU.mult).then_inc(s["gg_ok"], 1)

                def back(t, b):
                    if later(t, 2):
                        done(dve, "o_ps", t - 2)
                    for i in range(LV):
                        if i or later(t):
                            done(dve, "lv_ok", t, i, LV)
                        done(dve, "lv_ps", t, i + 1, LV)
                        dve.copy_predicated(sT[:, b], masks[:, i].unsqueeze(1).to_broadcast([P, NH, P]), psA_of(t, b, i)[:]).then_inc(s["lv_ok"], 1)
                    done(dve, "upd_ps", t)
                    if later(t):
                        done(dve, "o_ps", t - 1)
                    for h in range(NH):
                        last = dve.scalar_tensor_tensor(state[:, b, h], state[:, 1 - b, h], eL[:, b, h:h + 1], psU[:, h],
                                                        ALU.mult, ALU.add)
                    last.then_inc(s["state_ok"], 1)
                    done(dve, "osq_ok", t)
                    if later(t):
                        done(dve, "oln_ok", t - 1)
                    dve.tensor_reduce(oss[:], osq[:], AX.X, ALU.add).then_inc(s["oss_ok"], 1)
                    done(dve, "ors_ok", t)
                    dve.tensor_tensor(on[:], psO[b][:], ors[:].unsqueeze(2).to_broadcast([P, NH, P]), ALU.mult).then_inc(s["on_ok"], 1)
                    done(dve, "on_ok", t)
                    if later(t, 2):
                        dve.wait_ge(stored[b], (t - b) * 8)
                    dve.tensor_tensor(o[:, b], on[:], gg[:, b], ALU.mult).then_inc(s["o_ok"], 1)

                staggered(dve, front, back)

            @block.tensor
            def _(pe):
                pe.wait_ge(consts_in, 80)
                pe.wait_ge(init, 5)

                def tile(t, b):
                    done(pe, "kD_ok", t)
                    done(pe, "kDc_ok", t)
                    if later(t):
                        done(pe, "kDT_ok", t - 1)
                    for h in range(NH):
                        last = pe.transpose(psK[:, h], kD[:, b, h], ident[:])
                    last.then_inc(s["kDT_ps"], 1)
                    for i in range(LV):
                        if i == 0:
                            done(pe, "k0_ok", t)
                        elif i < LV - 1:
                            done(pe, "qH_ok", t, i, len(HALVES))
                            done(pe, "kH_ok", t, i, len(HALVES))
                        else:
                            done(pe, "kB_ok", t)
                        if i >= NA:
                            done(pe, "lv_ok", t, i - NA + 1, LV)
                        elif later(t):
                            done(pe, "lv_ok", t - 1, LV, LV)
                        for h in range(NH):
                            last = pe.matmul(psA_of(t, b, i)[:, h], kl[:, b, i, h], ql[:, b, i, h], start=True, stop=True)
                        last.then_inc(s["lv_ps"], 1)
                    done(pe, "kDT_ok", t)
                    if later(t):
                        done(pe, "state_ok", t - 1)
                    for h in range(NH):
                        last = pe.matmul(psU[:, h], kDT[:, b, h], v[:, b, h], start=True, stop=True)
                    last.then_inc(s["upd_ps"], 1)
                    done(pe, "lv_ok", t, LV, LV)
                    done(pe, "qI_ok", t)
                    done(pe, "qIc_ok", t)
                    if later(t, 2):
                        done(pe, "on_ok", t - 2)
                    for h in range(NH):
                        pe.matmul(psO[b][:, h], qI[:, b, h], state[:, 1 - b, h], start=True, stop=False)
                        last = pe.matmul(psO[b][:, h], sT[:, b, h], v[:, b, h], start=False, stop=True)
                    last.then_inc(s["o_ps"], 1)

                tiles(pe, tile)


HD = 64
CK = 512
LAM_INIT = 0.8 - 0.6 * 1.0


def attention(nc, tok, q_norm, k_norm, lam_q1, lam_k1, lam_q2, lam_k2, subln, ident_in, causal_in, mix):
    units = [[min(CK, (i + 1) * P - j * CK) for j in range(i // 4 + 1)] for i in range(NT)]
    first = [sum(len(u) for u in units[:i]) for i in range(NT)]
    CH = sum(len(u) for u in units)
    NPREP = 2 * 2 * (S // CK)
    with ExitStack() as stack:
        at = Place(nc, stack, "att")
        ident = at.sb("ident", [P, P])
        ident_bf = at.sb("ident_bf", [P, P], BF16)
        causal_f = at.sb("causal_f", [P, P])
        causal = at.sb("causal", [P, P], BF16)
        gcol = at.sb("gcol", [P, 2])
        gain = at.sb("gain", [P, P])
        lam_in = at.sb("lam_in", [P, 4, HD])
        lam_pr = at.sb("lam_pr", [P, 2, HD])
        lam_s = at.sb("lam_s", [P, 4])
        lamvec = at.sb("lamvec", [P, 2])
        eps = at.sb("eps", [P, 1])
        qk = at.sb("qk", [P, 2, NT, P])
        v = at.sb("v", [P, NH, NT, P])
        ms = at.sb("ms", [P, 2, 2 * NT])
        lnm = at.sb("lnm", [P, 2, 2 * NT])
        rs = at.sb("rs", [P, 2, 2 * NT])
        dup = at.sb("dup", [P, 2, NT, 2, 2, HD])
        qs = at.sb("qs", [P, 2, S], F32R)
        khi = at.sb("khi", [P, 2, S], F32R)
        klo = at.sb("klo", [P, 2, S], F32R)
        pr0 = at.sb("pr0", [P, 3, S])
        pr1 = at.sb("pr1", [P, 2, S])
        wT = at.sb("wT", [P, 2, 4, P])
        nm = at.sb("nm", [P, 2, 2, 4])
        sums = at.sb("sums", [P, 2, 2, 4])
        low = at.sb("low", [P, 2])
        dlt = at.sb("dlt", [P, 2, 4])
        ex = at.sb("ex", [P, 2, 4])
        exs = at.sb("exs", [P, 2, 4])
        tot = at.sb("tot", [P, 2])
        inv = at.sb("inv", [P, 2])
        invl = at.sb("invl", [P, 2])
        coef = at.sb("coef", [P, 2, 2, 4])
        o = at.sb("o", [P, NT, P])
        osq = at.sb("osq", [P, 4, P])
        oss = at.sb("oss", [P, 4])
        oln = at.sb("oln", [P, 4])
        ors = at.sb("ors", [P, 4])
        psS = [at.ps(f"psS{i}", (P, 2, CK)) for i in range(2)]
        psW = [at.ps(f"psW{i}") for i in range(2)]
        psO = [at.ps(f"psO{i}") for i in range(2)]

        consts_in = at.sem("consts_in")
        eps_set = at.sem("eps_set")
        mask_ok = at.sem("mask_ok")
        lam_ok = at.sem("lam_ok")
        qk_in = at.sem("qk_in")
        v_in = at.sem("v_in")
        sq_ok = at.sem("sq_ok")
        ms_ok = at.sem("ms_ok")
        lnm_ok = at.sem("lnm_ok")
        rs_ok = at.sem("rs_ok")
        dup_ok = [at.sem("dupq_ok"), at.sem("dupk_ok")]
        prep_ps = at.sem("prep_ps")
        prep_hi = at.sem("prep_hi")
        prep_lo = at.sem("prep_lo")
        score_ps = at.sem("score_ps")
        max_ok = at.sem("max_ok")
        exp_ok = at.sem("exp_ok")
        dl_ok = at.sem("dl_ok")
        ex_ok = at.sem("ex_ok")
        steps = at.sem("steps")
        stat_ok = at.sem("stat_ok")
        scaled = at.sem("scaled")
        comb_ok = at.sem("comb_ok")
        wT_ps = at.sem("wT_ps")
        wT_ok = at.sem("wT_ok")
        pv_ok = at.sem("pv_ok")
        o_ok = at.sem("o_ok")
        osq_ok = at.sem("osq_ok")
        oss_ok = at.sem("oss_ok")
        oln_ok = at.sem("oln_ok")
        ors_ok = at.sem("ors_ok")
        onorm = at.sem("onorm")
        gain_ok = at.sem("gain_ok")
        stored = [at.sem(f"stored{i}") for i in range(NT // 4)]
        STEPS = sum(1 if len(u) == 1 else 5 for u in units)
        HALF = NT // 2

        def later(h, n=1):
            return not isinstance(h, int) or h >= n

        def head_cols(part, h):
            c0 = (2 + part) * HW
            return tok[:, bass.ds(h * P + c0, P)].rearrange("(t p) c -> p t c", p=P)

        def chunks(i):
            return len(units[i]) if 0 <= i < NT else 0

        def upto(i, j):
            return first[i] + min(j + 1, len(units[i]))

        def prep_banks(i, j):
            return [((i - NT) * 4 + j) * 2 + k for k in range(2)] if i >= NT else []

        def prep_cut(n):
            return n // (NPREP // 2), n // (NPREP // 4) % 2, n % (S // CK)

        def prep_ps_bank(n):
            return psS[n // 2 % 2][:, n % 2, :]

        with nc.Block() as block:
            @block.sync
            def _(sp):
                for dst, src in ((ident, ident_in), (causal_f, causal_in)):
                    sp.dma_start(dst[:], src).then_inc(consts_in, 16)
                for i, g in enumerate((q_norm, k_norm)):
                    for c in range(2):
                        sp.dma_start(gcol[c * HD:(c + 1) * HD, i:i + 1], g.rearrange("a d -> d a"),
                                     allow_slow_non_contiguous=True).then_inc(consts_in, 16)
                for i, l in enumerate((lam_q1, lam_q2, lam_k1, lam_k2)):
                    sp.dma_start(lam_in[:, i, :], l.broadcast_to([P, HD])).then_inc(consts_in, 16)
                sp.dma_start(gain[:], subln.broadcast_to([P, P])).then_inc(consts_in, 16)

                def load(h):
                    if later(h):
                        sp.wait_ge(dup_ok[0], h * 2)
                        sp.wait_ge(dup_ok[1], h * 2)
                    for i in range(2):
                        sp.dma_start(qk[:, i], head_cols(i, h)).then_inc(qk_in, 16)

                def store(h, q):
                    at.hold(sp, onorm, (h * (NT // 4) + q + 1) * 2)
                    sp.dma_start(mix[q * 4 * P:(q + 1) * 4 * P, bass.ds(h * P + HW, P)].rearrange("(t p) c -> p t c", p=P),
                                 o[:, q * 4:q * 4 + 4, :]).then_inc(stored[q], 16)

                load(0)
                for h in range(NH):
                    sp.dma_start(v[:, h], head_cols(2, h)).then_inc(v_in, 16)
                load(1)

                def head(h, last):
                    if later(h):
                        store(h - 1, NT // 4 - 1)
                    store(h, 0)
                    if not last:
                        load(h + 2)
                    for q in range(1, NT // 4 - 1):
                        store(h, q)

                head(0, False)
                with sp.Fori(1, NH - 2) as h:
                    head(h, False)
                for h in range(NH - 2, NH):
                    head(h, True)
                store(NH - 1, NT // 4 - 1)
                for q in range(NT // 4):
                    sp.wait_ge(stored[q], 16 * NH)

            @block.gpsimd
            def _(pool):
                def normalise_q(h, half):
                    cut = slice(half * HALF, (half + 1) * HALF)
                    pool.wait_ge(qk_in, (h + 1) * 32)
                    pool.wait_ge(rs_ok, h + 1)
                    pool.tensor_tensor(dup[:, 0, cut].rearrange("p t c u d -> p (t c) u d"),
                                       qk[:, 0, cut].rearrange("p t (c d) -> p (t c) d", c=2).unsqueeze(2).to_broadcast([P, NT, 2, HD]),
                                       rs[:, 0, half * NT:(half + 1) * NT].unsqueeze(2).unsqueeze(3).to_broadcast([P, NT, 2, HD]),
                                       ALU.mult).then_inc(dup_ok[0], 1)

                def head(h, last):
                    for i in range(NT):
                        at.hold(pool, stat_ok, h * NT + i + 1)
                        for j, w in enumerate(units[i]):
                            cut = slice(j * CK, j * CK + w)
                            pool.tensor_scalar(pr1[:, i % 2, cut], pr1[:, i % 2, cut], coef[:, i % 2, 1, j:j + 1], None,
                                               ALU.mult).then_inc(scaled, 1)
                        if not last and i in (8, 9):
                            normalise_q(h + 1, i - 8)

                normalise_q(0, 0)
                normalise_q(0, 1)
                head(0, False)
                with pool.Fori(1, NH - 1) as h:
                    head(h, False)
                head(NH - 1, True)

            @block.scalar
            def _(act):
                act.preload_act_table_set("natural_log_exp_and_others")
                act.wait_ge(eps_set, 1)
                act.wait_ge(lam_ok, 2)
                act.activation(lam_s[:, 2:4], lam_s[:, 0:2], ACT.Exp).then_inc(lam_ok, 1)

                def squares(h, n):
                    i, half = n // 2, n % 2
                    act.wait_ge(qk_in, (h + 1) * 32)
                    if later(h) and n == 0:
                        act.wait_ge(prep_ps, h * NPREP)
                    act.activation(dup[:, i, half * HALF:(half + 1) * HALF, 0].rearrange("p t u d -> p t (u d)"),
                                   qk[:, i, half * HALF:(half + 1) * HALF, :], ACT.Square).then_inc(sq_ok, 1)

                def rstd(h):
                    act.wait_ge(ms_ok, h * 4 + 4)
                    act.activation(lnm[:], ms[:], ACT.Ln, bias=eps[:], scale=1.0 / HD).then_inc(lnm_ok, 1)
                    act.wait_ge(lnm_ok, h + 1)
                    act.activation(rs[:], lnm[:], ACT.Exp, scale=-0.5).then_inc(rs_ok, 1)

                def prep_high(h, n):
                    i, c, a = prep_cut(n)
                    act.wait_ge(prep_ps, h * NPREP + n + 1)
                    act.activation((qs, khi)[i][:, c, a * CK:(a + 1) * CK], prep_ps_bank(n), ACT.Copy,
                                   scale=gcol[:, i:i + 1]).then_inc(prep_hi, 1)

                def exponentials(h, i, j):
                    n, w = first[i] + j, units[i][j]
                    act.wait_ge(max_ok, h * CH + n + 1)
                    if i >= 3 or later(h):
                        act.wait_ge(wT_ps, h * CH + (upto(i - 3, j) if i >= 3 else 0))
                    if i >= 2 or later(h):
                        act.wait_ge(comb_ok, h * CH + (upto(i - 2, j) if i >= 2 else 0))
                    for c, dst in enumerate((pr0[:, i % 3], pr1[:, i % 2])):
                        act.activation(dst[:, j * CK:j * CK + w], psS[n % 2][:, c, 0:w], ACT.Exp,
                                       bias=nm[:, i % 2, c, j:j + 1],
                                       accum_out=sums[:, i % 2, c, j:j + 1]).then_inc(exp_ok, 1)

                def take_weights(h, i, j):
                    n, w = first[i] + j, units[i][j]
                    act.wait_ge(wT_ps, h * CH + n + 1)
                    if n >= 2 or later(h):
                        act.wait_ge(pv_ok, h * CH + n - 1)
                    act.activation(wT[:, n % 2, 0:w // P, :], psW[n % 2][:, 0:w].rearrange("p (k q) -> p k q", q=P),
                                   ACT.Copy).then_inc(wT_ok, 1)

                def head(h, last):
                    for i in range(NT + 2):
                        if i >= 1 and chunks(i - 1) > 1:
                            nj = chunks(i - 1)
                            act.wait_ge(dl_ok, h * (NT - 4) + i - 4)
                            act.activation(ex[:, :, 0:nj], dlt[:, :, 0:nj], ACT.Exp).then_inc(ex_ok, 1)
                        for j in range(4):
                            if j < chunks(i):
                                exponentials(h, i, j)
                            for n in prep_banks(i, j) if not last else []:
                                prep_high(h + 1, n)
                            if j < chunks(i - 2):
                                take_weights(h, i - 2, j)
                        if i >= 2:
                            act.wait_ge(pv_ok, h * CH + upto(i - 2, 4))
                            if (i - 2) % 4 == 0 and later(h):
                                act.wait_ge(stored[(i - 2) // 4], h * 16)
                            act.activation(o[:, i - 2, :], psO[i % 2][:, 0:P], ACT.Copy).then_inc(o_ok, 1)
                        if not last:
                            if 3 <= i < 7:
                                squares(h + 1, i - 3)
                            if i == 8:
                                rstd(h + 1)
                        if i % 4 == 2 and i < NT and (i >= 6 or later(h)):
                            out_squares(h, (i - 6) // 4)
                        if i % 4 == 0 and i >= 4 and (i >= 8 or later(h)):
                            out_rstd(h, (i - 8) // 4)

                def out_squares(h, q):
                    m, u = h * (NT // 4) + q, q % (NT // 4) * 4
                    act.wait_ge(o_ok, m * 4 + 4)
                    if later(m):
                        act.wait_ge(oss_ok, m)
                    act.activation(osq[:], o[:, u:u + 4, :], ACT.Square).then_inc(osq_ok, 1)

                def out_rstd(h, q):
                    m = h * (NT // 4) + q
                    act.wait_ge(oss_ok, m + 1)
                    act.activation(oln[:], oss[:], ACT.Ln, bias=eps[:], scale=1.0 / P).then_inc(oln_ok, 1)
                    act.wait_ge(oln_ok, m + 1)
                    if later(m):
                        act.wait_ge(onorm, m * 2)
                    act.activation(ors[:], oln[:], ACT.Exp, scale=-0.5).then_inc(ors_ok, 1)

                for n in range(4):
                    squares(0, n)
                rstd(0)
                for n in range(NPREP):
                    prep_high(0, n)
                head(0, False)
                with act.Fori(1, NH - 1) as h:
                    head(h, False)
                head(NH - 1, True)
                out_squares(NH, -1)
                out_rstd(NH, -1)

            @block.vector
            def _(dve):
                dve.memset(eps[:], EPS).then_inc(eps_set, 1)
                dve.wait_ge(consts_in, 16 * 11)
                dve.tensor_copy(ident_bf[:], ident[:]).then_inc(mask_ok, 1)
                dve.tensor_copy(causal[:], causal_f[:]).then_inc(mask_ok, 1)
                dve.tensor_scalar(gcol[:, 0:1], gcol[:, 0:1], HD ** -0.5, None, ALU.mult).then_inc(gain_ok, 1)
                dve.tensor_scalar(gain[:], gain[:], 1.0 - LAM_INIT, None, ALU.mult).then_inc(gain_ok, 1)
                dve.tensor_tensor(lam_pr[:], lam_in[:, 0:2], lam_in[:, 2:4], ALU.mult).then_inc(lam_ok, 1)
                dve.wait_ge(lam_ok, 1)
                dve.tensor_reduce(lam_s[:, 0:2], lam_pr[:], AX.X, ALU.add).then_inc(lam_ok, 1)
                dve.memset(lamvec[:, 0:1], 1.0).then_inc(gain_ok, 1)
                dve.wait_ge(lam_ok, 3)
                dve.scalar_tensor_tensor(lamvec[:, 1:2], lam_s[:, 3:4], LAM_INIT, lam_s[:, 2:3],
                                         ALU.subtract, ALU.subtract).then_inc(gain_ok, 1)
                dve.wait_ge(gain_ok, 4)

                def means(h, n):
                    i, half = n // 2, n % 2
                    dve.wait_ge(sq_ok, h * 4 + n + 1)
                    src = dup[:, i, half * HALF:(half + 1) * HALF, 0].rearrange("p t u d -> p t u d")
                    dve.tensor_reduce(ms[:, i, half * NT:(half + 1) * NT].rearrange("p (t c) -> p t c", c=2), src,
                                      AX.X, ALU.add).then_inc(ms_ok, 1)

                def normalise_k(h, half):
                    cut = slice(half * HALF, (half + 1) * HALF)
                    dve.wait_ge(qk_in, (h + 1) * 32)
                    dve.wait_ge(rs_ok, h + 1)
                    dve.tensor_tensor(dup[:, 1, cut].rearrange("p t c u d -> p (t c) u d"),
                                      qk[:, 1, cut].rearrange("p t (c d) -> p (t c) d", c=2).unsqueeze(2).to_broadcast([P, NT, 2, HD]),
                                      rs[:, 1, half * NT:(half + 1) * NT].unsqueeze(2).unsqueeze(3).to_broadcast([P, NT, 2, HD]),
                                      ALU.mult).then_inc(dup_ok[1], 1)

                def prep_low(h, n):
                    i, c, a = prep_cut(n)
                    dve.wait_ge(prep_hi, h * NPREP + n + 1)
                    cut = slice(a * CK, (a + 1) * CK)
                    lo, hi, r = ((qs, qs), (klo, khi))[i] + (slice(HD, P) if i == 0 else slice(0, P),)
                    dve.scalar_tensor_tensor(lo[r, c, cut], prep_ps_bank(n)[r, :], gcol[r, i:i + 1], hi[r, c, cut].bitcast(F32),
                                             ALU.mult, ALU.subtract).then_inc(prep_lo, 1)

                def maxima(h, i, j):
                    n, w = first[i] + j, units[i][j]
                    dve.wait_ge(score_ps, h * CH + n + 1)
                    dve.tensor_reduce(nm[:, i % 2, :, j:j + 1], psS[n % 2][:, :, 0:w], AX.X, ALU.max,
                                      negate=True).then_inc(max_ok, 1)

                def differences(h, i):
                    nj = chunks(i)
                    dve.wait_ge(max_ok, h * CH + first[i] + nj)
                    own(h, dve.tensor_reduce(low[:], nm[:, i % 2, :, 0:nj], AX.X, ALU.min))
                    dve.tensor_tensor(dlt[:, :, 0:nj], low[:].unsqueeze(2).to_broadcast([P, 2, nj]), nm[:, i % 2, :, 0:nj],
                                      ALU.subtract).then_inc(dl_ok, 1)

                def coefficients(h, i):
                    nj, u = chunks(i), i % 2
                    if nj > 1:
                        dve.wait_ge(ex_ok, h * (NT - 4) + i - 3)
                        dve.wait_ge(exp_ok, (h * CH + upto(i, 4)) * 2)
                        own(h, dve.tensor_tensor(exs[:, :, 0:nj], ex[:, :, 0:nj], sums[:, u, :, 0:nj], ALU.mult))
                        own(h, dve.tensor_reduce(tot[:], exs[:, :, 0:nj], AX.X, ALU.add))
                        own(h, dve.reciprocal(inv[:], tot[:]))
                        own(h, dve.tensor_tensor(invl[:], inv[:], lamvec[:], ALU.mult))
                        dve.tensor_tensor(coef[:, u, :, 0:nj], ex[:, :, 0:nj],
                                          invl[:].unsqueeze(2).to_broadcast([P, 2, nj]), ALU.mult).then_inc(stat_ok, 1)
                    else:
                        dve.wait_ge(exp_ok, (h * CH + upto(i, 4)) * 2)
                        own(h, dve.reciprocal(inv[:], sums[:, u, :, 0]))
                        dve.tensor_tensor(coef[:, u, :, 0], inv[:], lamvec[:], ALU.mult).then_inc(stat_ok, 1)

                def combine(h, i, j):
                    w = units[i][j]
                    cut = slice(j * CK, j * CK + w)
                    dve.wait_ge(stat_ok, h * NT + i + 1)
                    dve.wait_ge(scaled, h * CH + first[i] + j + 1)
                    dve.scalar_tensor_tensor(pr0[:, i % 3, cut], pr0[:, i % 3, cut], coef[:, i % 2, 0, j:j + 1], pr1[:, i % 2, cut],
                                             ALU.mult, ALU.add).then_inc(comb_ok, 1)

                def out_sums(h, q):
                    m = h * (NT // 4) + q
                    dve.wait_ge(osq_ok, m + 1)
                    if later(m):
                        dve.wait_ge(oln_ok, m)
                    dve.tensor_reduce(oss[:], osq[:], AX.X, ALU.add).then_inc(oss_ok, 1)

                def out_norm(h, q):
                    m, u = h * (NT // 4) + q, q % (NT // 4) * 4
                    dve.wait_ge(ors_ok, m + 1)
                    dve.tensor_tensor(o[:, u:u + 4, :], o[:, u:u + 4, :], ors[:].unsqueeze(2).to_broadcast([P, 4, P]),
                                      ALU.mult).then_inc(onorm, 1)
                    dve.wait_ge(onorm, m * 2 + 1)
                    dve.tensor_tensor(o[:, u:u + 4, :], o[:, u:u + 4, :], gain[:].unsqueeze(1).to_broadcast([P, 4, P]),
                                      ALU.mult).then_inc(onorm, 1)

                step = [0]

                def own(h, ins):
                    step[0] += 1
                    ins.then_inc(steps, 1)
                    dve.wait_ge(steps, h * STEPS + step[0])

                def head(h, last):
                    step[0] = 0
                    for i in range(NT + 2):
                        if i < NT:
                            maxima(h, i, 0)
                        if 1 <= i <= NT:
                            coefficients(h, i - 1)
                        for j in range(4):
                            if j + 1 < chunks(i):
                                maxima(h, i, j + 1)
                            for n in prep_banks(i, j) if not last else []:
                                prep_low(h + 1, n)
                            if j < chunks(i - 1):
                                combine(h, i - 1, j)
                        if chunks(i) > 1:
                            differences(h, i)
                        if not last:
                            if 4 <= i < 8:
                                means(h + 1, i - 4)
                            if i in (9, 11):
                                normalise_k(h + 1, (i - 9) // 2)
                        if i % 4 == 3 and i < NT and (i >= 7 or later(h)):
                            out_sums(h, (i - 7) // 4)
                        if i % 4 == 1 and i >= 5 and (i >= 9 or later(h)):
                            out_norm(h, (i - 9) // 4)

                for n in range(4):
                    means(0, n)
                normalise_k(0, 0)
                normalise_k(0, 1)
                for n in range(NPREP):
                    prep_low(0, n)
                head(0, False)
                with dve.Fori(1, NH - 1) as h:
                    head(h, False)
                head(NH - 1, True)
                out_sums(NH, -1)
                out_norm(NH, -1)

            @block.tensor
            def _(pe):
                pe.wait_ge(consts_in, 16 * 11)
                pe.wait_ge(mask_ok, 2)

                def prepare(h, n):
                    i, c, a = prep_cut(n)
                    if n % (NPREP // 2) == 0:
                        pe.wait_ge(dup_ok[i], (h + 1) * 2)
                    if n >= 4:
                        pe.wait_ge(prep_lo, h * NPREP + n - 3)
                    elif later(h):
                        pe.wait_ge(exp_ok, h * CH * 2)
                    for k in range(4):
                        last = pe.transpose(prep_ps_bank(n)[:, k * P:(k + 1) * P],
                                            dup[:, i, a * 4 + k, c].rearrange("p u d -> p (u d)"), ident[:])
                    last.then_inc(prep_ps, 1)

                def scores(h, i, j):
                    n, w = first[i] + j, units[i][j]
                    if i == 0:
                        pe.wait_ge(prep_lo, (h + 1) * NPREP)
                    if n >= 2:
                        pe.wait_ge(exp_ok, (h * CH + n - 1) * 2)
                    diag = j == len(units[i]) - 1
                    for c in range(2):
                        out = psS[n % 2][:, c, 0:w]
                        q = qs[:, c, i * P:(i + 1) * P]
                        pe.matmul(out, q, khi[:, c, j * CK:j * CK + w], start=True, stop=False)
                        last = pe.matmul(out, q, klo[:, c, j * CK:j * CK + w], start=False, stop=not diag)
                        if diag:
                            last = pe.matmul(psS[n % 2][:, c, w - P:w], ident_bf[:], causal[:], start=False, stop=True)
                    last.then_inc(score_ps, 1)

                def turn_weights(h, i, j):
                    n, w = first[i] + j, units[i][j]
                    pe.wait_ge(comb_ok, h * CH + n + 1)
                    if n >= 2 or later(h):
                        pe.wait_ge(wT_ok, h * CH + n - 1)
                    for k in range(w // P):
                        last = pe.transpose(psW[n % 2][:, k * P:(k + 1) * P],
                                            pr0[:, i % 3, j * CK + k * P:j * CK + (k + 1) * P], ident[:])
                    last.then_inc(wT_ps, 1)

                def times_values(h, i, j):
                    n = first[i] + j
                    pe.wait_ge(wT_ok, h * CH + n + 1)
                    if j == 0 and (i >= 2 or later(h)):
                        pe.wait_ge(o_ok, h * NT + i - 1)
                    for k in range(units[i][j] // P):
                        t = j * 4 + k
                        last = pe.matmul(psO[i % 2][:, 0:P], wT[:, n % 2, k, :], v[:, bass.ds(h, 1), t, :].rearrange("p a c -> p (a c)"),
                                         start=(t == 0), stop=(t == i))
                    last.then_inc(pv_ok, 1)

                def head(h, last):
                    for i in range(NT + 2):
                        for j in range(4):
                            if j < chunks(i):
                                scores(h, i, j)
                            for n in prep_banks(i, j) if not last else []:
                                prepare(h + 1, n)
                            if j < chunks(i - 2):
                                turn_weights(h, i - 2, j)
                            if 1 <= j and j - 1 < chunks(i - 2):
                                times_values(h, i - 2, j - 1)
                        if chunks(i - 2) == 4:
                            times_values(h, i - 2, 3)

                for n in range(NPREP):
                    prepare(0, n)
                pe.wait_ge(v_in, 16 * NH)
                head(0, False)
                with pe.Fori(1, NH - 1) as h:
                    head(h, False)
                head(NH - 1, True)


NE = 16
NGR = 4
GE = NE // NGR
HALF = D // 2


def project_out(nc, mix, x, w_out, ffn_norm, w_router, ident_in, h1, xn_rows, logits):
    NS = 4
    with ExitStack() as stack:
        at = Place(nc, stack, "out")
        ident = at.sb("ident", [P, P])
        gain = at.sb("gain", [P, D])
        eps = at.sb("eps", [P, 1])
        wraw = at.sb("wraw", [P, NS, D])
        whi = at.sb("whi", [P, KD, D], F32R)
        wlo = at.sb("wlo", [P, KD, D], F32R)
        wr = at.sb("wr", [P, KD, NE])
        m = at.sb("m", [P, NS, D])
        h = at.sb("h", [P, NS, D])
        mhi = at.sb("mhi", [P, 2, KD, P], F32R)
        mlo = at.sb("mlo", [P, 2, KD, P], F32R)
        sq = at.sb("sq", [P, D])
        ss, lnm, rs = (at.sb(n, [P, 2]) for n in ("ss", "lnm", "rs"))
        xn = at.sb("xn", [P, NS, D])
        xT = at.sb("xT", [P, KD, P])
        lg = at.sb("lg", [P, NT, NE])
        zero = at.sb("zero", [1, D])
        psT = [at.ps(f"psT{i}", (P, 4, P)) for i in range(2)]
        psM = at.ps("psM", (P, 2, HALF))
        psR = [at.ps(f"psR{i}", (P, 4, P)) for i in range(2)]
        psL = at.ps("psL")

        consts_in, gain_in, zero_ok, zero_out, eps_set = (at.sem(n) for n in ("consts_in", "gain_in", "zero_ok", "zero_out", "eps_set"))
        w_in = [at.sem(f"w_in{i}") for i in range(NS)]
        whi_ok, wlo_ok = at.sem("whi_ok"), at.sem("wlo_ok")
        m_in, x_in, h_out, n_out = ([at.sem(f"{n}{i}") for i in range(NS)] for n in ("m_in", "x_in", "h_out", "n_out"))
        mT_ps = at.sem("mT_ps")
        mhi_ok, mlo_ok = at.sem("mhi_ok"), at.sem("mlo_ok")
        mm_ok = at.sem("mm_ok")
        h_ok = at.sem("h_ok")
        sq_ok, lnm_ok, rs_ok = at.sem("sq_ok"), at.sem("lnm_ok"), at.sem("rs_ok")
        xn_ok = at.sem("xn_ok")
        xT_ps = at.sem("xT_ps")
        xT_ok = at.sem("xT_ok")
        lg_ps = at.sem("lg_ps")
        lg_ok = at.sem("lg_ok")
        lg_out = at.sem("lg_out")

        def later(t, n=1):
            return not isinstance(t, int) or t >= n

        def inside(t):
            return not isinstance(t, int) or t < NT

        def used(t, u):
            return (t - u % NS + NS) * (16 // NS)

        def steps(eng, body):
            for u in range(4):
                body(u, u)
            with eng.Fori(1, NT // 4 - 1) as g:
                for u in range(4):
                    body(g * 4 + u, u)
            for u in range(4):
                body(NT - 4 + u, u)

        with nc.Block() as block:
            @block.sync
            def _(sp):
                sp.dma_start(ident[:], ident_in).then_inc(consts_in, 16)

                def load(t, u):
                    v = u % NS
                    if later(t, NS):
                        at.hold(sp, mT_ps, (t - NS + 1) * 2)
                    sp.dma_start(m[:, v], mix[bass.ds(t * P, P), :]).then_inc(m_in[v], 16)
                    if later(t, NS):
                        at.hold(sp, h_out[v], used(t - NS, v))
                        at.hold(sp, xn_ok, t - NS + 1)
                    sp.dma_start(h[:, v], x[bass.ds(t * P, P), :]).then_inc(x_in[v], 16)

                load(0, 0)
                for k in range(KD):
                    if k >= NS:
                        sp.wait_ge(whi_ok, k - NS + 1)
                        sp.wait_ge(wlo_ok, k - NS + 1)
                    sp.dma_start(wraw[:, k % NS], w_out[k * P:(k + 1) * P, :]).then_inc(w_in[k % NS], 16)
                    if k == 3:
                        load(1, 1)
                sp.dma_start(gain[:], ffn_norm.broadcast_to([P, D])).then_inc(gain_in, 16)
                sp.dma_start(wr[:], w_router.rearrange("(k p) e -> p k e", p=P)).then_inc(gain_in, 16)
                load(2, 2)

                def step(t, u):
                    v = u % NS
                    if inside(t + 3):
                        load(t + 3, u + 3)
                    at.hold(sp, h_ok, t + 1)
                    sp.dma_start(h1[bass.ds(t * P, P), :], h[:, v]).then_inc(h_out[v], 16)
                    at.hold(sp, xn_ok, t + 1)
                    sp.dma_start(xn_rows[bass.ds(t * P, P), :], xn[:, v]).then_inc(n_out[v], 16)

                steps(sp, step)
                sp.wait_ge(lg_ok, NT)
                sp.dma_start(logits, lg[:].rearrange("p t e -> p (t e)")).then_inc(lg_out, 16)
                sp.wait_ge(lg_out, 16)
                for v in range(NS):
                    sp.wait_ge(h_out[v], NT // NS * 16)
                    sp.wait_ge(n_out[v], NT // NS * 16)

            @block.gpsimd
            def _(pool):
                pool.memset(zero[:], 0.0).then_inc(zero_ok, 1)
                pool.wait_ge(zero_ok, 1)
                pool.dma_start(xn_rows[S:S + 1, :], zero[:]).then_inc(zero_out, 16)
                pool.wait_ge(zero_out, 16)

            @block.scalar
            def _(act):
                act.preload_act_table_set("natural_log_exp_and_others")

                def split_w(k):
                    act.wait_ge(w_in[k % NS], 16 * (k // NS + 1))
                    act.activation(whi[:, k], wraw[:, k % NS], ACT.Copy).then_inc(whi_ok, 1)

                def front(t, u):
                    b = u % 2
                    if later(t, 2):
                        act.wait_ge(mm_ok, t - 1)
                    for i in range(2):
                        act.wait_ge(mT_ps, t * 2 + i + 1)
                        act.activation(mhi[:, b, i * 4:(i + 1) * 4], psT[i][:], ACT.Copy).then_inc(mhi_ok, 1)

                def take_xT(t):
                    if later(t):
                        act.wait_ge(lg_ps, t)
                    for i in range(2):
                        act.wait_ge(xT_ps, t * 2 + i + 1)
                        act.activation(xT[:, i * 4:(i + 1) * 4], psR[i][:], ACT.Copy).then_inc(xT_ok, 1)

                def step(t, u):
                    b, v = u % 2, u % NS
                    if inside(t + 1):
                        front(t + 1, u + 1)
                    if later(t):
                        take_xT(t - 1)
                    act.wait_ge(h_ok, t + 1)
                    if later(t):
                        act.wait_ge(sq_ok, t)
                    if later(t, 2):
                        act.wait_ge(xn_ok, t - 1)
                    act.activation(sq[:], h[:, v], ACT.Square, accum_out=ss[:, b:b + 1]).then_inc(sq_ok, 1)
                    act.wait_ge(sq_ok, t + 1)
                    act.activation(lnm[:, b:b + 1], ss[:, b:b + 1], ACT.Ln, bias=eps[:], scale=1.0 / D).then_inc(lnm_ok, 1)
                    act.wait_ge(lnm_ok, t + 1)
                    act.activation(rs[:, b:b + 1], lnm[:, b:b + 1], ACT.Exp, scale=-0.5).then_inc(rs_ok, 1)

                act.wait_ge(eps_set, 1)
                front(0, 0)
                for k in range(KD):
                    split_w(k)
                steps(act, step)
                take_xT(NT - 1)

            @block.vector
            def _(dve):
                dve.memset(eps[:], EPS).then_inc(eps_set, 1)

                def split_w(k):
                    dve.wait_ge(whi_ok, k + 1)
                    dve.tensor_tensor(wlo[:, k], wraw[:, k % NS], whi[:, k].bitcast(F32), ALU.subtract).then_inc(wlo_ok, 1)

                def front(t, u):
                    b = u % 2
                    for i in range(2):
                        dve.wait_ge(mhi_ok, t * 2 + i + 1)
                        dve.tensor_tensor(mlo[:, b, i * 4:(i + 1) * 4], psT[i][:], mhi[:, b, i * 4:(i + 1) * 4].bitcast(F32),
                                          ALU.subtract).then_inc(mlo_ok, 1)

                def take_logits(t):
                    dve.wait_ge(lg_ps, t + 1)
                    dve.tensor_copy(lg[:, bass.ds(t, 1), :], psL[:, 0:NE].unsqueeze(1)).then_inc(lg_ok, 1)

                def step(t, u):
                    b, v = u % 2, u % NS
                    if inside(t + 1):
                        front(t + 1, u + 1)
                    dve.wait_ge(mm_ok, t + 1)
                    dve.wait_ge(x_in[v], used(t, u))
                    dve.tensor_tensor(h[:, v], psM[:].rearrange("p a n -> p (a n)"), h[:, v], ALU.add).then_inc(h_ok, 1)
                    if later(t):
                        take_logits(t - 1)
                    dve.wait_ge(rs_ok, t + 1)
                    if later(t, NS):
                        dve.wait_ge(n_out[v], used(t - NS, v))
                    dve.scalar_tensor_tensor(xn[:, v], h[:, v], rs[:, b:b + 1], gain[:], ALU.mult, ALU.mult).then_inc(xn_ok, 1)

                front(0, 0)
                for k in range(KD):
                    split_w(k)
                dve.wait_ge(gain_in, 32)
                steps(dve, step)
                take_logits(NT - 1)

            @block.tensor
            def _(pe):
                pe.wait_ge(consts_in, 16)

                def front(t, u):
                    pe.wait_ge(m_in[u % NS], used(t, u))
                    for i in range(2):
                        if later(t):
                            pe.wait_ge(mlo_ok, t * 2 - 1 + i)
                        for j in range(4):
                            last = pe.transpose(psT[i][:, j], m[:, u % NS, (i * 4 + j) * P:(i * 4 + j + 1) * P], ident[:])
                        last.then_inc(mT_ps, 1)

                def product(t, u, n, k):
                    b, cut = u % 2, slice(n * HALF, (n + 1) * HALF)
                    for i, (l, r) in enumerate(((mhi, whi), (mhi, wlo), (mlo, whi))):
                        last = pe.matmul(psM[:, n], l[:, b, k], r[:, k, cut], start=(k == 0 and i == 0), stop=(k == KD - 1 and i == 2))
                    return last

                def turn_xn(t, u):
                    pe.wait_ge(xn_ok, t + 1)
                    if not later(t):
                        pe.wait_ge(gain_in, 32)
                    else:
                        pe.wait_ge(xT_ok, t * 2)
                    for i in range(2):
                        for j in range(4):
                            last = pe.transpose(psR[i][:, j], xn[:, u % NS, (i * 4 + j) * P:(i * 4 + j + 1) * P], ident[:])
                        last.then_inc(xT_ps, 1)

                def router(t):
                    pe.wait_ge(xT_ok, t * 2 + 2)
                    if later(t):
                        pe.wait_ge(lg_ok, t)
                    for k in range(KD):
                        last = pe.matmul(psL[:, 0:NE], xT[:, k], wr[:, k], start=(k == 0), stop=(k == KD - 1))
                    last.then_inc(lg_ps, 1)

                def step(t, u):
                    if inside(t + 1):
                        front(t + 1, u + 1)
                    pe.wait_ge(mlo_ok, t * 2 + 2)
                    if later(t):
                        pe.wait_ge(h_ok, t)
                        for n in range(2):
                            for k in range(KD):
                                last = product(t, u, n, k)
                            if n == 0:
                                turn_xn(t - 1, u + 3)
                        last.then_inc(mm_ok, 1)
                        router(t - 1)
                    else:
                        for k in range(KD):
                            pe.wait_ge(wlo_ok, k + 1)
                            for n in range(2):
                                last = product(t, u, n, k)
                        last.then_inc(mm_ok, 1)

                front(0, 0)
                steps(pe, step)
                turn_xn(NT - 1, NT - 1)
                router(NT - 1)


NB = 2 * S // P + NE - 1
NROW = NB * P


def route(nc, logits, below_in, upper_in, firsts_in, blocks_in, tokens_in, row_tok, dest_out, wgt_out, plan_out):
    with ExitStack() as stack:
        at = Place(nc, stack, "route")
        NG2 = NT * NGR
        lg = at.sb("lg", [P, NT, NE])
        below = at.sb("below", [P, GE, GE])
        upper = at.sb("upper", [P, 2, P])
        firsts = at.sb("firsts", [P, NE, NT])
        blocks = at.sb("blocks", [P, NB])
        tokens = at.sb("tokens", [P, NT], I32)
        pad = at.sb("pad", [P, NB], I32)
        mx, sm, inv = (at.sb(n, [P, NT]) for n in ("mx", "sm", "inv"))
        aff, tmp, first, second, sel, pre, dst = (at.sb(n, [P, NT, NE]) for n in ("aff", "tmp", "first", "second", "sel", "pre", "dst"))
        cmp1, cmp2 = (at.sb(n, [P, NG2, GE, GE]) for n in ("cmp1", "cmp2"))
        rank = at.sb("rank", [P, NG2, GE])
        gs = at.sb("gs", [P, NT, NGR])
        grank, gtop = at.sb("grank", [P, NT, NGR]), at.sb("gtop", [P, NT, NGR])
        totT, incl, excl = (at.sb(n, [P, NE, NT]) for n in ("totT", "incl", "excl"))
        cnt_i, nb_i, ends_i = (at.sb(n, [P, NE], I32) for n in ("cnt_i", "nb_i", "ends_i"))
        cnt, nb, ends, starts, ones = (at.sb(n, [P, NE]) for n in ("cnt", "nb", "ends", "starts", "ones"))
        dest_f = at.sb("dest_f", [P, 2, NT])
        dest = at.sb("dest", [P, 2, NT], I32)
        wgt = at.sb("wgt", [P, 2, NT])
        over = at.sb("over", [P, NB, NE])
        be = at.sb("be", [P, NB])
        plan = at.sb("plan", [P, 2 * NB + NE], I32)
        ps = at.ps("ps")
        consts_in, lg_in, pad_out, out = (at.sem(n) for n in ("consts_in", "lg_in", "pad_out", "out"))
        step, exp_ok, tok_ok, count_ps, dest_ok, plan_ok, pad_ok = (at.sem(n) for n in ("step", "exp_ok", "tok_ok", "count_ps", "dest_ok", "plan_ok", "pad_ok"))
        scattered = at.sem("scattered")

        def over_last(x, n):
            return x.unsqueeze(len(x.shape)).to_broadcast([*x.shape, n])

        with nc.Block() as block:
            @block.sync
            def _(sp):
                sp.dma_start(lg[:].rearrange("p t e -> p (t e)"), logits).then_inc(lg_in, 16)
                for dst_, src in ((below, below_in), (upper, upper_in), (firsts, firsts_in), (blocks, blocks_in), (tokens, tokens_in)):
                    sp.dma_start(dst_[:], src).then_inc(consts_in, 16)
                sp.wait_ge(pad_ok, 1)
                sp.dma_start(row_tok.rearrange("(p b) o -> p (b o)", p=P), pad[:]).then_inc(pad_out, 16)
                sp.wait_ge(plan_ok, 1)
                sp.dma_start(dest_out, dest[:].rearrange("p a t -> p (a t)")).then_inc(out, 16)
                sp.dma_start(wgt_out, wgt[:].rearrange("p a t -> p (a t)")).then_inc(out, 16)
                sp.dma_start(plan_out, plan[:]).then_inc(out, 16)
                sp.wait_ge(out, 48)

            @block.scalar
            def _(act):
                act.wait_ge(exp_ok, 1)
                act.activation(aff[:], tmp[:], ACT.Exp).then_inc(exp_ok, 1)

            @block.tensor
            def _(pe):
                pe.wait_ge(consts_in, 80)
                pe.wait_ge(tok_ok, 1)
                for i in range(2):
                    last = pe.matmul(ps[:, i * 256:(i + 1) * 256], upper[:, i], sel[:].rearrange("p t e -> p (t e)"), start=True, stop=True)
                last.then_inc(count_ps, 1)

            @block.gpsimd
            def _(pool):
                pool.memset(pad[:], S).then_inc(pad_ok, 1)
                pool.wait_ge(dest_ok, 1)
                pool.wait_ge(pad_out, 16)
                pool.wait_ge(consts_in, 80)
                for t in range(NT):
                    for a in range(2):
                        pool.indirect_dma_start(row_tok, bass.IndirectOffsetOnAxis(ap=dest[:, a, t:t + 1], axis=0),
                                                tokens[:, t:t + 1], None).then_inc(scattered, 16)
                pool.wait_ge(scattered, 2 * NT * 16)

            @block.vector
            def _(dve):
                count = [0]

                def link(ins):
                    count[0] += 1
                    ins.then_inc(step, 1)
                    dve.wait_ge(step, count[0])

                dve.wait_ge(lg_in, 16)
                dve.wait_ge(consts_in, 80)
                TT, TS = dve.tensor_tensor, dve.tensor_scalar
                link(dve.tensor_reduce(mx[:], lg[:], AX.X, ALU.max))
                TT(tmp[:], lg[:], over_last(mx[:], NE), ALU.subtract).then_inc(exp_ok, 1)
                dve.wait_ge(exp_ok, 2)
                link(dve.tensor_reduce(sm[:], aff[:], AX.X, ALU.add))
                link(dve.reciprocal(inv[:], sm[:]))
                link(TT(aff[:], aff[:], over_last(inv[:], NE), ALU.mult))

                def ranks(x, out_, n):
                    e, j = over_last(x, n), x.unsqueeze(2).to_broadcast([P, x.shape[1], n, n])
                    c1, c2 = cmp1[:, 0:x.shape[1]], cmp2[:, 0:x.shape[1]]
                    link(TT(c1, j, e, ALU.is_equal))
                    link(TT(c1, c1, below[:].unsqueeze(1).to_broadcast([P, x.shape[1], n, n]), ALU.mult))
                    link(TT(c2, j, e, ALU.is_gt))
                    link(TT(c1, c1, c2, ALU.add))
                    link(dve.tensor_reduce(out_, c1, AX.X, ALU.add))

                def by_group(x):
                    return x.rearrange("p t (g e) -> p (t g) e", e=GE)

                ranks(by_group(aff[:]), rank[:], GE)
                link(TS(by_group(tmp[:]), rank[:], 1.5, None, ALU.is_lt))
                link(TT(tmp[:], aff[:], tmp[:], ALU.mult))
                link(dve.tensor_reduce(gs[:].rearrange("p t g -> p (t g)"), by_group(tmp[:]), AX.X, ALU.add))
                ranks(gs[:], grank[:], NGR)
                link(TS(gtop[:], grank[:], 0.5, None, ALU.is_lt))
                top = over_last(gtop[:].rearrange("p t g -> p (t g)"), GE)
                link(TS(by_group(first[:]), rank[:], 0.5, None, ALU.is_lt))
                link(TT(by_group(first[:]), by_group(first[:]), top, ALU.mult))
                link(TS(by_group(second[:]), rank[:], 1.0, None, ALU.is_equal))
                link(TT(by_group(second[:]), by_group(second[:]), top, ALU.mult))
                TT(sel[:], first[:], second[:], ALU.add).then_inc(tok_ok, 1)
                dve.wait_ge(tok_ok, 1)
                for a, x in enumerate((first, second)):
                    link(TT(tmp[:], aff[:], x[:], ALU.mult))
                    link(dve.tensor_reduce(wgt[:, a], tmp[:], AX.X, ALU.add))
                link(TT(sm[:], wgt[:, 0], wgt[:, 1], ALU.add))
                link(dve.reciprocal(inv[:], sm[:]))
                link(TT(wgt[:], wgt[:], inv[:].unsqueeze(1).to_broadcast([P, 2, NT]), ALU.mult))
                dve.wait_ge(count_ps, 1)
                link(dve.tensor_copy(totT[:].rearrange("p e t -> p t e"), ps[:, 256:512].rearrange("p (t e) -> p t e", e=NE)))
                link(dve.tensor_tensor_scan(incl[:].rearrange("p e t -> p (e t)"), firsts[:].rearrange("p e t -> p (e t)"),
                                            totT[:].rearrange("p e t -> p (e t)"), 0.0, ALU.mult, ALU.add))
                link(TT(excl[:], incl[:], totT[:], ALU.subtract))
                link(TS(cnt[:], incl[:, :, NT - 1], P - 1.0, None, ALU.add))
                link(dve.tensor_copy(cnt_i[:], cnt[:]))
                link(TS(nb_i[:], cnt_i[:], 7, None, ALU.arith_shift_right))
                link(dve.tensor_copy(nb[:], nb_i[:]))
                link(dve.memset(ones[:], 1.0))
                link(dve.tensor_tensor_scan(ends[:], ones[:], nb[:], 0.0, ALU.mult, ALU.add))
                link(TT(starts[:], ends[:], nb[:], ALU.subtract))
                link(TS(starts[:], starts[:], float(P), None, ALU.mult))
                link(TT(dst[:], ps[:, 0:256].rearrange("p (t e) -> p t e", e=NE), excl[:].rearrange("p e t -> p t e"), ALU.add))
                link(TT(dst[:], dst[:], starts[:].unsqueeze(1).to_broadcast([P, NT, NE]), ALU.add))
                for a, x in enumerate((first, second)):
                    link(TT(tmp[:], dst[:], x[:], ALU.mult))
                    link(dve.tensor_reduce(dest_f[:, a], tmp[:], AX.X, ALU.add))
                dve.tensor_copy(dest[:], dest_f[:]).then_inc(dest_ok, 1)
                link(TT(over[:], ends[:].unsqueeze(1).to_broadcast([P, NB, NE]), over_last(blocks[:], NE), ALU.is_le))
                link(dve.tensor_reduce(be[:], over[:], AX.X, ALU.add))
                link(TS(be[:], be[:], NE - 1.0, None, ALU.min))
                link(dve.tensor_copy(plan[:, NB:2 * NB], be[:]))
                link(TS(plan[:, 0:NB], plan[:, NB:2 * NB], 1, None, ALU.bitwise_and))
                link(TS(be[:], be[:], 1.0, 16.0, ALU.add, ALU.mult))
                link(dve.tensor_copy(plan[:, NB:2 * NB], be[:]))
                link(TS(ends[:], ends[:], 1.0, None, ALU.add))
                dve.wait_ge(dest_ok, 1)
                dve.tensor_copy(plan[:, 2 * NB:], ends[:]).then_inc(plan_ok, 1)


FF = 512
KF = FF // P


def experts(nc, xn_rows, row_tok, plan_in, w_gate, w_up, w_down, ident_in, y_rows):
    with ExitStack() as stack:
        at = Place(nc, stack, "moe")
        ident = at.sb("ident", [P, P])
        rows = at.sb("rows", [P, NB], I32)
        plan = at.sb("plan", [P, 2 * NB + NE], I32)
        idx = [at.sb(f"idx{i}", [P, 1], I32) for i in range(2)]
        wg = at.sb("wg", [P, 2, KD, FF])
        wu = at.sb("wu", [P, 2, KD, FF])
        wd = at.sb("wd", [P, 2, KF, D])
        x = at.sb("x", [P, 2, D])
        xT = at.sb("xT", [P, 2, KD, P])
        sg = at.sb("sg", [P, FF])
        gg = at.sb("gg", [P, FF])
        hh = at.sb("hh", [P, FF])
        hT = at.sb("hT", [P, 2, KF, P])
        y = at.sb("y", [P, 2, D])
        psT = [at.ps(f"psT{i}", (P, 4, P)) for i in range(2)]
        psG, psU, psH = at.ps("psG"), at.ps("psU"), at.ps("psH")
        psY = at.ps("psY", (P, 2, HALF))
        consts_in = at.sem("consts_in")
        wg_in, wu_in, wd_in = at.sem("wg_in"), at.sem("wu_in"), at.sem("wd_in")
        s = {n: at.sem(n) for n in "idx_ok xT_ps xT_ok g_ps u_ps sg_ok gg_ok hh_ok hT_ps hT_ok y_ps y_ok".split()}
        x_in = [at.sem(f"x_in{i}") for i in range(2)]
        y_out = [at.sem(f"y_out{i}") for i in range(2)]

        def later(t, n=1):
            return not isinstance(t, int) or t >= n

        def done(eng, name, t, n=1, per=1):
            if eng in (nc.sync, nc.gpsimd):
                at.hold(eng, s[name], t * per + n)
            else:
                eng.wait_ge(s[name], t * per + n)

        def inside(t):
            return not isinstance(t, int) or t < NB

        def blocks_of(eng, body):
            body(0, 0)
            body(1, 1)
            with eng.Fori(1, NB // 2 - 1) as pair:
                body(pair * 2, 0)
                body(pair * 2 + 1, 1)
            for t in range(NB // 2 * 2 - 2, NB):
                body(t, t % 2)

        with nc.Block() as block:
            @block.sync
            def _(sp):
                sp.dma_start(plan[:], plan_in).then_inc(consts_in, 16)
                sp.dma_start(ident[:], ident_in).then_inc(consts_in, 16)
                with nc.allow_non_contiguous_dma(reason="one row number per partition and block"):
                    sp.dma_start(rows[:], row_tok.rearrange("(b p) o -> p (b o)", p=P)).then_inc(consts_in, 16)

                def load(e, slot):
                    if later(e, 2):
                        end = sp.value_load(plan[0:1, bass.ds(e + (2 * NB - 2), 1)], min_val=1, max_val=NB + 1)
                        at.hold(sp, s["y_ps"], end)
                    for dst, src, w_in in ((wg, w_gate, wg_in), (wu, w_up, wu_in), (wd, w_down, wd_in)):
                        if later(e):
                            at.hold(sp, w_in, e * 16)
                        sp.dma_start(dst[:, slot], src[0, bass.ds(e, 1)].rearrange("a (k p) n -> p (a k) n", p=P)).then_inc(w_in, 16)

                sp.wait_ge(consts_in, 48)
                load(0, 0)
                load(1, 1)
                with sp.Fori(1, NE // 2) as pair:
                    load(pair * 2, 0)
                    load(pair * 2 + 1, 1)

            @block.gpsimd
            def _(pool):
                pool.wait_ge(consts_in, 48)

                def gather(t, b):
                    done(pool, "idx_ok", t)
                    if later(t, 2):
                        done(pool, "xT_ps", t - 2, 2, 2)
                    pool.indirect_dma_start(x[:, b], None, xn_rows, bass.IndirectOffsetOnAxis(ap=idx[b][:], axis=0)).then_inc(x_in[b], 16)

                def store(t, b):
                    done(pool, "y_ok", t, 2, 2)
                    pool.dma_start(y_rows[bass.ds(t * P, P), :], y[:, b]).then_inc(y_out[b], 16)

                for t in range(3):
                    gather(t, t % 2)

                def tile(t, b):
                    if inside(t + 3):
                        gather(t + 3, 1 - b)
                    if later(t):
                        store(t - 1, 1 - b)

                blocks_of(pool, tile)
                store(NB - 1, (NB - 1) % 2)
                for b in range(2):
                    pool.wait_ge(y_out[b], (NB + 1 - b) // 2 * 16)

            @block.scalar
            def _(act):
                def take_xT(t, b):
                    for i in range(2):
                        done(act, "xT_ps", t, i + 1, 2)
                        if i == 0 and later(t, 2):
                            done(act, "u_ps", t - 2)
                        act.activation(xT[:, b, i * 4:(i + 1) * 4], psT[i][:], ACT.Copy).then_inc(s["xT_ok"], 1)

                def tile(t, b):
                    done(act, "g_ps", t)
                    if later(t):
                        done(act, "gg_ok", t - 1)
                    act.activation(sg[:], psG[:], ACT.Sigmoid).then_inc(s["sg_ok"], 1)
                    if inside(t + 1):
                        take_xT(t + 1, 1 - b)
                    if later(t):
                        evac_y(t - 1, 1 - b)
                    done(act, "hT_ps", t)
                    if later(t, 2):
                        done(act, "y_ps", t - 2, 2)
                    act.activation(hT[:, b], psH[:].rearrange("p (k t) -> p k t", k=KF), ACT.Copy).then_inc(s["hT_ok"], 1)

                def evac_y(t, b):
                    done(act, "y_ps", t, 2)
                    if later(t, 2):
                        act.wait_ge(y_out[b], (t - b) * 8)
                    act.activation(y[:, b, HALF:D], psY[:, 1], ACT.Copy).then_inc(s["y_ok"], 1)

                take_xT(0, 0)
                blocks_of(act, tile)
                evac_y(NB - 1, (NB - 1) % 2)

            @block.vector
            def _(dve):
                dve.wait_ge(consts_in, 48)

                def index(t, b):
                    if later(t, 2):
                        dve.wait_ge(x_in[b], (t - b) * 8)
                    dve.tensor_copy(idx[b][:], rows[:, bass.ds(t, 1)]).then_inc(s["idx_ok"], 1)

                def tile(t, b):
                    done(dve, "sg_ok", t)
                    if later(t):
                        done(dve, "hh_ok", t - 1)
                    dve.tensor_tensor(gg[:], psG[:], sg[:], ALU.mult).then_inc(s["gg_ok"], 1)
                    done(dve, "gg_ok", t)
                    done(dve, "u_ps", t)
                    if later(t):
                        done(dve, "hT_ps", t - 1)
                    dve.tensor_tensor(hh[:], psU[:], gg[:], ALU.mult).then_inc(s["hh_ok"], 1)
                    if inside(t + 3):
                        index(t + 3, 1 - b)
                    if later(t):
                        evac_y(t - 1, 1 - b)

                def evac_y(t, b):
                    done(dve, "y_ps", t, 2)
                    if later(t, 2):
                        dve.wait_ge(y_out[b], (t - b) * 8)
                    dve.tensor_copy(y[:, b, 0:HALF], psY[:, 0]).then_inc(s["y_ok"], 1)

                index(0, 0)
                index(1, 1)
                index(2, 0)
                blocks_of(dve, tile)
                evac_y(NB - 1, (NB - 1) % 2)

            @block.tensor
            def _(pe):
                pe.sem_inc(s["y_ps"], 1)
                pe.wait_ge(consts_in, 48)

                def transpose_x(t, b):
                    pe.wait_ge(x_in[b], (t - b + 2) * 8)
                    for i in range(2):
                        if later(t):
                            done(pe, "xT_ok", t - 1, i + 1, 2)
                        for j in range(4):
                            last = pe.transpose(psT[i][:, j], x[:, b, (i * 4 + j) * P:(i * 4 + j + 1) * P], ident[:])
                        last.then_inc(s["xT_ps"], 1)

                def slot_of(t):
                    return pe.value_load(plan[0:1, bass.ds(t, 1)], min_val=0, max_val=1)

                def up(t, b, slot):
                    have = pe.value_load(plan[0:1, bass.ds(t + NB, 1)], min_val=16, max_val=NE * 16)
                    done(pe, "xT_ok", t, 2, 2)
                    for ps, w, w_in, name, free in ((psG, wg, wg_in, "g_ps", "gg_ok"), (psU, wu, wu_in, "u_ps", "hh_ok")):
                        pe.wait_ge(w_in, have)
                        if later(t):
                            done(pe, free, t - 1)
                        for k in range(KD):
                            last = pe.matmul(ps[:], xT[:, b, k], w[:, bass.ds(slot, 1), k, :], start=(k == 0), stop=(k == KD - 1))
                        last.then_inc(s[name], 1)

                def down(t, b, slot):
                    have = pe.value_load(plan[0:1, bass.ds(t + NB, 1)], min_val=16, max_val=NE * 16)
                    pe.wait_ge(wd_in, have)
                    done(pe, "hT_ok", t)
                    if later(t):
                        done(pe, "y_ok", t - 1, 2, 2)
                    for n in range(2):
                        for k in range(KF):
                            last = pe.matmul(psY[:, n], hT[:, b, k], wd[:, bass.ds(slot, 1), k, n * HALF:(n + 1) * HALF],
                                             start=(k == 0), stop=(k == KF - 1))
                    last.then_inc(s["y_ps"], 1)

                def turn_h(t, b):
                    done(pe, "hh_ok", t)
                    if later(t):
                        done(pe, "hT_ok", t - 1)
                    for k in range(KF):
                        last = pe.transpose(psH[:, k * P:(k + 1) * P], hh[:, k * P:(k + 1) * P], ident[:])
                    last.then_inc(s["hT_ps"], 1)

                def tile(t, b):
                    up(t, b, slot_of(t))
                    if inside(t + 1):
                        transpose_x(t + 1, 1 - b)
                    if later(t):
                        down(t - 1, 1 - b, slot_of(t - 1))
                    turn_h(t, b)

                transpose_x(0, 0)
                blocks_of(pe, tile)
                down(NB - 1, (NB - 1) % 2, slot_of(NB - 1))


PD = 256
KP = PD // P


def embed(nc, h1, y_rows, dest_in, wgt_in, p_in, ple_proj, ple_norm, ple_gate, ident_in, out):
    NW = KD + KP
    NS = 4
    with ExitStack() as stack:
        at = Place(nc, stack, "ple")
        ident = at.sb("ident", [P, P])
        gain = at.sb("gain", [P, D])
        eps = at.sb("eps", [P, 1])
        dest = at.sb("dest", [P, 2, NT], I32)
        wgt = at.sb("wgt", [P, 2, NT])
        idx = [[at.sb(f"idx{i}{a}", [P, 1], I32) for a in range(2)] for i in range(2)]
        wraw = at.sb("wraw", [P, NS, D])
        whi = at.sb("whi", [P, NW, D], F32R)
        wlo = at.sb("wlo", [P, NW, D], F32R)
        h = at.sb("h", [P, NS, D])
        y = at.sb("y", [P, 2, 2, D])
        pp = at.sb("pp", [P, NS, PD])
        ahi = at.sb("ahi", [P, 2, NW, P], F32R)
        alo = at.sb("alo", [P, 2, NW, P], F32R)
        sq = at.sb("sq", [P, D])
        ss, lnm, rs = (at.sb(n, [P, 2]) for n in ("ss", "lnm", "rs"))
        ple = at.sb("ple", [P, 2, D])
        sg = at.sb("sg", [P, 2, D])
        psT = [at.ps(f"psT{i}", (P, 4, P)) for i in range(2)]
        psP = at.ps("psP", (P, KP, P))
        psG = at.ps("psG", (P, 2, HALF))
        psE = at.ps("psE", (P, 2, HALF))
        consts_in, gain_in, eps_set = at.sem("consts_in"), at.sem("gain_in"), at.sem("eps_set")
        w_in = [at.sem(f"w_in{i}") for i in range(NS)]
        whi_ok, wlo_ok = at.sem("whi_ok"), at.sem("wlo_ok")
        h_in, p_sem, stored = ([at.sem(f"{n}{i}") for i in range(NS)] for n in ("h_in", "p_in", "stored"))
        y_in = [at.sem(f"y_in{i}") for i in range(2)]
        idx_ok = at.sem("idx_ok")
        ha_ok = at.sem("ha_ok")
        hb_ok = at.sem("hb_ok")
        pT_ps = at.sem("pT_ps")
        aT_ps = at.sem("aT_ps")
        phi_ok, plo_ok = at.sem("phi_ok"), at.sem("plo_ok")
        ahi_ok, alo_ok = at.sem("ahi_ok"), at.sem("alo_ok")
        e_ps = at.sem("e_ps")
        g_ps = at.sem("g_ps")
        sq_ok, lnm_ok, rs_ok = at.sem("sq_ok"), at.sem("lnm_ok"), at.sem("rs_ok")
        ple_ok = at.sem("ple_ok")
        sg_ok = at.sem("sg_ok")
        sp_ok = at.sem("sp_ok")
        o_ok = at.sem("o_ok")

        def later(t, n=1):
            return not isinstance(t, int) or t >= n

        def inside(t):
            return not isinstance(t, int) or t < NT

        def used(t, slots, u):
            return (t - u % slots + slots) * (16 // slots)

        def steps(eng, body):
            for u in range(4):
                body(u, u)
            with eng.Fori(1, NT // 4 - 1) as g:
                for u in range(4):
                    body(g * 4 + u, u)
            for u in range(4):
                body(NT - 4 + u, u)

        with nc.Block() as block:
            @block.sync
            def _(sp):
                sp.dma_start(ident[:], ident_in).then_inc(consts_in, 16)
                sp.dma_start(dest[:].rearrange("p a t -> p (a t)"), dest_in).then_inc(consts_in, 16)
                sp.dma_start(wgt[:].rearrange("p a t -> p (a t)"), wgt_in).then_inc(consts_in, 16)

                def load(t, u):
                    v = u % NS
                    if later(t, NS):
                        at.hold(sp, stored[v], used(t - NS, NS, v))
                        at.hold(sp, pT_ps, t - NS + 1)
                    sp.dma_start(pp[:, v], p_in[bass.ds(t * P, P), :]).then_inc(p_sem[v], 16)
                    sp.dma_start(h[:, v], h1[bass.ds(t * P, P), :]).then_inc(h_in[v], 16)

                load(0, 0)
                load(1, 1)
                for k in range(NW):
                    if k >= NS:
                        sp.wait_ge(whi_ok, k - NS + 1)
                        sp.wait_ge(wlo_ok, k - NS + 1)
                    src = ple_proj[k * P:(k + 1) * P] if k < KP else ple_gate[(k - KP) * P:(k - KP + 1) * P]
                    sp.dma_start(wraw[:, k % NS], src).then_inc(w_in[k % NS], 16)
                sp.dma_start(gain[:], ple_norm.broadcast_to([P, D])).then_inc(gain_in, 16)
                load(2, 2)

                def step(t, u):
                    if inside(t + 3):
                        load(t + 3, u + 3)
                    at.hold(sp, o_ok, t + 1)
                    sp.dma_start(out[bass.ds(t * P, P), :], h[:, u % NS]).then_inc(stored[u % NS], 16)

                steps(sp, step)
                for v in range(NS):
                    sp.wait_ge(stored[v], NT // NS * 16)

            @block.gpsimd
            def _(pool):
                pool.wait_ge(consts_in, 48)

                def gather(t, u):
                    b = u % 2
                    at.hold(pool, idx_ok, (t + 1) * 2)
                    if later(t, 2):
                        at.hold(pool, hb_ok, t - 1)
                    for a in range(2):
                        pool.indirect_dma_start(y[:, b, a], None, y_rows, bass.IndirectOffsetOnAxis(ap=idx[b][a][:], axis=0)).then_inc(y_in[b], 16)

                for t in range(3):
                    gather(t, t)

                def step(t, u):
                    b = u % 2
                    if inside(t + 3):
                        gather(t + 3, u + 3)
                    pool.wait_ge(ple_ok, t + 1)
                    pool.wait_ge(sg_ok, t + 1)
                    pool.tensor_tensor(ple[:, b], ple[:, b], sg[:, b], ALU.mult).then_inc(sp_ok, 1)

                steps(pool, step)

            @block.scalar
            def _(act):
                def split_w(k):
                    act.wait_ge(w_in[k % NS], 16 * (k // NS + 1))
                    act.activation(whi[:, k], wraw[:, k % NS], ACT.Copy).then_inc(whi_ok, 1)

                def front(t, u):
                    b = u % 2
                    act.wait_ge(pT_ps, t + 1)
                    if later(t, 2):
                        act.wait_ge(g_ps, t - 1)
                    act.activation(ahi[:, b, 0:KP], psP[:], ACT.Copy).then_inc(phi_ok, 1)
                    for i in range(2):
                        act.wait_ge(aT_ps, t * 2 + i + 1)
                        act.activation(ahi[:, b, KP + i * 4:KP + (i + 1) * 4], psT[i][:], ACT.Copy).then_inc(ahi_ok, 1)

                def step(t, u):
                    b = u % 2
                    if inside(t + 1):
                        front(t + 1, u + 1)
                    act.wait_ge(e_ps, t + 1)
                    if later(t, 2):
                        act.wait_ge(ple_ok, t - 1)
                    if later(t):
                        act.wait_ge(sq_ok, t)
                    act.activation(sq[:], psE[:].rearrange("p a n -> p (a n)"), ACT.Square, accum_out=ss[:, b:b + 1]).then_inc(sq_ok, 1)
                    act.wait_ge(sq_ok, t + 1)
                    act.activation(lnm[:, b:b + 1], ss[:, b:b + 1], ACT.Ln, bias=eps[:], scale=1.0 / D).then_inc(lnm_ok, 1)
                    act.wait_ge(lnm_ok, t + 1)
                    act.activation(rs[:, b:b + 1], lnm[:, b:b + 1], ACT.Exp, scale=-0.5).then_inc(rs_ok, 1)
                    act.wait_ge(g_ps, t + 1)
                    if later(t, 2):
                        act.wait_ge(sp_ok, t - 1)
                    act.activation(sg[:, b], psG[:].rearrange("p a n -> p (a n)"), ACT.Sigmoid).then_inc(sg_ok, 1)

                act.wait_ge(eps_set, 1)
                for k in range(NW):
                    split_w(k)
                    if k == 0:
                        front(0, 0)
                steps(act, step)

            @block.vector
            def _(dve):
                dve.memset(eps[:], EPS).then_inc(eps_set, 1)
                dve.wait_ge(consts_in, 48)

                def index(t, u):
                    if later(t, 2):
                        dve.wait_ge(y_in[u % 2], used(t - 2, 2, u) * 2)
                    for a in range(2):
                        dve.tensor_copy(idx[u % 2][a][:], dest[:, a, bass.ds(t, 1)]).then_inc(idx_ok, 1)

                def split_w(k):
                    dve.wait_ge(whi_ok, k + 1)
                    dve.tensor_tensor(wlo[:, k], wraw[:, k % NS], whi[:, k].bitcast(F32), ALU.subtract).then_inc(wlo_ok, 1)

                def add(t, u):
                    b, v = u % 2, u % NS
                    dve.wait_ge(h_in[v], used(t, NS, u))
                    dve.wait_ge(y_in[b], used(t, 2, u) * 2)
                    dve.scalar_tensor_tensor(h[:, v], y[:, b, 0], wgt[:, 0, bass.ds(t, 1)], h[:, v], ALU.mult, ALU.add).then_inc(ha_ok, 1)
                    dve.wait_ge(ha_ok, t + 1)
                    dve.scalar_tensor_tensor(h[:, v], y[:, b, 1], wgt[:, 1, bass.ds(t, 1)], h[:, v], ALU.mult, ALU.add).then_inc(hb_ok, 1)

                def split(t, u):
                    b = u % 2
                    dve.wait_ge(phi_ok, t + 1)
                    dve.tensor_tensor(alo[:, b, 0:KP], psP[:], ahi[:, b, 0:KP].bitcast(F32), ALU.subtract).then_inc(plo_ok, 1)
                    for i in range(2):
                        dve.wait_ge(ahi_ok, t * 2 + i + 1)
                        cut = slice(KP + i * 4, KP + (i + 1) * 4)
                        dve.tensor_tensor(alo[:, b, cut], psT[i][:], ahi[:, b, cut].bitcast(F32), ALU.subtract).then_inc(alo_ok, 1)

                def finish(t, u):
                    b, v = u % 2, u % NS
                    dve.wait_ge(sp_ok, t + 1)
                    dve.tensor_tensor(h[:, v], h[:, v], ple[:, b], ALU.add).then_inc(o_ok, 1)

                def step(t, u):
                    b = u % 2
                    if inside(t + 1):
                        split(t + 1, u + 1)
                    if inside(t + 2):
                        add(t + 2, u + 2)
                    if inside(t + 4):
                        index(t + 4, u + 4)
                    if later(t):
                        finish(t - 1, u + 3)
                    dve.wait_ge(rs_ok, t + 1)
                    if later(t, 2):
                        dve.wait_ge(o_ok, t - 1)
                    dve.scalar_tensor_tensor(ple[:, b], psE[:].rearrange("p a n -> p (a n)"), rs[:, b:b + 1], gain[:],
                                             ALU.mult, ALU.mult).then_inc(ple_ok, 1)

                index(0, 0)
                index(1, 1)
                add(0, 0)
                index(2, 2)
                split_w(0)
                split(0, 0)
                for k in range(1, NW):
                    split_w(k)
                    if k == 3:
                        add(1, 1)
                        index(3, 3)
                dve.wait_ge(gain_in, 16)
                steps(dve, step)
                finish(NT - 1, NT - 1)

            @block.tensor
            def _(pe):
                pe.wait_ge(consts_in, 48)

                def front(t, u):
                    pe.wait_ge(p_sem[u % NS], used(t, NS, u))
                    if later(t):
                        pe.wait_ge(plo_ok, t)
                    for j in range(KP):
                        last = pe.transpose(psP[:, j], pp[:, u % NS, j * P:(j + 1) * P], ident[:])
                    last.then_inc(pT_ps, 1)
                    pe.wait_ge(hb_ok, t + 1)
                    for i in range(2):
                        if later(t):
                            pe.wait_ge(alo_ok, t * 2 - 1 + i)
                        for j in range(4):
                            last = pe.transpose(psT[i][:, j], h[:, u % NS, (i * 4 + j) * P:(i * 4 + j + 1) * P], ident[:])
                        last.then_inc(aT_ps, 1)

                def step(t, u):
                    b = u % 2
                    first = isinstance(t, int) and t == 0
                    if inside(t + 1):
                        front(t + 1, u + 1)
                    pe.wait_ge(plo_ok, t + 1)
                    for ps, k0, k1, done, free in ((psE, 0, KP, e_ps, ple_ok), (psG, KP, NW, g_ps, sg_ok)):
                        if k0:
                            pe.wait_ge(alo_ok, t * 2 + 2)
                        if later(t):
                            pe.wait_ge(free, t)
                        for k in range(k0, k1):
                            if first:
                                pe.wait_ge(wlo_ok, k + 1)
                            for n in range(2):
                                cut = slice(n * HALF, (n + 1) * HALF)
                                for i, (l, r) in enumerate(((ahi, whi), (ahi, wlo), (alo, whi))):
                                    last = pe.matmul(ps[:, n], l[:, b, k], r[:, k, cut], start=(k == k0 and i == 0),
                                                     stop=(k == k1 - 1 and i == 2))
                        last.then_inc(done, 1)

                front(0, 0)
                steps(pe, step)


def build(nc, a, out):
    def scratch(name, shape, dt=F32):
        return nc.dram_tensor(name, list(shape), dt, kind="Internal").ap()

    hgrn_q, hgrn_f, hgrn_k = (scratch(f"hgrn_{n}", (HW, S)) for n in "qfk")
    tok = scratch("tok", (S, 5 * HW))
    mix = scratch("mix", (S, D))
    h1 = scratch("h1", (S, D))
    xn_rows = scratch("xn_rows", (S + 1, D))
    logits = scratch("logits", (P, NT * NE))
    row_tok = scratch("row_tok", (NROW, 1), I32)
    dest = scratch("dest", (P, 2 * NT), I32)
    wgt = scratch("wgt", (P, 2 * NT))
    plan = scratch("plan", (P, 2 * NB + NE), I32)
    y_rows = scratch("y_rows", (NROW, D))
    x, ident = a["x"].rearrange("a s d -> (a s) d"), a["ident"]

    project_in(nc, x, a["mix_norm"], a["w_in"][0], ident, hgrn_q, hgrn_f, hgrn_k, tok)
    recurrence(nc, hgrn_q, hgrn_f, hgrn_k, tok, a["hgrn_lb"], a["hgrn_out_norm"], ident, a["masks"], a["resets"], mix)
    attention(nc, tok, a["q_norm"], a["k_norm"], a["lam_q1"], a["lam_k1"], a["lam_q2"], a["lam_k2"], a["diff_subln"],
              ident, a["causal"], mix)
    project_out(nc, mix, x, a["w_out"][0], a["ffn_norm"], a["w_router"], ident, h1, xn_rows, logits)
    route(nc, logits, a["below"], a["upper"], a["firsts"], a["blocks"], a["tokens"], row_tok, dest, wgt, plan)
    experts(nc, xn_rows, row_tok, plan, a["w_gate"], a["w_up"], a["w_down"], ident, y_rows)
    embed(nc, h1, y_rows, dest, wgt, a["p"].rearrange("a b s d -> (a b s) d"), a["ple_proj"][0], a["ple_norm"],
          a["ple_gate"][0], ident, out.rearrange("a s d -> (a s) d"))


def shape_constants():
    import numpy as np

    s, t = np.meshgrid(np.arange(P), np.arange(P), indexing="ij")
    masks = np.zeros((P, LV, P), np.int32)
    for i, half in enumerate((CH, *HALVES)):
        masks[:, i] = (s // (2 * half) == t // (2 * half)) & (s // half % 2 == 0) & (t // half % 2 == 1)
    base = HALVES[-1]
    masks[:, LV - 1] = (s // base == t // base) & (s <= t)
    resets = np.ones((P, NH * P // CH, CH), np.float32)
    resets[:, :, 0] = 0
    upper = np.stack([s < t, np.ones((P, P), bool)], 1).astype(np.float32)
    firsts = np.ones((P, NE, NT), np.float32)
    firsts[:, :, 0] = 0
    j = np.arange(GE)
    return {
        "ident": np.eye(P, dtype=np.float32),
        "causal": np.where(t > s, -1e30, 0.0).astype(np.float32),
        "masks": masks,
        "resets": resets.reshape(P, NH * P),
        "below": np.tile((j[None, :] < j[:, None]).astype(np.float32), (P, 1, 1)),
        "upper": upper,
        "firsts": firsts,
        "blocks": np.tile(np.arange(NB, dtype=np.float32), (P, 1)),
        "tokens": (np.arange(NT)[None, :] * P + np.arange(P)[:, None]).astype(np.int32),
    }


INPUTS = ("x p mix_norm w_in hgrn_lb hgrn_out_norm q_norm k_norm lam_q1 lam_k1 lam_q2 lam_k2 diff_subln w_out "
          "ffn_norm w_router w_gate w_up w_down ple_proj ple_norm ple_gate").split()


def kernel(**inputs):
    import numpy as np
    import concourse.bacc as bacc
    from concourse.bass_utils import run_bass_kernel_spmd

    nc = bacc.Bacc("TRN2", target_bir_lowering=False, num_devices=1)
    arrays = {n: np.ascontiguousarray(inputs[n]) for n in INPUTS} | shape_constants()
    aps = {n: nc.dram_tensor(n, v.shape, mybir.dt.from_np(v.dtype), kind="ExternalInput").ap() for n, v in arrays.items()}
    out = nc.dram_tensor("out", (1, S, D), F32, kind="ExternalOutput").ap()
    build(nc, aps, out)
    return run_bass_kernel_spmd(nc, [arrays], core_ids=[0]).results[0]["out"]
```

```python
from contextlib import ExitStack

import concourse.bass as bass
from concourse import mybir

F32 = mybir.dt.float32
F32R = mybir.dt.float32r
BF16 = mybir.dt.bfloat16
I32 = mybir.dt.int32

ALU = mybir.AluOpType
ACT = mybir.ActivationFunctionType
AX = mybir.AxisListType
P = 128

D = 1024
S = 2048
KD = D // P
NT = S // P
HW = 512
NH = HW // P
EPS = 1e-6


class Place:

    def __init__(self, nc, stack, stage):
        self.nc, self.stack, self.stage, self.sems, self.held = nc, stack, stage, [], None
        stack.callback(self.clear)

    def sb(self, name, shape, dt=F32):
        return self.stack.enter_context(self.nc.sbuf_tensor(f"{self.stage}_{name}", shape, dt))

    def ps(self, name, shape=(P, 512)):
        return self.stack.enter_context(self.nc.psum_tensor(f"{self.stage}_{name}", list(shape), F32))

    def clear(self):
        self.nc.clear_and_free_semaphores(self.sems)
        self.nc.all_engine_barrier()

    def hold(self, eng, sem, value):
        eng.wait_ge(sem, value)
        if not isinstance(value, int):
            if self.held is None:
                self.held = self.sem("held")
            eng.sem_inc(self.held, 1)

    def sem(self, name):
        self.sems.append(self.nc.alloc_semaphore(f"{self.stage}_{name}"))
        return self.sems[-1]


GT = 4
GW = GT * P
NG = NT // GT
SLICES = [(2 * HW, HW, "zi"), (3 * HW, HW, "zg"), (4 * HW, HW, "dq"), (5 * HW, HW, "dk"), (6 * HW, HW, "dv"),
          (0, HW, "zq"), (HW, HW // 2, "zf0"), (HW + HW // 2, HW // 2, "zf1")]
NSL = len(SLICES)


def project_in(nc, x, mix_norm, w_in, ident_in, hgrn_q, hgrn_f, hgrn_k, tok):
    groups = [[(s, j) for j in range(GT if s < 5 else w // P)] for s, (_, w, _) in enumerate(SLICES)]
    NGRP = sum(len(g) for g in groups)
    upto = [sum(len(g) for g in groups[:s + 1]) for s in range(NSL)]
    NST = 8
    with ExitStack() as stack:
        at = Place(nc, stack, "in")
        ident = at.sb("ident", [P, P])
        gain = at.sb("gain", [P, KD])
        eps = at.sb("eps", [P, 1])
        xs = at.sb("xs", [P, 2, D])
        xn = at.sb("xn", [P, D])
        ss = at.sb("ss", [P, GT])
        lnms = at.sb("lnms", [P, GT])
        rstd = at.sb("rstd", [P, GT])
        xT = at.sb("xT", [P, KD, GW])
        hhi = at.sb("hhi", [P, KD, GW], F32R)
        hlo = at.sb("hlo", [P, KD, GW], F32R)
        wraw = at.sb("wraw", [P, 2, KD, HW])
        whi = at.sb("whi", [P, 2, KD, HW], F32R)
        wlo = at.sb("wlo", [P, 2, KD, HW], F32R)
        st = at.sb("st", [P, NST, GW])
        psT = [at.ps(f"psT{i}") for i in range(2)]
        psM = [at.ps(f"psM{i}") for i in range(4)]
        NM = len(psM)

        consts_in = at.sem("consts_in")
        x_in = [at.sem(f"x_in{i}") for i in range(2)]
        w_in_sem = [at.sem(f"w_in{i}") for i in range(2)]
        eps_set = at.sem("eps_set")
        squares = at.sem("squares")
        logs = at.sem("logs")
        rstd_ok = at.sem("rstd_ok")
        xn_ok = at.sem("xn_ok")
        xT_ps = at.sem("xT_ps")
        xT_ok = at.sem("xT_ok")
        hi_ok = at.sem("hi_ok")
        lo_ok = at.sem("lo_ok")
        whi_ok = at.sem("whi_ok")
        wlo_ok = at.sem("wlo_ok")
        mm_ok = at.sem("mm_ok")
        sig_ok = at.sem("sig_ok")
        out_ok = at.sem("out_ok")
        out_ok2 = at.sem("out_ok2")
        stored = [at.sem(f"stored{i}") for i in range(NST)]

        stores = []
        for s in range(NSL):
            for (_, j) in groups[s]:
                n = upto[s] - len(groups[s]) + j
                for part in range(2 if s >= 6 else 1):
                    stores.append((s, j, n, part))
        NSTO = len(stores)
        slot = {(s, j, part): k % NST for k, (s, j, n, part) in enumerate(stores)}
        ordinal = {(s, j, part): k for k, (s, j, n, part) in enumerate(stores)}
        assert NSTO % NST == 0 and NGRP % NM == 0, (NSTO, NGRP)
        PER = NSTO // NST

        def x_row(g, t):
            return x[bass.ds((g * GT + t) * P, P), :]

        def by_vector(s, j):
            return s in (1, 5) or (s in (0, 2, 3, 4) and j % 2 == 0)

        order = {}
        nv = ns = 0
        for (s, j, n, part) in stores:
            if by_vector(s, j):
                nv += 1
                order[(s, j, part)] = (out_ok, nv)
            else:
                ns += 1
                order[(s, j, part)] = (out_ok2, ns)
        writer_total = {False: nv, True: ns}

        def writer(s, j, part):
            return order[(s, j, part)]

        def slot_free(eng, g, s, j, part):
            m = ordinal[(s, j, part)] // NST
            if not (isinstance(g, int) and g == 0 and m == 0):
                eng.wait_ge(stored[slot[(s, j, part)]], (g * PER + m) * 16)

        with nc.Block() as block:
            @block.sync
            def _(sp):
                sp.dma_start(ident[:], ident_in).then_inc(consts_in, 16)
                sp.dma_start(gain[:], mix_norm.rearrange("a (k p) -> p (a k)", p=P), allow_slow_non_contiguous=True).then_inc(consts_in, 16)

                def load_x(g, t, n):
                    if not isinstance(n, int) or n >= 2:
                        sp.wait_ge(xn_ok, n - 1)
                    sp.dma_start(xs[:, t % 2, :], x_row(g, t)).then_inc(x_in[t % 2], 16)

                def load_w(g, s):
                    c0, w, _ = SLICES[s]
                    if not (isinstance(g, int) and g == 0 and s < 2):
                        sp.wait_ge(whi_ok, g * NSL + s - 1)
                        sp.wait_ge(wlo_ok, g * NSL + s - 1)
                    sp.dma_start(wraw[:, s % 2, :, 0:w], w_in[:, c0:c0 + w].rearrange("(k p) n -> p k n", p=P)) \
                        .then_inc(w_in_sem[s % 2], 16)

                for t in range(GT):
                    load_x(0, t, t)
                    if t == 1:
                        load_w(0, 0)
                for s in range(1, 3):
                    load_w(0, s)
                sp.wait_ge(xn_ok, GT)

                def group(g, last):
                    for s in range(3, NSL):
                        load_w(g, s)
                        if not last and s - 3 < GT:
                            load_x(g + 1, s - 3, (g + 1) * GT + s - 3)
                    if not last:
                        for s in range(3):
                            load_w(g + 1, s)

                group(0, False)
                with sp.Fori(1, NG - 1) as g:
                    group(g, False)
                group(NG - 1, True)

            @block.gpsimd
            def _(pool):
                def group(g):
                    for (s, j, n, part) in stores:
                        k = slot[(s, j, part)]
                        sem, cnt = writer(s, j, part)
                        at.hold(pool, sem, g * writer_total[sem is out_ok2] + cnt)
                        if s < 5:
                            dst = tok[bass.ds((g * GT + j) * P, P), s * HW:(s + 1) * HW]
                        elif s == 5:
                            dst = hgrn_q[j * P:(j + 1) * P, bass.ds(g * GW, GW)]
                        else:
                            r = (s - 6) * (HW // 2) + j * P
                            dst = (hgrn_f, hgrn_k)[part][r:r + P, bass.ds(g * GW, GW)]
                        pool.dma_start(dst, st[:, k, :]).then_inc(stored[k], 16)

                with pool.Fori(0, NG) as g:
                    group(g)
                for k in range(NST):
                    pool.wait_ge(stored[k], 16 * PER * NG)

            @block.scalar
            def _(act):
                def norm_stats(g, t):
                    n = g * GT + t
                    act.wait_ge(x_in[t % 2], (g * (GT // 2) + t // 2 + 1) * 16)
                    if not (isinstance(g, int) and g == 0 and t == 0):
                        act.wait_ge(xT_ps, n * 2)
                    act.activation(xn[:], xs[:, t % 2, :], ACT.Square, accum_out=ss[:, t:t + 1]).then_inc(squares, 1)
                    act.wait_ge(squares, n + 1)
                    act.activation(lnms[:, t:t + 1], ss[:, t:t + 1], ACT.Ln, bias=eps[:], scale=1.0 / D).then_inc(logs, 1)
                    act.wait_ge(logs, n + 1)
                    act.activation(rstd[:, t:t + 1], lnms[:, t:t + 1], ACT.Exp, scale=-0.5).then_inc(rstd_ok, 1)
                    act.wait_ge(rstd_ok, n + 1)
                    act.activation(xn[:], xs[:, t % 2, :], ACT.Copy, scale=rstd[:, t:t + 1]).then_inc(xn_ok, 1)

                def split_h(g, t):
                    act.wait_ge(xT_ok, (g * GT + t + 1) * 2)
                    if not (isinstance(g, int) and g == 0) and t == 0:
                        act.wait_ge(mm_ok, g * NGRP)
                    act.activation(hhi[:, :, t * P:(t + 1) * P], xT[:, :, t * P:(t + 1) * P], ACT.Copy).then_inc(hi_ok, 1)

                def split_w(g, s):
                    w = SLICES[s][1]
                    act.wait_ge(w_in_sem[s % 2], (g * (NSL // 2) + s // 2 + 1) * 16)
                    if not (isinstance(g, int) and g == 0 and s < 2):
                        before = g * NGRP + (upto[s - 2] if s >= 2 else upto[s - 2 + NSL] - NGRP)
                        act.wait_ge(mm_ok, before)
                    act.activation(whi[:, s % 2, :, 0:w], wraw[:, s % 2, :, 0:w], ACT.Copy).then_inc(whi_ok, 1)

                def evacuate(g, s):
                    for (_, j) in groups[s]:
                        n = upto[s] - len(groups[s]) + j
                        src = psM[n % NM]
                        if s in (1, 5):
                            act.wait_ge(mm_ok, g * NGRP + n + 1)
                            slot_free(act, g, s, j, 0)
                            act.activation(st[:, slot[(s, j, 0)], :], src[:], ACT.Sigmoid).then_inc(sig_ok, 1)
                        elif s >= 6:
                            act.wait_ge(mm_ok, g * NGRP + n + 1)
                            for part in range(2):
                                slot_free(act, g, s, j, part)
                                act.activation(st[:, slot[(s, j, part)], :], src[:], ACT.Sigmoid,
                                               scale=(1.0, -1.0)[part]).then_inc(out_ok2, 1)
                        elif not by_vector(s, j):
                            act.wait_ge(mm_ok, g * NGRP + n + 1)
                            slot_free(act, g, s, j, 0)
                            act.activation(st[:, slot[(s, j, 0)], :], src[:], ACT.Copy).then_inc(out_ok2, 1)

                act.wait_ge(eps_set, 1)
                for t in range(GT):
                    norm_stats(0, t)
                split_w(0, 0)

                def body(g, last):
                    for t in range(GT):
                        split_h(g, t)
                    for s in range(NSL):
                        if s + 1 < NSL:
                            split_w(g, s + 1)
                        elif not last:
                            split_w(g + 1, 0)
                        if 2 <= s < 2 + GT and not last:
                            norm_stats(g + 1, s - 2)
                        evacuate(g, s)

                body(0, False)
                with act.Fori(1, NG - 1) as g:
                    body(g, False)
                body(NG - 1, True)

            @block.vector
            def _(dve):
                dve.memset(eps[:], EPS).then_inc(eps_set, 1)
                dve.wait_ge(consts_in, 32)

                def take_xT(g, t):
                    for half in range(2):
                        dve.wait_ge(xT_ps, (g * GT + t) * 2 + half + 1)
                        if not (isinstance(g, int) and g == 0) and t == 0 and half == 0:
                            dve.wait_ge(hi_ok, g * GT)
                            dve.wait_ge(lo_ok, g * GT)
                        k0 = half * KD // 2
                        dve.tensor_tensor(xT[:, k0:k0 + KD // 2, t * P:(t + 1) * P],
                                          psT[half][:].rearrange("p (k t) -> p k t", k=KD // 2),
                                          gain[:, k0:k0 + KD // 2].unsqueeze(2).to_broadcast([P, KD // 2, P]),
                                          ALU.mult).then_inc(xT_ok, 1)

                def split_h(g, t):
                    dve.wait_ge(hi_ok, g * GT + t + 1)
                    dve.tensor_tensor(hlo[:, :, t * P:(t + 1) * P], xT[:, :, t * P:(t + 1) * P],
                                      hhi[:, :, t * P:(t + 1) * P].bitcast(F32), ALU.subtract).then_inc(lo_ok, 1)

                def split_w(g, s):
                    w = SLICES[s][1]
                    dve.wait_ge(whi_ok, g * NSL + s + 1)
                    dve.tensor_tensor(wlo[:, s % 2, :, 0:w], wraw[:, s % 2, :, 0:w],
                                      whi[:, s % 2, :, 0:w].bitcast(F32), ALU.subtract).then_inc(wlo_ok, 1)

                def evacuate(g, s):
                    for (_, j) in groups[s]:
                        n = upto[s] - len(groups[s]) + j
                        src = psM[n % NM]
                        if s in (1, 5):
                            i = j if s == 1 else GT + j
                            dve.wait_ge(sig_ok, g * 2 * GT + i + 1)
                            o = st[:, slot[(s, j, 0)], :]
                            dve.tensor_tensor(o, src[:], o, ALU.mult).then_inc(out_ok, 1)
                        elif by_vector(s, j):
                            dve.wait_ge(mm_ok, g * NGRP + n + 1)
                            slot_free(dve, g, s, j, 0)
                            dve.tensor_copy(st[:, slot[(s, j, 0)], :], src[:]).then_inc(out_ok, 1)

                for t in range(GT):
                    take_xT(0, t)
                split_w(0, 0)

                def body(g, last):
                    for t in range(GT):
                        split_h(g, t)
                    for s in range(NSL):
                        if s + 1 < NSL:
                            split_w(g, s + 1)
                        elif not last:
                            split_w(g + 1, 0)
                        if 3 <= s < 3 + GT and not last:
                            take_xT(g + 1, s - 3)
                        evacuate(g, s)

                body(0, False)
                with dve.Fori(1, NG - 1) as g:
                    body(g, False)
                body(NG - 1, True)

            @block.tensor
            def _(pe):
                pe.wait_ge(consts_in, 32)

                def transpose_x(g, t):
                    pe.wait_ge(xn_ok, g * GT + t + 1)
                    for half in range(2):
                        if not (isinstance(g, int) and g == 0 and t == 0):
                            pe.wait_ge(xT_ok, (g * GT + t) * 2 - 1 + half)
                        for i in range(KD // 2):
                            k = half * KD // 2 + i
                            last = pe.transpose(psT[half][:, i * P:(i + 1) * P], xn[:, k * P:(k + 1) * P], ident[:])
                        last.then_inc(xT_ps, 1)

                def bank_free(g, s, j):
                    n = upto[s] - len(groups[s]) + j - NM
                    back = n < 0
                    if back and isinstance(g, int) and g == 0:
                        return
                    if back:
                        n += NGRP
                    s2 = next(i for i in range(NSL) if n < upto[i])
                    j2 = n - (upto[s2] - len(groups[s2]))
                    sem, cnt = writer(s2, j2, 1 if s2 >= 6 else 0)
                    total = writer_total[sem is out_ok2]
                    pe.wait_ge(sem, g * total + (cnt - total if back else cnt))

                def multiply(g, s):
                    pe.wait_ge(wlo_ok, g * NSL + s + 1)
                    pe.wait_ge(whi_ok, g * NSL + s + 1)
                    b = s % 2
                    for (_, j) in groups[s]:
                        n = upto[s] - len(groups[s]) + j
                        if s == 0:
                            pe.wait_ge(hi_ok, g * GT + j + 1)
                            pe.wait_ge(lo_ok, g * GT + j + 1)
                        bank_free(g, s, j)
                        out = psM[n % NM][:]
                        cut = slice(j * P, (j + 1) * P)
                        for k in range(KD):
                            if s < 5:
                                three = ((hhi[:, k, cut], whi[:, b, k, :]), (hhi[:, k, cut], wlo[:, b, k, :]),
                                         (hlo[:, k, cut], whi[:, b, k, :]))
                            else:
                                three = ((whi[:, b, k, cut], hhi[:, k, :]), (whi[:, b, k, cut], hlo[:, k, :]),
                                         (wlo[:, b, k, cut], hhi[:, k, :]))
                            for i, (l, r) in enumerate(three):
                                last = pe.matmul(out, l, r, start=(k == 0 and i == 0), stop=(k == KD - 1 and i == 2))
                        last.then_inc(mm_ok, 1)

                for t in range(GT):
                    transpose_x(0, t)

                def body(g, last):
                    for s in range(NSL):
                        if 3 <= s < 3 + GT and not last:
                            transpose_x(g + 1, s - 3)
                        multiply(g, s)

                body(0, False)
                with pe.Fori(1, NG - 1) as g:
                    body(g, False)
                body(NG - 1, True)


CH = 64
MIN_FORGET = 1e-6
HALVES = (32, 16, 8, 4)
LV = 2 + len(HALVES)


def recurrence(nc, hgrn_q, hgrn_f, hgrn_k, tok, hgrn_lb, out_norm, ident_in, masks_in, resets_in, mix):
    with ExitStack() as stack:
        at = Place(nc, stack, "rec")
        ident = at.sb("ident", [P, P])
        masks = at.sb("masks", [P, LV, P], I32)
        resets = at.sb("resets", [P, NH * P])
        lb_in = at.sb("lb_in", [P, NH])
        lbs = at.sb("lbs", [P, 5, NH])
        gain = at.sb("gain", [P, P])
        eps = at.sb("eps", [P, 1])
        W4 = [P, 2, NH, P]
        q, f, k, v, g = (at.sb(n, W4) for n in ("q", "f", "k", "v", "g"))
        km = at.sb("km", W4)
        fm, fl, lf, cum = (at.sb(n, [P, NH, P]) for n in ("fm", "fl", "lf", "cum"))
        d64, dB = at.sb("d64", [P, NH, P]), at.sb("dB", W4)
        dH = at.sb("dH", [P, len(HALVES), NH, P])
        e0, eK = at.sb("e0", [P, NH, P]), at.sb("eK", [P, NH, P])
        eH = at.sb("eH", [P, len(HALVES), NH, P])
        eBq, eBk = at.sb("eBq", [P, NH, P]), at.sb("eBk", [P, NH, P])
        ql = at.sb("ql", [P, 2, LV, NH, P])
        kl = at.sb("kl", [P, 2, LV, NH, P])
        qI, kD = at.sb("qI", W4), at.sb("kD", W4)
        eL = at.sb("eL", [P, 2, NH])
        sT = at.sb("sT", W4)
        kDT = at.sb("kDT", W4)
        state = at.sb("state", [P, 2, NH, P])
        osq = at.sb("osq", [P, NH, P])
        oss, oln, ors = (at.sb(n, [P, NH]) for n in ("oss", "oln", "ors"))
        gg = at.sb("gg", W4)
        on = at.sb("on", [P, NH, P])
        o = at.sb("o", W4)
        psA = [at.ps(f"psA{i}", (P, NH, P)) for i in range(3)]
        psK = at.ps("psK", (P, NH, P))
        psU = at.ps("psU", (P, NH, P))
        psO = [at.ps(f"psO{i}", (P, NH, P)) for i in range(2)]
        NA = len(psA)

        consts_in, init = at.sem("consts_in"), at.sem("init")
        lb_ok = at.sem("lb_ok")
        fk_in, qg_in, v_in = ([at.sem(f"{n}{i}") for i in range(2)] for n in ("fk_in", "qg_in", "v_in"))
        names = ("fm_ok km_ok fl_ok lf_ok cum_ok d64_ok dB_ok dH_ok e0_ok eK_ok eH_ok eB_ok q0_ok k0_ok qH_ok kH_ok qB_ok kB_ok "
                 "qI_ok kD_ok eL_ok qIc_ok kDc_ok kDT_ps kDT_ok lv_ps lv_ok upd_ps state_ok o_ps osq_ok oss_ok oln_ok ors_ok gg_ok on_ok o_ok").split()
        s = {n: at.sem(n) for n in names}
        stored = [at.sem(f"stored{i}") for i in range(2)]

        def later(t, n=1):
            return not isinstance(t, int) or t >= n

        def done(eng, name, t, n=1, per=1):
            if eng in (nc.sync, nc.gpsimd) or name == "lv_ps" and eng is nc.vector:
                at.hold(eng, s[name], t * per + n)
            else:
                eng.wait_ge(s[name], t * per + n)

        def second(x, H):
            return x.rearrange("p h (b t) -> p (h b) t", t=2 * H)[:, :, H:2 * H]

        def first_(x, H):
            return x.rearrange("p h (b t) -> p (h b) t", t=2 * H)[:, :, 0:H]

        def from_middle(x, H, at_):
            b = x.rearrange("p h (b t) -> p (h b) t", t=2 * H)
            return b, b[:, :, at_:at_ + 1].to_broadcast([P, NH * P // (2 * H), 2 * H])

        def has(t):
            return not isinstance(t, int) or 0 <= t < NT

        def steps(eng, body):
            for t in range(-1, 4):
                body(t, t % 2)
            with eng.Fori(2, NT // 2 - 1) as pair:
                body(pair * 2, 0)
                body(pair * 2 + 1, 1)
            for t in range(NT - 2, NT + 2):
                body(t, t % 2)

        def loaded(eng, sem, t, b, loads):
            at.hold(eng, sem[b], (t - b + 2) * 8 * loads)

        with nc.Block() as block:
            @block.sync
            def _(sp):
                for dst, src in ((ident, ident_in), (masks, masks_in), (resets, resets_in)):
                    sp.dma_start(dst[:], src).then_inc(consts_in, 16)
                sp.dma_start(lb_in[:], hgrn_lb.rearrange("a (h d) -> d (a h)", d=P), allow_slow_non_contiguous=True).then_inc(consts_in, 16)
                sp.dma_start(gain[:], out_norm.broadcast_to([P, P])).then_inc(consts_in, 16)

                def by_channel(src, t):
                    return src.rearrange("(h d) t -> d h t", d=P)[:, :, bass.ds(t * P, P)]

                def load_fk(t, b):
                    if later(t, 2):
                        done(sp, "fm_ok", t - 2, NH, NH)
                        done(sp, "km_ok", t - 2)
                    for dst, src in ((f, hgrn_f), (k, hgrn_k)):
                        sp.dma_start(dst[:, b], by_channel(src, t)).then_inc(fk_in[b], 16)

                def load_qg(t, b):
                    if later(t, 2):
                        done(sp, "qB_ok", t - 2)
                        done(sp, "gg_ok", t - 2)
                    sp.dma_start(q[:, b], by_channel(hgrn_q, t)).then_inc(qg_in[b], 16)
                    sp.dma_start(g[:, b].rearrange("p h c -> p (h c)"), tok[bass.ds(t * P, P), HW:2 * HW]).then_inc(qg_in[b], 16)

                def load_v(t, b):
                    if later(t, 2):
                        done(sp, "o_ps", t - 2)
                    sp.dma_start(v[:, b].rearrange("p h c -> p (h c)"), tok[bass.ds(t * P, P), 0:HW]).then_inc(v_in[b], 16)

                def step(t, b):
                    if has(t + 2):
                        load_fk(t + 2, b)
                    if has(t + 1):
                        load_qg(t + 1, 1 - b)
                    if has(t):
                        load_v(t, b)

                load_fk(0, 0)
                steps(sp, step)

            @block.gpsimd
            def _(pool):
                pool.wait_ge(lb_ok, 5)

                def gates(t, b):
                    loaded(pool, fk_in, t, b, 2)
                    oml = lbs[:, 4].unsqueeze(2).to_broadcast([P, NH, P])
                    if later(t, 2):
                        done(pool, "kB_ok", t - 2)
                        done(pool, "kH_ok", t - 2, len(HALVES), len(HALVES))
                    pool.tensor_tensor(km[:, b], k[:, b], oml, ALU.mult).then_inc(s["km_ok"], 1)

                def differences(t, b):
                    done(pool, "cum_ok", t)
                    for i, H in enumerate(HALVES):
                        if later(t):
                            done(pool, "eH_ok", t - 1, 2 * i + 2, 2 * len(HALVES))
                        a, m = from_middle(cum[:], H, H - 1)
                        pool.tensor_tensor(dH[:, i].rearrange("p h (b t) -> p (h b) t", t=2 * H), a, m, ALU.subtract).then_inc(s["dH_ok"], 1)

                def decays(t, b):
                    for i, H in enumerate(HALVES):
                        done(pool, "eH_ok", t, 2 * i + 2, 2 * len(HALVES))
                        done(pool, "km_ok", t)
                        if later(t, 2):
                            done(pool, "lv_ps", t - 2, LV, LV)
                        pool.tensor_tensor(first_(kl[:, b, 1 + i], H), first_(km[:, b], H), first_(eH[:, i], H), ALU.mult).then_inc(s["kH_ok"], 1)

                def gain_gate(t, b):
                    loaded(pool, qg_in, t, b, 2)
                    if later(t, 2):
                        done(pool, "o_ok", t - 2)
                    pool.tensor_tensor(gg[:, b], g[:, b], gain[:].unsqueeze(1).to_broadcast([P, NH, P]), ALU.mult).then_inc(s["gg_ok"], 1)

                def store(t, b):
                    done(pool, "o_ok", t)
                    pool.dma_start(mix[bass.ds(t * P, P), 0:HW], o[:, b].rearrange("p h c -> p (h c)")).then_inc(stored[b], 16)

                def step(t, b):
                    if has(t + 1):
                        gates(t + 1, 1 - b)
                    if has(t):
                        decays(t, b)
                    if has(t + 1):
                        differences(t + 1, 1 - b)
                    if has(t - 2):
                        store(t - 2, b)
                    if has(t):
                        gain_gate(t, b)

                steps(pool, step)
                for b in range(2):
                    pool.wait_ge(stored[b], 16 * NT // 2)

            @block.scalar
            def _(act):
                act.preload_act_table_set("natural_log_exp_and_others")
                act.wait_ge(lb_ok, 1)
                act.activation(lbs[:, 1], lbs[:, 0], ACT.Exp).then_inc(lb_ok, 1)
                act.wait_ge(init, 1)
                act.wait_ge(lb_ok, 5)

                def forget(t, b):
                    loaded(act, fk_in, t, b, 2)
                    if later(t):
                        done(act, "fl_ok", t - 1)
                    for h in range(NH):
                        act.activation(fm[:, h], f[:, b, h], ACT.Identity, bias=lbs[:, 3, h:h + 1], scale=lbs[:, 4, h:h + 1]) \
                            .then_inc(s["fm_ok"], 1)

                def log_forget(t, b):
                    done(act, "fl_ok", t)
                    if later(t):
                        done(act, "cum_ok", t - 1)
                    act.activation(lf[:], fl[:], ACT.Ln).then_inc(s["lf_ok"], 1)

                def decay_start(t, b):
                    done(act, "cum_ok", t)
                    if later(t):
                        done(act, "kD_ok", t - 1)
                    act.activation(e0[:], cum[:], ACT.Exp).then_inc(s["e0_ok"], 1)

                def decay_end(t, b):
                    done(act, "d64_ok", t)
                    if later(t):
                        done(act, "k0_ok", t - 1)
                    act.activation(eK[:], d64[:], ACT.Exp).then_inc(s["eK_ok"], 1)

                def decay_half(t, b, i):
                    H = HALVES[i]
                    done(act, "dH_ok", t, i + 1, len(HALVES))
                    if later(t):
                        done(act, "qH_ok", t - 1, i + 1, len(HALVES))
                        done(act, "kH_ok", t - 1, i + 1, len(HALVES))
                    act.activation(second(eH[:, i], H), second(dH[:, i], H), ACT.Exp).then_inc(s["eH_ok"], 1)
                    act.activation(first_(eH[:, i], H), first_(dH[:, i], H), ACT.Exp, scale=-1.0).then_inc(s["eH_ok"], 1)

                def decay_base(t, b):
                    done(act, "dB_ok", t)
                    if later(t):
                        done(act, "qB_ok", t - 1)
                        done(act, "kB_ok", t - 1)
                    act.activation(eBq[:], dB[:, b], ACT.Exp).then_inc(s["eB_ok"], 1)
                    act.activation(eBk[:], dB[:, b], ACT.Exp, scale=-1.0).then_inc(s["eB_ok"], 1)
                    done(act, "q0_ok", t)
                    done(act, "k0_ok", t)
                    if later(t, 2):
                        done(act, "o_ps", t - 2)
                        done(act, "kDT_ps", t - 2)
                    act.activation(qI[:, b, :, 0:CH], ql[:, b, 0, :, 0:CH], ACT.Copy).then_inc(s["qIc_ok"], 1)
                    act.activation(kD[:, b, :, CH:P], kl[:, b, 0, :, CH:P], ACT.Copy).then_inc(s["kDc_ok"], 1)

                def take_kD(t, b):
                    done(act, "kDT_ps", t)
                    if later(t, 2):
                        done(act, "upd_ps", t - 2)
                    act.activation(kDT[:, b], psK[:], ACT.Copy).then_inc(s["kDT_ok"], 1)

                def squares(t, b):
                    done(act, "o_ps", t)
                    if later(t):
                        done(act, "oss_ok", t - 1)
                    act.activation(osq[:], psO[b][:], ACT.Square).then_inc(s["osq_ok"], 1)

                def rstd(t, b):
                    done(act, "oss_ok", t)
                    act.activation(oln[:], oss[:], ACT.Ln, bias=eps[:], scale=1.0 / P).then_inc(s["oln_ok"], 1)
                    done(act, "oln_ok", t)
                    if later(t):
                        done(act, "on_ok", t - 1)
                    act.activation(ors[:], oln[:], ACT.Exp, scale=-0.5).then_inc(s["ors_ok"], 1)

                def step(t, b):
                    if has(t):
                        decay_start(t, b)
                    if has(t + 1):
                        forget(t + 1, 1 - b)
                    if has(t - 1):
                        take_kD(t - 1, 1 - b)
                    if has(t):
                        decay_end(t, b)
                    if has(t + 1):
                        log_forget(t + 1, 1 - b)
                    if has(t - 2):
                        squares(t - 2, b)
                    if has(t):
                        for i in range(len(HALVES)):
                            decay_half(t, b, i)
                    if has(t - 2):
                        rstd(t - 2, b)
                    if has(t):
                        decay_base(t, b)

                steps(act, step)

            @block.vector
            def _(dve):
                for x, value in ((eps[:], EPS), (ql[:], 0.0)):
                    dve.memset(x, value).then_inc(init, 1)
                dve.wait_ge(consts_in, 80)
                dve.tensor_tensor(lbs[:, 0], lb_in[:], lb_in[:], ALU.subtract).then_inc(lb_ok, 1)
                dve.wait_ge(lb_ok, 2)
                dve.reciprocal(lbs[:, 2], lbs[:, 1]).then_inc(lb_ok, 1)
                dve.wait_ge(lb_ok, 3)
                dve.tensor_tensor(lbs[:, 2], lbs[:, 1], lbs[:, 2], ALU.mult).then_inc(init, 1)
                dve.wait_ge(init, 3)
                dve.tensor_tensor(lbs[:, 3], lbs[:, 2], lbs[:, 2], ALU.subtract).then_inc(lb_ok, 1)
                dve.wait_ge(lb_ok, 4)
                dve.tensor_scalar(lbs[:, 4], lbs[:, 3], -1.0, 1.0, ALU.mult, ALU.add).then_inc(lb_ok, 1)
                for x in (state[:, 1], kl[:], sT[:]):
                    dve.memset(x, 0.0).then_inc(init, 1)
                dve.wait_ge(init, 6)

                def bound_forget(t, b):
                    done(dve, "fm_ok", t, NH, NH)
                    if later(t):
                        done(dve, "lf_ok", t - 1)
                    dve.tensor_scalar(fl[:], fm[:], MIN_FORGET, None, ALU.max).then_inc(s["fl_ok"], 1)

                def cumulate(t, b):
                    done(dve, "lf_ok", t)
                    if later(t):
                        done(dve, "dH_ok", t - 1, len(HALVES), len(HALVES))
                        done(dve, "e0_ok", t - 1)
                        done(dve, "dB_ok", t - 1)
                    dve.tensor_tensor_scan(cum[:].rearrange("p h t -> p (h t)"), resets[:], lf[:].rearrange("p h t -> p (h t)"),
                                           0.0, ALU.mult, ALU.add).then_inc(s["cum_ok"], 1)
                    done(dve, "cum_ok", t)
                    if later(t):
                        done(dve, "eK_ok", t - 1)
                    a, m = from_middle(cum[:], CH // 2, CH - 1)
                    dve.tensor_tensor(d64[:].rearrange("p h (b t) -> p (h b) t", t=CH), m, a, ALU.subtract).then_inc(s["d64_ok"], 1)
                    if later(t, 2):
                        done(dve, "eB_ok", t - 2, 2, 2)
                    a, m = from_middle(cum[:], 2, 1)
                    dve.tensor_tensor(dB[:, b].rearrange("p h (b t) -> p (h b) t", t=4), a, m, ALU.subtract).then_inc(s["dB_ok"], 1)

                def decay_q(t, b):
                    loaded(dve, qg_in, t, b, 2)
                    done(dve, "e0_ok", t)
                    if later(t, 2):
                        done(dve, "lv_ps", t - 2, LV, LV)
                    dve.tensor_tensor(ql[:, b, 0], q[:, b], e0[:], ALU.mult).then_inc(s["q0_ok"], 1)

                def decay_k(t, b):
                    done(dve, "eK_ok", t)
                    done(dve, "km_ok", t)
                    dve.tensor_tensor(kl[:, b, 0], km[:, b], eK[:], ALU.mult).then_inc(s["k0_ok"], 1)

                def to_and_from_state(t, b):
                    if later(t, 2):
                        done(dve, "state_ok", t - 2)
                        done(dve, "o_ps", t - 2)
                        done(dve, "kDT_ps", t - 2)
                    dve.tensor_tensor(eL[:, b], e0[:, :, CH - 1], e0[:, :, P - 1], ALU.mult).then_inc(s["eL_ok"], 1)
                    done(dve, "q0_ok", t)
                    dve.tensor_tensor(qI[:, b, :, CH:P], ql[:, b, 0, :, CH:P], e0[:, :, CH - 1:CH].to_broadcast([P, NH, CH]), ALU.mult).then_inc(s["qI_ok"], 1)
                    done(dve, "k0_ok", t)
                    dve.tensor_tensor(kD[:, b, :, 0:CH], kl[:, b, 0, :, 0:CH], e0[:, :, P - 1:P].to_broadcast([P, NH, CH]), ALU.mult).then_inc(s["kD_ok"], 1)

                def decay_half(t, b, i):
                    H = HALVES[i]
                    done(dve, "eH_ok", t, 2 * i + 1, 2 * len(HALVES))
                    dve.tensor_tensor(second(ql[:, b, 1 + i], H), second(q[:, b], H), second(eH[:, i], H), ALU.mult).then_inc(s["qH_ok"], 1)

                def decay_base(t, b):
                    done(dve, "eB_ok", t, 2, 2)
                    dve.tensor_tensor(ql[:, b, LV - 1], q[:, b], eBq[:], ALU.mult).then_inc(s["qB_ok"], 1)
                    dve.tensor_tensor(kl[:, b, LV - 1], km[:, b], eBk[:], ALU.mult).then_inc(s["kB_ok"], 1)

                def take_level(t, b, i):
                    if i == 0 and later(t, 2):
                        done(dve, "o_ps", t - 2)
                    if i or later(t):
                        done(dve, "lv_ok", t, i, LV)
                    done(dve, "lv_ps", t, i + 1, LV)
                    dve.copy_predicated(sT[:, b], masks[:, i].unsqueeze(1).to_broadcast([P, NH, P]), psA[i % NA][:]).then_inc(s["lv_ok"], 1)

                def advance(t, b):
                    done(dve, "upd_ps", t)
                    if later(t):
                        done(dve, "o_ps", t - 1)
                    for h in range(NH):
                        last = dve.scalar_tensor_tensor(state[:, b, h], state[:, 1 - b, h], eL[:, b, h:h + 1], psU[:, h],
                                                        ALU.mult, ALU.add)
                    last.then_inc(s["state_ok"], 1)

                def sum_squares(t, b):
                    done(dve, "osq_ok", t)
                    if later(t):
                        done(dve, "oln_ok", t - 1)
                    dve.tensor_reduce(oss[:], osq[:], AX.X, ALU.add).then_inc(s["oss_ok"], 1)

                def normalise(t, b):
                    done(dve, "ors_ok", t)
                    if later(t):
                        done(dve, "o_ok", t - 1)
                    dve.tensor_tensor(on[:], psO[b][:], ors[:].unsqueeze(2).to_broadcast([P, NH, P]), ALU.mult).then_inc(s["on_ok"], 1)

                def gate(t, b):
                    done(dve, "on_ok", t)
                    done(dve, "gg_ok", t)
                    if later(t, 2):
                        dve.wait_ge(stored[b], (t - b) * 8)
                    dve.tensor_tensor(o[:, b], on[:], gg[:, b], ALU.mult).then_inc(s["o_ok"], 1)

                def step(t, b):
                    c = 1 - b
                    if has(t):
                        decay_q(t, b)
                    if has(t + 1):
                        bound_forget(t + 1, c)
                    if has(t):
                        decay_k(t, b)
                    if has(t - 1):
                        take_level(t - 1, c, 0)
                    if has(t):
                        to_and_from_state(t, b)
                    if has(t - 1):
                        take_level(t - 1, c, 1)
                    if has(t + 1):
                        cumulate(t + 1, c)
                    if has(t - 1):
                        take_level(t - 1, c, 2)
                    if has(t - 2):
                        sum_squares(t - 2, b)
                    for i in range(len(HALVES)):
                        if has(t):
                            decay_half(t, b, i)
                        if has(t - 1) and i < 3:
                            take_level(t - 1, c, 3 + i)
                    if has(t - 2):
                        normalise(t - 2, b)
                    if has(t - 1):
                        advance(t - 1, c)
                    if has(t - 2):
                        gate(t - 2, b)
                    if has(t):
                        decay_base(t, b)

                steps(dve, step)

            @block.tensor
            def _(pe):
                pe.wait_ge(consts_in, 80)
                pe.wait_ge(init, 6)

                def tile(t, b):
                    done(pe, "kD_ok", t)
                    done(pe, "kDc_ok", t)
                    if later(t):
                        done(pe, "kDT_ok", t - 1)
                    for h in range(NH):
                        last = pe.transpose(psK[:, h], kD[:, b, h], ident[:])
                    last.then_inc(s["kDT_ps"], 1)
                    for i in range(LV):
                        if i == 0:
                            done(pe, "k0_ok", t)
                        elif i < LV - 1:
                            done(pe, "qH_ok", t, i, len(HALVES))
                            done(pe, "kH_ok", t, i, len(HALVES))
                        else:
                            done(pe, "kB_ok", t)
                        if i >= NA:
                            done(pe, "lv_ok", t, i - NA + 1, LV)
                        elif later(t):
                            done(pe, "lv_ok", t - 1, LV, LV)
                        for h in range(NH):
                            last = pe.matmul(psA[i % NA][:, h], kl[:, b, i, h], ql[:, b, i, h], start=True, stop=True)
                        last.then_inc(s["lv_ps"], 1)
                    done(pe, "kDT_ok", t)
                    if later(t):
                        done(pe, "state_ok", t - 1)
                    at.hold(pe, v_in[b], (t - b + 2) * 8)
                    for h in range(NH):
                        last = pe.matmul(psU[:, h], kDT[:, b, h], v[:, b, h], start=True, stop=True)
                    last.then_inc(s["upd_ps"], 1)
                    done(pe, "lv_ok", t, LV, LV)
                    done(pe, "qI_ok", t)
                    done(pe, "qIc_ok", t)
                    if later(t, 2):
                        done(pe, "on_ok", t - 2)
                    for h in range(NH):
                        pe.matmul(psO[b][:, h], qI[:, b, h], state[:, 1 - b, h], start=True, stop=False)
                        last = pe.matmul(psO[b][:, h], sT[:, b, h], v[:, b, h], start=False, stop=True)
                    last.then_inc(s["o_ps"], 1)

                def step(t, b):
                    if has(t - 1):
                        tile(t - 1, 1 - b)

                steps(pe, step)


HD = 64
CK = 512
LAM_INIT = 0.8 - 0.6 * 1.0


def attention(nc, tok, q_norm, k_norm, lam_q1, lam_k1, lam_q2, lam_k2, subln, ident_in, causal_in, mix):
    units = [[min(CK, (i + 1) * P - j * CK) for j in range(i // 4 + 1)] for i in range(NT)]
    first = [sum(len(u) for u in units[:i]) for i in range(NT)]
    CH = sum(len(u) for u in units)
    NPREP = 2 * 2 * (S // CK)
    with ExitStack() as stack:
        at = Place(nc, stack, "att")
        ident = at.sb("ident", [P, P])
        ident_bf = at.sb("ident_bf", [P, P], BF16)
        causal_f = at.sb("causal_f", [P, P])
        causal = at.sb("causal", [P, P], BF16)
        gcol = at.sb("gcol", [P, 2])
        gain = at.sb("gain", [P, P])
        lam_in = at.sb("lam_in", [P, 4, HD])
        lam_pr = at.sb("lam_pr", [P, 2, HD])
        lam_s = at.sb("lam_s", [P, 4])
        lamvec = at.sb("lamvec", [P, 2])
        eps = at.sb("eps", [P, 1])
        qk = at.sb("qk", [P, 2, NT, P])
        v = at.sb("v", [P, NH, NT, P])
        ms = at.sb("ms", [P, 2, 2 * NT])
        lnm = at.sb("lnm", [P, 2, 2 * NT])
        rs = at.sb("rs", [P, 2, 2 * NT])
        dup = at.sb("dup", [P, 2, NT, 2, 2, HD])
        qs = at.sb("qs", [P, 2, S], F32R)
        khi = at.sb("khi", [P, 2, S], F32R)
        klo = at.sb("klo", [P, 2, S], F32R)
        pr0 = at.sb("pr0", [P, 4, S])
        pr1 = at.sb("pr1", [P, 3, S])
        wT = at.sb("wT", [P, 2, 4, P])
        nm = at.sb("nm", [P, 2, 2, 4])
        sums = at.sb("sums", [P, 2, 2, 4])
        low = at.sb("low", [P, 2])
        dlt = at.sb("dlt", [P, 2, 4])
        ex = at.sb("ex", [P, 2, 4])
        exs = at.sb("exs", [P, 2, 4])
        tot = at.sb("tot", [P, 2])
        inv = at.sb("inv", [P, 2])
        invl = at.sb("invl", [P, 2])
        coef = at.sb("coef", [P, 2, 2, 4])
        o = at.sb("o", [P, NT, P])
        osq = at.sb("osq", [P, 4, P])
        oss = at.sb("oss", [P, 4])
        oln = at.sb("oln", [P, 4])
        ors = at.sb("ors", [P, 4])
        psS = [at.ps(f"psS{i}", (P, 2, CK)) for i in range(2)]
        psW = [at.ps(f"psW{i}") for i in range(2)]
        psO = [at.ps(f"psO{i}") for i in range(2)]

        consts_in = at.sem("consts_in")
        eps_set = at.sem("eps_set")
        mask_ok = at.sem("mask_ok")
        lam_ok = at.sem("lam_ok")
        qk_in = at.sem("qk_in")
        v_in = at.sem("v_in")
        sq_ok = at.sem("sq_ok")
        ms_ok = at.sem("ms_ok")
        lnm_ok = at.sem("lnm_ok")
        rs_ok = at.sem("rs_ok")
        dup_ok = [at.sem("dupq_ok"), at.sem("dupk_ok")]
        prep_ps = at.sem("prep_ps")
        prep_hi = at.sem("prep_hi")
        prep_lo = at.sem("prep_lo")
        score_ps = at.sem("score_ps")
        max_ok = at.sem("max_ok")
        exp_ok = at.sem("exp_ok")
        dl_ok = at.sem("dl_ok")
        ex_ok = at.sem("ex_ok")
        steps = at.sem("steps")
        stat_ok = at.sem("stat_ok")
        scaled = at.sem("scaled")
        comb_ok = at.sem("comb_ok")
        wT_ps = at.sem("wT_ps")
        wT_ok = at.sem("wT_ok")
        pv_ok = at.sem("pv_ok")
        o_ok = at.sem("o_ok")
        osq_ok = at.sem("osq_ok")
        oss_ok = at.sem("oss_ok")
        oln_ok = at.sem("oln_ok")
        ors_ok = at.sem("ors_ok")
        onorm = at.sem("onorm")
        gain_ok = at.sem("gain_ok")
        stored = [at.sem(f"stored{i}") for i in range(NT // 4)]
        STEPS = sum(1 if len(u) == 1 else 5 for u in units)
        HALF = NT // 2

        def later(h, n=1):
            return not isinstance(h, int) or h >= n

        def head_cols(part, h):
            c0 = (2 + part) * HW
            return tok[:, bass.ds(h * P + c0, P)].rearrange("(t p) c -> p t c", p=P)

        def chunks(i):
            return len(units[i]) if 0 <= i < NT else 0

        def upto(i, j):
            return first[i] + min(j + 1, len(units[i]))

        def prep_banks(i, j):
            if i < NT:
                return []
            return [j * 2, j * 2 + 1] if i == NT else [(i - NT + 1) * 4 + j]

        def prep_cut(n):
            return n // (NPREP // 2), n // (NPREP // 4) % 2, n % (S // CK)

        def prep_ps_bank(n):
            return psS[n // 2 % 2][:, n % 2, :]

        with nc.Block() as block:
            @block.sync
            def _(sp):
                def load(h):
                    if later(h):
                        sp.wait_ge(dup_ok[0], h * 2)
                        sp.wait_ge(dup_ok[1], h * 2)
                    for i in range(2):
                        sp.dma_start(qk[:, i], head_cols(i, h)).then_inc(qk_in, 16)

                def store(h, q):
                    at.hold(sp, onorm, (h * (NT // 4) + q + 1) * 2)
                    sp.dma_start(mix[q * 4 * P:(q + 1) * 4 * P, bass.ds(h * P + HW, P)].rearrange("(t p) c -> p t c", p=P),
                                 o[:, q * 4:q * 4 + 4, :]).then_inc(stored[q], 16)

                load(0)
                for dst, src in ((ident, ident_in), (causal_f, causal_in)):
                    sp.dma_start(dst[:], src).then_inc(consts_in, 16)
                for i, g in enumerate((q_norm, k_norm)):
                    for c in range(2):
                        sp.dma_start(gcol[c * HD:(c + 1) * HD, i:i + 1], g.rearrange("a d -> d a"),
                                     allow_slow_non_contiguous=True).then_inc(consts_in, 16)
                for i, l in enumerate((lam_q1, lam_q2, lam_k1, lam_k2)):
                    sp.dma_start(lam_in[:, i, :], l.broadcast_to([P, HD])).then_inc(consts_in, 16)
                sp.dma_start(gain[:], subln.broadcast_to([P, P])).then_inc(consts_in, 16)
                for h in range(NH):
                    sp.dma_start(v[:, h], head_cols(2, h)).then_inc(v_in, 16)
                load(1)

                def head(h, last):
                    if later(h):
                        store(h - 1, NT // 4 - 1)
                    store(h, 0)
                    if not last:
                        load(h + 2)
                    for q in range(1, NT // 4 - 1):
                        store(h, q)

                head(0, False)
                with sp.Fori(1, NH - 2) as h:
                    head(h, False)
                for h in range(NH - 2, NH):
                    head(h, True)
                store(NH - 1, NT // 4 - 1)
                for q in range(NT // 4):
                    sp.wait_ge(stored[q], 16 * NH)

            @block.gpsimd
            def _(pool):
                def normalise_q(h, half):
                    cut = slice(half * HALF, (half + 1) * HALF)
                    pool.wait_ge(qk_in, (h + 1) * 32)
                    pool.wait_ge(rs_ok, h + 1)
                    pool.tensor_tensor(dup[:, 0, cut].rearrange("p t c u d -> p (t c) u d"),
                                       qk[:, 0, cut].rearrange("p t (c d) -> p (t c) d", c=2).unsqueeze(2).to_broadcast([P, NT, 2, HD]),
                                       rs[:, 0, half * NT:(half + 1) * NT].unsqueeze(2).unsqueeze(3).to_broadcast([P, NT, 2, HD]),
                                       ALU.mult).then_inc(dup_ok[0], 1)

                def head(h, last):
                    for i in range(NT):
                        at.hold(pool, stat_ok, h * NT + i + 1)
                        for j, w in enumerate(units[i]):
                            cut = slice(j * CK, j * CK + w)
                            pool.tensor_scalar(pr1[:, i % 3, cut], pr1[:, i % 3, cut], coef[:, i % 2, 1, j:j + 1], None,
                                               ALU.mult).then_inc(scaled, 1)
                        if not last and i in (8, 9):
                            normalise_q(h + 1, i - 8)

                normalise_q(0, 0)
                normalise_q(0, 1)
                head(0, False)
                with pool.Fori(1, NH - 1) as h:
                    head(h, False)
                head(NH - 1, True)

            @block.scalar
            def _(act):
                act.preload_act_table_set("natural_log_exp_and_others")
                act.wait_ge(eps_set, 1)
                act.wait_ge(lam_ok, 2)
                act.activation(lam_s[:, 2:4], lam_s[:, 0:2], ACT.Exp).then_inc(lam_ok, 1)

                def squares(h, n):
                    i, half = n // 2, n % 2
                    act.wait_ge(qk_in, (h + 1) * 32)
                    if later(h) and n == 0:
                        act.wait_ge(prep_ps, h * NPREP)
                    act.activation(dup[:, i, half * HALF:(half + 1) * HALF, 0].rearrange("p t u d -> p t (u d)"),
                                   qk[:, i, half * HALF:(half + 1) * HALF, :], ACT.Square).then_inc(sq_ok, 1)

                def rstd(h):
                    act.wait_ge(ms_ok, h * 4 + 4)
                    act.activation(lnm[:], ms[:], ACT.Ln, bias=eps[:], scale=1.0 / HD).then_inc(lnm_ok, 1)
                    act.wait_ge(lnm_ok, h + 1)
                    act.activation(rs[:], lnm[:], ACT.Exp, scale=-0.5).then_inc(rs_ok, 1)

                def prep_high(h, n):
                    i, c, a = prep_cut(n)
                    act.wait_ge(prep_ps, h * NPREP + n + 1)
                    act.activation((qs, khi)[i][:, c, a * CK:(a + 1) * CK], prep_ps_bank(n), ACT.Copy,
                                   scale=gcol[:, i:i + 1]).then_inc(prep_hi, 1)

                def exponentials(h, i, j):
                    n, w = first[i] + j, units[i][j]
                    act.wait_ge(max_ok, h * CH + n + 1)
                    if i >= 4 or later(h):
                        act.wait_ge(wT_ps, h * CH + (upto(i - 4, j) if i >= 4 else 0))
                    if i >= 3 or later(h):
                        act.wait_ge(comb_ok, h * CH + (upto(i - 3, j) if i >= 3 else 0))
                    if i >= 2 or later(h):
                        act.wait_ge(stat_ok, h * NT + i - 1)
                    for c, dst in enumerate((pr0[:, i % 4], pr1[:, i % 3])):
                        act.activation(dst[:, j * CK:j * CK + w], psS[n % 2][:, c, 0:w], ACT.Exp,
                                       bias=nm[:, i % 2, c, j:j + 1],
                                       accum_out=sums[:, i % 2, c, j:j + 1]).then_inc(exp_ok, 1)

                def take_weights(h, i, j):
                    n, w = first[i] + j, units[i][j]
                    act.wait_ge(wT_ps, h * CH + n + 1)
                    if n >= 2 or later(h):
                        act.wait_ge(pv_ok, h * CH + n - 1)
                    act.activation(wT[:, n % 2, 0:w // P, :], psW[n % 2][:, 0:w].rearrange("p (k q) -> p k q", q=P),
                                   ACT.Copy).then_inc(wT_ok, 1)

                def head(h, last):
                    for i in range(NT + 3):
                        if i >= 1 and chunks(i - 1) > 1:
                            nj = chunks(i - 1)
                            act.wait_ge(dl_ok, h * (NT - 4) + i - 4)
                            act.activation(ex[:, :, 0:nj], dlt[:, :, 0:nj], ACT.Exp).then_inc(ex_ok, 1)
                        for j in range(4):
                            if j < chunks(i - 3):
                                take_weights(h, i - 3, j)
                            if j < chunks(i):
                                exponentials(h, i, j)
                            for n in prep_banks(i, j) if not last else []:
                                prep_high(h + 1, n)
                        if i >= 3:
                            act.wait_ge(pv_ok, h * CH + upto(i - 3, 4))
                            if (i - 3) % 4 == 0 and later(h):
                                act.wait_ge(stored[(i - 3) // 4], h * 16)
                            act.activation(o[:, i - 3, :], psO[(i - 3) % 2][:, 0:P], ACT.Copy).then_inc(o_ok, 1)
                        if not last:
                            if 3 <= i < 7:
                                squares(h + 1, i - 3)
                            if i == 8:
                                rstd(h + 1)
                        if i % 4 == 2 and i < NT and (i >= 6 or later(h)):
                            out_squares(h, (i - 6) // 4)
                        if i % 4 == 0 and i >= 4 and (i >= 8 or later(h)):
                            out_rstd(h, (i - 8) // 4)

                def out_squares(h, q):
                    m, u = h * (NT // 4) + q, q % (NT // 4) * 4
                    act.wait_ge(o_ok, m * 4 + 4)
                    if later(m):
                        act.wait_ge(oss_ok, m)
                    act.activation(osq[:], o[:, u:u + 4, :], ACT.Square).then_inc(osq_ok, 1)

                def out_rstd(h, q):
                    m = h * (NT // 4) + q
                    act.wait_ge(oss_ok, m + 1)
                    act.activation(oln[:], oss[:], ACT.Ln, bias=eps[:], scale=1.0 / P).then_inc(oln_ok, 1)
                    act.wait_ge(oln_ok, m + 1)
                    if later(m):
                        act.wait_ge(onorm, m * 2)
                    act.activation(ors[:], oln[:], ACT.Exp, scale=-0.5).then_inc(ors_ok, 1)

                for n in range(4):
                    squares(0, n)
                rstd(0)
                for n in range(NPREP):
                    prep_high(0, n)
                head(0, False)
                with act.Fori(1, NH - 1) as h:
                    head(h, False)
                head(NH - 1, True)
                out_squares(NH, -1)
                out_rstd(NH, -1)

            @block.vector
            def _(dve):
                dve.memset(eps[:], EPS).then_inc(eps_set, 1)
                dve.wait_ge(consts_in, 16 * 11)
                dve.tensor_copy(ident_bf[:], ident[:]).then_inc(mask_ok, 1)
                dve.tensor_copy(causal[:], causal_f[:]).then_inc(mask_ok, 1)
                dve.tensor_scalar(gcol[:, 0:1], gcol[:, 0:1], HD ** -0.5, None, ALU.mult).then_inc(gain_ok, 1)
                dve.tensor_scalar(gain[:], gain[:], 1.0 - LAM_INIT, None, ALU.mult).then_inc(gain_ok, 1)
                dve.tensor_tensor(lam_pr[:], lam_in[:, 0:2], lam_in[:, 2:4], ALU.mult).then_inc(lam_ok, 1)
                dve.wait_ge(lam_ok, 1)
                dve.tensor_reduce(lam_s[:, 0:2], lam_pr[:], AX.X, ALU.add).then_inc(lam_ok, 1)
                dve.memset(lamvec[:, 0:1], 1.0).then_inc(gain_ok, 1)
                dve.wait_ge(lam_ok, 3)
                dve.scalar_tensor_tensor(lamvec[:, 1:2], lam_s[:, 3:4], LAM_INIT, lam_s[:, 2:3],
                                         ALU.subtract, ALU.subtract).then_inc(gain_ok, 1)
                dve.wait_ge(gain_ok, 4)

                def means(h, n):
                    i, half = n // 2, n % 2
                    dve.wait_ge(sq_ok, h * 4 + n + 1)
                    src = dup[:, i, half * HALF:(half + 1) * HALF, 0].rearrange("p t u d -> p t u d")
                    dve.tensor_reduce(ms[:, i, half * NT:(half + 1) * NT].rearrange("p (t c) -> p t c", c=2), src,
                                      AX.X, ALU.add).then_inc(ms_ok, 1)

                def normalise_k(h, half):
                    cut = slice(half * HALF, (half + 1) * HALF)
                    dve.wait_ge(qk_in, (h + 1) * 32)
                    dve.wait_ge(rs_ok, h + 1)
                    dve.tensor_tensor(dup[:, 1, cut].rearrange("p t c u d -> p (t c) u d"),
                                      qk[:, 1, cut].rearrange("p t (c d) -> p (t c) d", c=2).unsqueeze(2).to_broadcast([P, NT, 2, HD]),
                                      rs[:, 1, half * NT:(half + 1) * NT].unsqueeze(2).unsqueeze(3).to_broadcast([P, NT, 2, HD]),
                                      ALU.mult).then_inc(dup_ok[1], 1)

                def prep_low(h, n):
                    i, c, a = prep_cut(n)
                    dve.wait_ge(prep_hi, h * NPREP + n + 1)
                    cut = slice(a * CK, (a + 1) * CK)
                    lo, hi, r = ((qs, qs), (klo, khi))[i] + (slice(HD, P) if i == 0 else slice(0, P),)
                    dve.scalar_tensor_tensor(lo[r, c, cut], prep_ps_bank(n)[r, :], gcol[r, i:i + 1], hi[r, c, cut].bitcast(F32),
                                             ALU.mult, ALU.subtract).then_inc(prep_lo, 1)

                def maxima(h, i, j):
                    n, w = first[i] + j, units[i][j]
                    dve.wait_ge(score_ps, h * CH + n + 1)
                    dve.tensor_reduce(nm[:, i % 2, :, j:j + 1], psS[n % 2][:, :, 0:w], AX.X, ALU.max,
                                      negate=True).then_inc(max_ok, 1)

                def differences(h, i):
                    nj = chunks(i)
                    dve.wait_ge(max_ok, h * CH + first[i] + nj)
                    own(h, dve.tensor_reduce(low[:], nm[:, i % 2, :, 0:nj], AX.X, ALU.min))
                    dve.tensor_tensor(dlt[:, :, 0:nj], low[:].unsqueeze(2).to_broadcast([P, 2, nj]), nm[:, i % 2, :, 0:nj],
                                      ALU.subtract).then_inc(dl_ok, 1)

                def coefficients(h, i):
                    nj, u = chunks(i), i % 2
                    if i or later(h):
                        dve.wait_ge(stat_ok, h * NT + i)
                    if nj > 1:
                        dve.wait_ge(ex_ok, h * (NT - 4) + i - 3)
                        dve.wait_ge(exp_ok, (h * CH + upto(i, 4)) * 2)
                        own(h, dve.tensor_tensor(exs[:, :, 0:nj], ex[:, :, 0:nj], sums[:, u, :, 0:nj], ALU.mult))
                        own(h, dve.tensor_reduce(tot[:], exs[:, :, 0:nj], AX.X, ALU.add))
                        own(h, dve.reciprocal(inv[:], tot[:]))
                        own(h, dve.tensor_tensor(invl[:], inv[:], lamvec[:], ALU.mult))
                        dve.tensor_tensor(coef[:, u, :, 0:nj], ex[:, :, 0:nj],
                                          invl[:].unsqueeze(2).to_broadcast([P, 2, nj]), ALU.mult).then_inc(stat_ok, 1)
                    else:
                        dve.wait_ge(exp_ok, (h * CH + upto(i, 4)) * 2)
                        own(h, dve.reciprocal(inv[:], sums[:, u, :, 0]))
                        dve.tensor_tensor(coef[:, u, :, 0], inv[:], lamvec[:], ALU.mult).then_inc(stat_ok, 1)

                def combine(h, i, j):
                    w = units[i][j]
                    cut = slice(j * CK, j * CK + w)
                    dve.wait_ge(stat_ok, h * NT + i + 1)
                    dve.wait_ge(scaled, h * CH + first[i] + j + 1)
                    dve.scalar_tensor_tensor(pr0[:, i % 4, cut], pr0[:, i % 4, cut], coef[:, i % 2, 0, j:j + 1], pr1[:, i % 3, cut],
                                             ALU.mult, ALU.add).then_inc(comb_ok, 1)

                def out_sums(h, q):
                    m = h * (NT // 4) + q
                    dve.wait_ge(osq_ok, m + 1)
                    if later(m):
                        dve.wait_ge(oln_ok, m)
                    dve.tensor_reduce(oss[:], osq[:], AX.X, ALU.add).then_inc(oss_ok, 1)

                def out_norm(h, q):
                    m, u = h * (NT // 4) + q, q % (NT // 4) * 4
                    dve.wait_ge(ors_ok, m + 1)
                    dve.tensor_tensor(o[:, u:u + 4, :], o[:, u:u + 4, :], ors[:].unsqueeze(2).to_broadcast([P, 4, P]),
                                      ALU.mult).then_inc(onorm, 1)
                    dve.wait_ge(onorm, m * 2 + 1)
                    dve.tensor_tensor(o[:, u:u + 4, :], o[:, u:u + 4, :], gain[:].unsqueeze(1).to_broadcast([P, 4, P]),
                                      ALU.mult).then_inc(onorm, 1)

                step = [0]

                def own(h, ins):
                    step[0] += 1
                    ins.then_inc(steps, 1)
                    dve.wait_ge(steps, h * STEPS + step[0])

                def head(h, last):
                    step[0] = 0
                    for i in range(NT + 3):
                        if i < NT:
                            maxima(h, i, 0)
                        if 1 <= i <= NT:
                            coefficients(h, i - 1)
                        for j in range(4):
                            if j + 1 < chunks(i):
                                maxima(h, i, j + 1)
                            for n in prep_banks(i, j) if not last else []:
                                prep_low(h + 1, n)
                            if j < chunks(i - 2):
                                combine(h, i - 2, j)
                        if chunks(i) > 1:
                            differences(h, i)
                        if not last:
                            if 4 <= i < 8:
                                means(h + 1, i - 4)
                            if i in (9, 11):
                                normalise_k(h + 1, (i - 9) // 2)
                        if i % 4 == 3 and i < NT and (i >= 7 or later(h)):
                            out_sums(h, (i - 7) // 4)
                        if i % 4 == 1 and i >= 5 and (i >= 9 or later(h)):
                            out_norm(h, (i - 9) // 4)

                for n in range(4):
                    means(0, n)
                normalise_k(0, 0)
                normalise_k(0, 1)
                for n in range(NPREP):
                    prep_low(0, n)
                head(0, False)
                with dve.Fori(1, NH - 1) as h:
                    head(h, False)
                head(NH - 1, True)
                out_sums(NH, -1)
                out_norm(NH, -1)

            @block.tensor
            def _(pe):
                pe.wait_ge(consts_in, 16 * 11)
                pe.wait_ge(mask_ok, 2)

                def prepare(h, n):
                    i, c, a = prep_cut(n)
                    pe.wait_ge(dup_ok[i], h * 2 + 1 + a // 2)
                    if n >= 4:
                        pe.wait_ge(prep_lo, h * NPREP + n - 3)
                    elif later(h):
                        pe.wait_ge(exp_ok, h * CH * 2)
                    for k in range(4):
                        last = pe.transpose(prep_ps_bank(n)[:, k * P:(k + 1) * P],
                                            dup[:, i, a * 4 + k, c].rearrange("p u d -> p (u d)"), ident[:])
                    last.then_inc(prep_ps, 1)

                def scores(h, i, j):
                    n, w = first[i] + j, units[i][j]
                    if i == 0:
                        pe.wait_ge(prep_lo, (h + 1) * NPREP)
                    if n >= 2:
                        pe.wait_ge(exp_ok, (h * CH + n - 1) * 2)
                    diag = j == len(units[i]) - 1
                    for c in range(2):
                        out = psS[n % 2][:, c, 0:w]
                        q = qs[:, c, i * P:(i + 1) * P]
                        pe.matmul(out, q, khi[:, c, j * CK:j * CK + w], start=True, stop=False)
                        last = pe.matmul(out, q, klo[:, c, j * CK:j * CK + w], start=False, stop=not diag)
                        if diag:
                            last = pe.matmul(psS[n % 2][:, c, w - P:w], ident_bf[:], causal[:], start=False, stop=True)
                    last.then_inc(score_ps, 1)

                def turn_weights(h, i, j):
                    n, w = first[i] + j, units[i][j]
                    pe.wait_ge(comb_ok, h * CH + n + 1)
                    if n >= 2 or later(h):
                        pe.wait_ge(wT_ok, h * CH + n - 1)
                    for k in range(w // P):
                        last = pe.transpose(psW[n % 2][:, k * P:(k + 1) * P],
                                            pr0[:, i % 4, j * CK + k * P:j * CK + (k + 1) * P], ident[:])
                    last.then_inc(wT_ps, 1)

                def times_values(h, i, j):
                    n = first[i] + j
                    pe.wait_ge(wT_ok, h * CH + n + 1)
                    if j == 0 and (i >= 2 or later(h)):
                        pe.wait_ge(o_ok, h * NT + i - 1)
                    for k in range(units[i][j] // P):
                        t = j * 4 + k
                        last = pe.matmul(psO[i % 2][:, 0:P], wT[:, n % 2, k, :], v[:, bass.ds(h, 1), t, :].rearrange("p a c -> p (a c)"),
                                         start=(t == 0), stop=(t == i))
                    last.then_inc(pv_ok, 1)

                def head(h, last):
                    for i in range(NT + 3):
                        for j in range(4):
                            if j < chunks(i):
                                scores(h, i, j)
                            for n in prep_banks(i, j) if not last else []:
                                prepare(h + 1, n)
                            if j < chunks(i - 3):
                                turn_weights(h, i - 3, j)
                            if 1 <= j and j - 1 < chunks(i - 3):
                                times_values(h, i - 3, j - 1)
                        if chunks(i - 3) == 4:
                            times_values(h, i - 3, 3)

                for n in range(NPREP):
                    prepare(0, n)
                pe.wait_ge(v_in, 16 * NH)
                head(0, False)
                with pe.Fori(1, NH - 1) as h:
                    head(h, False)
                head(NH - 1, True)


NE = 16
NGR = 4
GE = NE // NGR
HALF = D // 2


def project_out(nc, mix, x, w_out, ffn_norm, w_router, ident_in, h1, xn_rows, logits):
    NS = 4
    with ExitStack() as stack:
        at = Place(nc, stack, "out")
        ident = at.sb("ident", [P, P])
        gain = at.sb("gain", [P, D])
        eps = at.sb("eps", [P, 1])
        wraw = at.sb("wraw", [P, NS, D])
        whi = at.sb("whi", [P, KD, D], F32R)
        wlo = at.sb("wlo", [P, KD, D], F32R)
        wr = at.sb("wr", [P, KD, NE])
        m = at.sb("m", [P, NS, D])
        h = at.sb("h", [P, NS, D])
        mhi = at.sb("mhi", [P, 2, KD, P], F32R)
        mlo = at.sb("mlo", [P, 2, KD, P], F32R)
        sq = at.sb("sq", [P, D])
        ss, lnm, rs = (at.sb(n, [P, 2]) for n in ("ss", "lnm", "rs"))
        xn = at.sb("xn", [P, NS, D])
        xT = at.sb("xT", [P, KD, P])
        lg = at.sb("lg", [P, NT, NE])
        zero = at.sb("zero", [1, D])
        psT = [at.ps(f"psT{i}", (P, 4, P)) for i in range(2)]
        psM = at.ps("psM", (P, 2, HALF))
        psR = [at.ps(f"psR{i}", (P, 4, P)) for i in range(2)]
        psL = at.ps("psL")

        consts_in, gain_in, zero_ok, zero_out, eps_set = (at.sem(n) for n in ("consts_in", "gain_in", "zero_ok", "zero_out", "eps_set"))
        w_in = [at.sem(f"w_in{i}") for i in range(NS)]
        whi_ok, wlo_ok = at.sem("whi_ok"), at.sem("wlo_ok")
        m_in, x_in, h_out, n_out = ([at.sem(f"{n}{i}") for i in range(NS)] for n in ("m_in", "x_in", "h_out", "n_out"))
        mT_ps = at.sem("mT_ps")
        mhi_ok, mlo_ok = at.sem("mhi_ok"), at.sem("mlo_ok")
        mm_ok = at.sem("mm_ok")
        h_ok = at.sem("h_ok")
        sq_ok, lnm_ok, rs_ok = at.sem("sq_ok"), at.sem("lnm_ok"), at.sem("rs_ok")
        xn_ok = at.sem("xn_ok")
        xT_ps = at.sem("xT_ps")
        xT_ok = at.sem("xT_ok")
        lg_ps = at.sem("lg_ps")
        lg_ok = at.sem("lg_ok")
        lg_out = at.sem("lg_out")

        def later(t, n=1):
            return not isinstance(t, int) or t >= n

        def inside(t):
            return not isinstance(t, int) or t < NT

        def used(t, u):
            return (t - u % NS + NS) * (16 // NS)

        def steps(eng, body):
            for u in range(4):
                body(u, u)
            with eng.Fori(1, NT // 4 - 1) as g:
                for u in range(4):
                    body(g * 4 + u, u)
            for u in range(4):
                body(NT - 4 + u, u)

        with nc.Block() as block:
            @block.sync
            def _(sp):
                sp.dma_start(ident[:], ident_in).then_inc(consts_in, 16)

                def load(t, u):
                    v = u % NS
                    if later(t, NS):
                        at.hold(sp, mT_ps, (t - NS + 1) * 2)
                    sp.dma_start(m[:, v], mix[bass.ds(t * P, P), :]).then_inc(m_in[v], 16)
                    if later(t, NS):
                        at.hold(sp, h_out[v], used(t - NS, v))
                        at.hold(sp, xn_ok, t - NS + 1)
                    sp.dma_start(h[:, v], x[bass.ds(t * P, P), :]).then_inc(x_in[v], 16)

                load(0, 0)
                for k in range(KD):
                    if k >= NS:
                        sp.wait_ge(whi_ok, k - NS + 1)
                        sp.wait_ge(wlo_ok, k - NS + 1)
                    sp.dma_start(wraw[:, k % NS], w_out[k * P:(k + 1) * P, :]).then_inc(w_in[k % NS], 16)
                    if k == 3:
                        load(1, 1)
                sp.dma_start(gain[:], ffn_norm.broadcast_to([P, D])).then_inc(gain_in, 16)
                sp.dma_start(wr[:], w_router.rearrange("(k p) e -> p k e", p=P)).then_inc(gain_in, 16)
                load(2, 2)

                def step(t, u):
                    v = u % NS
                    if inside(t + 3):
                        load(t + 3, u + 3)
                    at.hold(sp, h_ok, t + 1)
                    sp.dma_start(h1[bass.ds(t * P, P), :], h[:, v]).then_inc(h_out[v], 16)
                    at.hold(sp, xn_ok, t + 1)
                    sp.dma_start(xn_rows[bass.ds(t * P, P), :], xn[:, v]).then_inc(n_out[v], 16)

                steps(sp, step)
                sp.wait_ge(lg_ok, NT)
                sp.dma_start(logits, lg[:].rearrange("p t e -> p (t e)")).then_inc(lg_out, 16)
                sp.wait_ge(lg_out, 16)
                for v in range(NS):
                    sp.wait_ge(h_out[v], NT // NS * 16)
                    sp.wait_ge(n_out[v], NT // NS * 16)

            @block.gpsimd
            def _(pool):
                pool.memset(zero[:], 0.0).then_inc(zero_ok, 1)
                pool.wait_ge(zero_ok, 1)
                pool.dma_start(xn_rows[S:S + 1, :], zero[:]).then_inc(zero_out, 16)
                pool.wait_ge(zero_out, 16)

            @block.scalar
            def _(act):
                act.preload_act_table_set("natural_log_exp_and_others")

                def split_w(k):
                    act.wait_ge(w_in[k % NS], 16 * (k // NS + 1))
                    act.activation(whi[:, k], wraw[:, k % NS], ACT.Copy).then_inc(whi_ok, 1)

                def front(t, u):
                    b = u % 2
                    if later(t, 2):
                        act.wait_ge(mm_ok, t - 1)
                    for i in range(2):
                        act.wait_ge(mT_ps, t * 2 + i + 1)
                        act.activation(mhi[:, b, i * 4:(i + 1) * 4], psT[i][:], ACT.Copy).then_inc(mhi_ok, 1)

                def take_xT(t):
                    if later(t):
                        act.wait_ge(lg_ps, t)
                    for i in range(2):
                        act.wait_ge(xT_ps, t * 2 + i + 1)
                        act.activation(xT[:, i * 4:(i + 1) * 4], psR[i][:], ACT.Copy).then_inc(xT_ok, 1)

                def step(t, u):
                    b, v = u % 2, u % NS
                    if inside(t + 1):
                        front(t + 1, u + 1)
                    if later(t):
                        take_xT(t - 1)
                    act.wait_ge(h_ok, t + 1)
                    if later(t):
                        act.wait_ge(sq_ok, t)
                    if later(t, 2):
                        act.wait_ge(xn_ok, t - 1)
                    act.activation(sq[:], h[:, v], ACT.Square, accum_out=ss[:, b:b + 1]).then_inc(sq_ok, 1)
                    act.wait_ge(sq_ok, t + 1)
                    act.activation(lnm[:, b:b + 1], ss[:, b:b + 1], ACT.Ln, bias=eps[:], scale=1.0 / D).then_inc(lnm_ok, 1)
                    act.wait_ge(lnm_ok, t + 1)
                    act.activation(rs[:, b:b + 1], lnm[:, b:b + 1], ACT.Exp, scale=-0.5).then_inc(rs_ok, 1)

                act.wait_ge(eps_set, 1)
                front(0, 0)
                for k in range(KD):
                    split_w(k)
                steps(act, step)
                take_xT(NT - 1)

            @block.vector
            def _(dve):
                dve.memset(eps[:], EPS).then_inc(eps_set, 1)

                def split_w(k):
                    dve.wait_ge(whi_ok, k + 1)
                    dve.tensor_tensor(wlo[:, k], wraw[:, k % NS], whi[:, k].bitcast(F32), ALU.subtract).then_inc(wlo_ok, 1)

                def front(t, u):
                    b = u % 2
                    for i in range(2):
                        dve.wait_ge(mhi_ok, t * 2 + i + 1)
                        dve.tensor_tensor(mlo[:, b, i * 4:(i + 1) * 4], psT[i][:], mhi[:, b, i * 4:(i + 1) * 4].bitcast(F32),
                                          ALU.subtract).then_inc(mlo_ok, 1)

                def take_logits(t):
                    dve.wait_ge(lg_ps, t + 1)
                    dve.tensor_copy(lg[:, bass.ds(t, 1), :], psL[:, 0:NE].unsqueeze(1)).then_inc(lg_ok, 1)

                def step(t, u):
                    b, v = u % 2, u % NS
                    if inside(t + 1):
                        front(t + 1, u + 1)
                    dve.wait_ge(mm_ok, t + 1)
                    dve.wait_ge(x_in[v], used(t, u))
                    dve.tensor_tensor(h[:, v], psM[:].rearrange("p a n -> p (a n)"), h[:, v], ALU.add).then_inc(h_ok, 1)
                    if later(t):
                        take_logits(t - 1)
                    dve.wait_ge(rs_ok, t + 1)
                    if later(t, NS):
                        dve.wait_ge(n_out[v], used(t - NS, v))
                    dve.scalar_tensor_tensor(xn[:, v], h[:, v], rs[:, b:b + 1], gain[:], ALU.mult, ALU.mult).then_inc(xn_ok, 1)

                front(0, 0)
                for k in range(KD):
                    split_w(k)
                dve.wait_ge(gain_in, 32)
                steps(dve, step)
                take_logits(NT - 1)

            @block.tensor
            def _(pe):
                pe.wait_ge(consts_in, 16)

                def front(t, u):
                    pe.wait_ge(m_in[u % NS], used(t, u))
                    for i in range(2):
                        if later(t):
                            pe.wait_ge(mlo_ok, t * 2 - 1 + i)
                        for j in range(4):
                            last = pe.transpose(psT[i][:, j], m[:, u % NS, (i * 4 + j) * P:(i * 4 + j + 1) * P], ident[:])
                        last.then_inc(mT_ps, 1)

                def product(t, u, n, k):
                    b, cut = u % 2, slice(n * HALF, (n + 1) * HALF)
                    for i, (l, r) in enumerate(((mhi, whi), (mhi, wlo), (mlo, whi))):
                        last = pe.matmul(psM[:, n], l[:, b, k], r[:, k, cut], start=(k == 0 and i == 0), stop=(k == KD - 1 and i == 2))
                    return last

                def turn_xn(t, u):
                    pe.wait_ge(xn_ok, t + 1)
                    if not later(t):
                        pe.wait_ge(gain_in, 32)
                    else:
                        pe.wait_ge(xT_ok, t * 2)
                    for i in range(2):
                        for j in range(4):
                            last = pe.transpose(psR[i][:, j], xn[:, u % NS, (i * 4 + j) * P:(i * 4 + j + 1) * P], ident[:])
                        last.then_inc(xT_ps, 1)

                def router(t):
                    pe.wait_ge(xT_ok, t * 2 + 2)
                    if later(t):
                        pe.wait_ge(lg_ok, t)
                    for k in range(KD):
                        last = pe.matmul(psL[:, 0:NE], xT[:, k], wr[:, k], start=(k == 0), stop=(k == KD - 1))
                    last.then_inc(lg_ps, 1)

                def step(t, u):
                    if inside(t + 1):
                        front(t + 1, u + 1)
                    pe.wait_ge(mlo_ok, t * 2 + 2)
                    if later(t):
                        pe.wait_ge(h_ok, t)
                        for n in range(2):
                            for k in range(KD):
                                last = product(t, u, n, k)
                            if n == 0:
                                turn_xn(t - 1, u + 3)
                        last.then_inc(mm_ok, 1)
                        router(t - 1)
                    else:
                        for k in range(KD):
                            pe.wait_ge(wlo_ok, k + 1)
                            for n in range(2):
                                last = product(t, u, n, k)
                        last.then_inc(mm_ok, 1)

                front(0, 0)
                steps(pe, step)
                turn_xn(NT - 1, NT - 1)
                router(NT - 1)


NB = 2 * S // P + NE - 1
NROW = NB * P


def route(nc, logits, below_in, upper_in, firsts_in, blocks_in, row_tok, dest_out, wgt_out, plan_out):
    with ExitStack() as stack:
        at = Place(nc, stack, "route")
        NG2 = NT * NGR
        lg = at.sb("lg", [P, NT, NE])
        below = at.sb("below", [P, GE, GE])
        upper = at.sb("upper", [P, 2, P])
        firsts = at.sb("firsts", [P, NE, NT])
        blocks = at.sb("blocks", [P, NB])
        pad = at.sb("pad", [P, NB], I32)
        mx, sm, inv = (at.sb(n, [P, NT]) for n in ("mx", "sm", "inv"))
        aff, tmp, first, second, sel, pre, dst = (at.sb(n, [P, NT, NE]) for n in ("aff", "tmp", "first", "second", "sel", "pre", "dst"))
        cmp1, cmp2 = (at.sb(n, [P, NG2, GE, GE]) for n in ("cmp1", "cmp2"))
        rank = at.sb("rank", [P, NG2, GE])
        gs = at.sb("gs", [P, NT, NGR])
        grank, gtop = at.sb("grank", [P, NT, NGR]), at.sb("gtop", [P, NT, NGR])
        totT, incl, excl = (at.sb(n, [P, NE, NT]) for n in ("totT", "incl", "excl"))
        cnt_i, nb_i, ends_i = (at.sb(n, [P, NE], I32) for n in ("cnt_i", "nb_i", "ends_i"))
        cnt, nb, ends, starts, ones = (at.sb(n, [P, NE]) for n in ("cnt", "nb", "ends", "starts", "ones"))
        dest_f = at.sb("dest_f", [P, 2, NT])
        dest = at.sb("dest", [P, 2, NT], I32)
        wgt = at.sb("wgt", [P, 2, NT])
        over = at.sb("over", [P, NB, NE])
        be = at.sb("be", [P, NB])
        plan = at.sb("plan", [P, 2 * NB + NE], I32)
        ps = at.ps("ps")
        consts_in, lg_in, pad_out, out = (at.sem(n) for n in ("consts_in", "lg_in", "pad_out", "out"))
        step, exp_ok, tok_ok, count_ps, dest_ok, plan_ok, pad_ok = (at.sem(n) for n in ("step", "exp_ok", "tok_ok", "count_ps", "dest_ok", "plan_ok", "pad_ok"))

        def over_last(x, n):
            return x.unsqueeze(len(x.shape)).to_broadcast([*x.shape, n])

        with nc.Block() as block:
            @block.sync
            def _(sp):
                sp.dma_start(lg[:].rearrange("p t e -> p (t e)"), logits).then_inc(lg_in, 16)
                for dst_, src in ((below, below_in), (upper, upper_in), (firsts, firsts_in), (blocks, blocks_in)):
                    sp.dma_start(dst_[:], src).then_inc(consts_in, 16)
                sp.wait_ge(pad_ok, 1)
                sp.dma_start(row_tok.rearrange("(p b) o -> p (b o)", p=P), pad[:]).then_inc(pad_out, 16)
                sp.wait_ge(plan_ok, 1)
                sp.dma_start(dest_out, dest[:].rearrange("p a t -> p (a t)")).then_inc(out, 16)
                sp.dma_start(wgt_out, wgt[:].rearrange("p a t -> p (a t)")).then_inc(out, 16)
                sp.dma_start(plan_out, plan[:]).then_inc(out, 16)
                sp.wait_ge(out, 48)
                sp.wait_ge(pad_out, 16)

            @block.scalar
            def _(act):
                act.wait_ge(exp_ok, 1)
                act.activation(aff[:], tmp[:], ACT.Exp).then_inc(exp_ok, 1)

            @block.tensor
            def _(pe):
                pe.wait_ge(consts_in, 64)
                pe.wait_ge(tok_ok, 1)
                for i in range(2):
                    last = pe.matmul(ps[:, i * 256:(i + 1) * 256], upper[:, i], sel[:].rearrange("p t e -> p (t e)"), start=True, stop=True)
                last.then_inc(count_ps, 1)

            @block.gpsimd
            def _(pool):
                pool.memset(pad[:], S).then_inc(pad_ok, 1)

            @block.vector
            def _(dve):
                count = [0]

                def link(ins):
                    count[0] += 1
                    ins.then_inc(step, 1)
                    dve.wait_ge(step, count[0])

                dve.wait_ge(lg_in, 16)
                dve.wait_ge(consts_in, 64)
                TT, TS = dve.tensor_tensor, dve.tensor_scalar
                link(dve.tensor_reduce(mx[:], lg[:], AX.X, ALU.max))
                TT(tmp[:], lg[:], over_last(mx[:], NE), ALU.subtract).then_inc(exp_ok, 1)
                dve.wait_ge(exp_ok, 2)
                link(dve.tensor_reduce(sm[:], aff[:], AX.X, ALU.add))
                link(dve.reciprocal(inv[:], sm[:]))
                link(TT(aff[:], aff[:], over_last(inv[:], NE), ALU.mult))

                def ranks(x, out_, n):
                    e, j = over_last(x, n), x.unsqueeze(2).to_broadcast([P, x.shape[1], n, n])
                    c1, c2 = cmp1[:, 0:x.shape[1]], cmp2[:, 0:x.shape[1]]
                    link(TT(c1, j, e, ALU.is_equal))
                    link(TT(c1, c1, below[:].unsqueeze(1).to_broadcast([P, x.shape[1], n, n]), ALU.mult))
                    link(TT(c2, j, e, ALU.is_gt))
                    link(TT(c1, c1, c2, ALU.add))
                    link(dve.tensor_reduce(out_, c1, AX.X, ALU.add))

                def by_group(x):
                    return x.rearrange("p t (g e) -> p (t g) e", e=GE)

                ranks(by_group(aff[:]), rank[:], GE)
                link(TS(by_group(tmp[:]), rank[:], 1.5, None, ALU.is_lt))
                link(TT(tmp[:], aff[:], tmp[:], ALU.mult))
                link(dve.tensor_reduce(gs[:].rearrange("p t g -> p (t g)"), by_group(tmp[:]), AX.X, ALU.add))
                ranks(gs[:], grank[:], NGR)
                link(TS(gtop[:], grank[:], 0.5, None, ALU.is_lt))
                top = over_last(gtop[:].rearrange("p t g -> p (t g)"), GE)
                link(TS(by_group(first[:]), rank[:], 0.5, None, ALU.is_lt))
                link(TT(by_group(first[:]), by_group(first[:]), top, ALU.mult))
                link(TS(by_group(second[:]), rank[:], 1.0, None, ALU.is_equal))
                link(TT(by_group(second[:]), by_group(second[:]), top, ALU.mult))
                TT(sel[:], first[:], second[:], ALU.add).then_inc(tok_ok, 1)
                dve.wait_ge(tok_ok, 1)
                for a, x in enumerate((first, second)):
                    link(TT(tmp[:], aff[:], x[:], ALU.mult))
                    link(dve.tensor_reduce(wgt[:, a], tmp[:], AX.X, ALU.add))
                link(TT(sm[:], wgt[:, 0], wgt[:, 1], ALU.add))
                link(dve.reciprocal(inv[:], sm[:]))
                link(TT(wgt[:], wgt[:], inv[:].unsqueeze(1).to_broadcast([P, 2, NT]), ALU.mult))
                dve.wait_ge(count_ps, 1)
                link(dve.tensor_copy(totT[:].rearrange("p e t -> p t e"), ps[:, 256:512].rearrange("p (t e) -> p t e", e=NE)))
                link(dve.tensor_tensor_scan(incl[:].rearrange("p e t -> p (e t)"), firsts[:].rearrange("p e t -> p (e t)"),
                                            totT[:].rearrange("p e t -> p (e t)"), 0.0, ALU.mult, ALU.add))
                link(TT(excl[:], incl[:], totT[:], ALU.subtract))
                link(TS(cnt[:], incl[:, :, NT - 1], P - 1.0, None, ALU.add))
                link(dve.tensor_copy(cnt_i[:], cnt[:]))
                link(TS(nb_i[:], cnt_i[:], 7, None, ALU.arith_shift_right))
                link(dve.tensor_copy(nb[:], nb_i[:]))
                link(TS(nb[:], nb[:], 1.0, None, ALU.max))
                link(dve.memset(ones[:], 1.0))
                link(dve.tensor_tensor_scan(ends[:], ones[:], nb[:], 0.0, ALU.mult, ALU.add))
                link(TT(starts[:], ends[:], nb[:], ALU.subtract))
                link(TS(starts[:], starts[:], float(P), None, ALU.mult))
                link(TT(dst[:], ps[:, 0:256].rearrange("p (t e) -> p t e", e=NE), excl[:].rearrange("p e t -> p t e"), ALU.add))
                link(TT(dst[:], dst[:], starts[:].unsqueeze(1).to_broadcast([P, NT, NE]), ALU.add))
                for a, x in enumerate((first, second)):
                    link(TT(tmp[:], dst[:], x[:], ALU.mult))
                    link(dve.tensor_reduce(dest_f[:, a], tmp[:], AX.X, ALU.add))
                dve.tensor_copy(dest[:], dest_f[:]).then_inc(dest_ok, 1)
                link(TT(over[:], ends[:].unsqueeze(1).to_broadcast([P, NB, NE]), over_last(blocks[:], NE), ALU.is_le))
                link(dve.tensor_reduce(be[:], over[:], AX.X, ALU.add))
                link(TS(be[:], be[:], NE - 1.0, None, ALU.min))
                link(dve.tensor_copy(plan[:, NB:2 * NB], be[:]))
                link(TS(plan[:, 0:NB], plan[:, NB:2 * NB], 1, None, ALU.bitwise_and))
                link(TS(be[:], be[:], 1.0, 16.0, ALU.add, ALU.mult))
                link(dve.tensor_copy(plan[:, NB:2 * NB], be[:]))
                link(TS(ends[:], ends[:], 1.0, None, ALU.add))
                dve.wait_ge(dest_ok, 1)
                dve.tensor_copy(plan[:, 2 * NB:], ends[:]).then_inc(plan_ok, 1)


FF = 512
KF = FF // P


def experts(nc, xn_rows, row_tok, plan_in, dest_in, tokens_in, w_gate, w_up, w_down, ident_in, y_rows):
    RING = 6
    NPC = 12
    with ExitStack() as stack:
        at = Place(nc, stack, "moe")
        ident = at.sb("ident", [P, P])
        dest = at.sb("dest", [P, 2, NT], I32)
        tokens = at.sb("tokens", [P, NT], I32)
        rows_b = at.sb("rows_b", [NB, P], I32)
        rows_f = at.sb("rows_f", [NB, P])
        rows = at.sb("rows", [P, NB], I32)
        plan = at.sb("plan", [P, 2 * NB + NE], I32)
        idx = [at.sb(f"idx{i}", [P, 1], I32) for i in range(2)]
        wg = at.sb("wg", [P, 2, KD, FF])
        wu = at.sb("wu", [P, 2, KD, FF])
        wd = at.sb("wd", [P, 2, KF, D])
        x = at.sb("x", [P, 2, D])
        wh = at.sb("wh", [P, RING, 2, FF], F32R)
        wl = at.sb("wl", [P, RING, 2, FF], F32R)
        xh = at.sb("xh", [P, 2, KD, P], F32R)
        xl = at.sb("xl", [P, 2, KD, P], F32R)
        sg = at.sb("sg", [P, FF])
        gg = at.sb("gg", [P, FF])
        hh = at.sb("hh", [P, FF])
        hTh = at.sb("hTh", [P, 2, KF, P], F32R)
        hTl = at.sb("hTl", [P, 2, KF, P], F32R)
        y = at.sb("y", [P, 2, D])
        psT = [at.ps(f"psT{i}", (P, 4, P)) for i in range(2)]
        psG, psU, psH = at.ps("psG"), at.ps("psU"), at.ps("psH")
        psY = at.ps("psY", (P, 2, HALF))
        consts_in = at.sem("consts_in")
        scattered, rows_in, rows_f_ok, rows_ps, rows_ok = (at.sem(n) for n in ("scattered", "rows_in", "rows_f_ok", "rows_ps", "rows_ok"))
        wg_in, wu_in, wd_in = at.sem("wg_in"), at.sem("wu_in"), at.sem("wd_in")
        s = {n: at.sem(n) for n in "idx_ok xT_ps xh_ok xl_ok sg_ok gg_ok hh_ok hT_ps hTh_ok hTl_ok y_ps y_ok".split()}
        x_in = [at.sem(f"x_in{i}") for i in range(2)]
        y_out = [at.sem(f"y_out{i}") for i in range(2)]
        wh_ok = at.sem("wh_ok")
        wl_ok = at.sem("wl_ok")
        w_used = at.sem("w_used")

        def later(t, n=1):
            return not isinstance(t, int) or t >= n

        def done(eng, name, t, n=1, per=1):
            if eng in (nc.sync, nc.gpsimd):
                at.hold(eng, s[name], t * per + n)
            else:
                eng.wait_ge(s[name], t * per + n)

        def inside(t):
            return not isinstance(t, int) or t < NB

        def piece(t, n):
            if isinstance(t, int):
                return t * NPC + n - (0 if t == 0 else 4 if t < NB else NPC)
            return t * NPC + (n - 4)

        def ring(t, n):
            m = piece(t, n) if isinstance(t, int) else NPC + n - 4
            return m % RING

        def multiplied(eng, t, n):
            eng.wait_ge(w_used, piece(t, n) + 1)

        def raw(n, slot):
            if n < 8:
                return (wg, wu)[n // 4][:, bass.ds(slot, 1), n % 4 * 2:n % 4 * 2 + 2, :].rearrange("p a k n -> p (a k) n")
            return wd[:, bass.ds(slot, 1), n - 8, :].rearrange("p a (k n) -> p (a k) n", k=2)

        def slot_of(eng, t):
            return eng.value_load(plan[0:1, bass.ds(t, 1)], min_val=0, max_val=1)

        def blocks_of(eng, body):
            body(0, 0)
            body(1, 1)
            with eng.Fori(1, NB // 2 - 1) as pair:
                body(pair * 2, 0)
                body(pair * 2 + 1, 1)
            for t in range(NB // 2 * 2 - 2, NB):
                body(t, t % 2)

        with nc.Block() as block:
            @block.sync
            def _(sp):
                sp.dma_start(dest[:].rearrange("p a t -> p (a t)"), dest_in).then_inc(consts_in, 16)
                sp.dma_start(tokens[:], tokens_in).then_inc(consts_in, 16)
                sp.dma_start(plan[:], plan_in).then_inc(consts_in, 16)
                sp.dma_start(ident[:], ident_in).then_inc(consts_in, 16)

                def load(e, slot):
                    if later(e, 2):
                        end = sp.value_load(plan[0:1, bass.ds(e + (2 * NB - 2), 1)], min_val=1, max_val=NB + 1)
                        at.hold(sp, s["y_ps"], end)
                    for dst, src, w_in in ((wg, w_gate, wg_in), (wu, w_up, wu_in), (wd, w_down, wd_in)):
                        if later(e):
                            at.hold(sp, w_in, e * 16)
                        sp.dma_start(dst[:, slot], src[0, bass.ds(e, 1)].rearrange("a (k p) n -> p (a k) n", p=P)).then_inc(w_in, 16)

                sp.wait_ge(consts_in, 64)
                load(0, 0)
                load(1, 1)
                with sp.Fori(1, NE // 2) as pair:
                    load(pair * 2, 0)
                    load(pair * 2 + 1, 1)

            @block.gpsimd
            def _(pool):
                pool.wait_ge(consts_in, 64)
                for t in range(NT):
                    for a in range(2):
                        pool.indirect_dma_start(row_tok, bass.IndirectOffsetOnAxis(ap=dest[:, a, t:t + 1], axis=0),
                                                tokens[:, t:t + 1], None).then_inc(scattered, 16)
                pool.wait_ge(scattered, 2 * NT * 16)
                pool.dma_start(rows_b[:], row_tok.rearrange("(b p) o -> b (p o)", p=P)).then_inc(rows_in, 16)

                def gather(t, b):
                    done(pool, "idx_ok", t)
                    if later(t, 2):
                        done(pool, "xT_ps", t - 2, 2, 2)
                    pool.indirect_dma_start(x[:, b], None, xn_rows, bass.IndirectOffsetOnAxis(ap=idx[b][:], axis=0)).then_inc(x_in[b], 16)

                def store(t, b):
                    done(pool, "y_ok", t)
                    pool.dma_start(y_rows[bass.ds(t * P, P), :], y[:, b]).then_inc(y_out[b], 16)

                for t in range(3):
                    gather(t, t % 2)

                def tile(t, b):
                    if inside(t + 3):
                        gather(t + 3, 1 - b)
                    if later(t):
                        store(t - 1, 1 - b)

                blocks_of(pool, tile)
                store(NB - 1, (NB - 1) % 2)
                for b in range(2):
                    pool.wait_ge(y_out[b], (NB + 1 - b) // 2 * 16)

            @block.scalar
            def _(act):
                act.wait_ge(consts_in, 64)

                def high(t, n, slot, have):
                    if n in (0, 4, 8):
                        act.wait_ge((wg_in, wu_in, wd_in)[n // 4], have)
                    if later(piece(t, n), RING):
                        act.wait_ge(w_used, piece(t, n) - RING + 1)
                    act.activation(wh[:, ring(t, n)], raw(n, slot), ACT.Copy).then_inc(wh_ok, 1)

                def which(t):
                    return slot_of(act, t), act.value_load(plan[0:1, bass.ds(t + NB, 1)], min_val=16, max_val=NE * 16)

                def take_x(t, b):
                    if later(t, 2):
                        multiplied(act, t - 2, 7)
                    for i in range(2):
                        done(act, "xT_ps", t, i + 1, 2)
                        act.activation(xh[:, b, i * 4:(i + 1) * 4], psT[i][:], ACT.Copy).then_inc(s["xh_ok"], 1)

                def evac_y(t, b):
                    done(act, "y_ps", t, 2)
                    if later(t, 2):
                        act.wait_ge(y_out[b], (t - b) * 8)
                    act.activation(y[:, b], psY[:].rearrange("p a n -> p (a n)"), ACT.Copy).then_inc(s["y_ok"], 1)

                def take_h(t, b):
                    done(act, "hT_ps", t)
                    if later(t, 2):
                        done(act, "y_ps", t - 2, 2)
                    act.activation(hTh[:, b], psH[:].rearrange("p (k t) -> p k t", k=KF), ACT.Copy).then_inc(s["hTh_ok"], 1)

                def tile(t, b):
                    multiplied(act, t, 3)
                    if later(t):
                        done(act, "gg_ok", t - 1)
                    act.activation(sg[:], psG[:], ACT.Sigmoid).then_inc(s["sg_ok"], 1)
                    if later(t):
                        slot, have = which(t - 1)
                        for n in range(8, NPC):
                            high(t, n, slot, have)
                    if inside(t + 1):
                        slot, have = which(t + 1)
                        high(t + 1, 0, slot, have)
                        take_x(t + 1, 1 - b)
                        for n in range(1, 5):
                            high(t + 1, n, slot, have)
                    if later(t):
                        evac_y(t - 1, 1 - b)
                    if inside(t + 1):
                        high(t + 1, 5, slot, have)
                    take_h(t, b)
                    if inside(t + 1):
                        for n in range(6, 8):
                            high(t + 1, n, slot, have)

                take_x(0, 0)
                slot, have = which(0)
                for n in range(8):
                    high(0, n, slot, have)
                blocks_of(act, tile)
                slot, have = which(NB - 1)
                for n in range(8, NPC):
                    high(NB, n, slot, have)
                evac_y(NB - 1, (NB - 1) % 2)

            @block.vector
            def _(dve):
                dve.wait_ge(consts_in, 64)
                dve.wait_ge(rows_in, 16)
                dve.tensor_copy(rows_f[:], rows_b[:]).then_inc(rows_f_ok, 1)
                dve.wait_ge(rows_ps, 1)
                dve.tensor_copy(rows[:], psH[:, 0:NB]).then_inc(rows_ok, 1)
                dve.wait_ge(rows_ok, 1)

                def low(t, n, slot):
                    dve.wait_ge(wh_ok, piece(t, n) + 1)
                    dve.tensor_tensor(wl[:, ring(t, n)], raw(n, slot), wh[:, ring(t, n)].bitcast(F32), ALU.subtract).then_inc(wl_ok, 1)

                def index(t, b):
                    if later(t, 2):
                        dve.wait_ge(x_in[b], (t - b) * 8)
                    dve.tensor_copy(idx[b][:], rows[:, bass.ds(t, 1)]).then_inc(s["idx_ok"], 1)

                def take_x(t, b):
                    for i in range(2):
                        done(dve, "xh_ok", t, i + 1, 2)
                        dve.tensor_tensor(xl[:, b, i * 4:(i + 1) * 4], psT[i][:], xh[:, b, i * 4:(i + 1) * 4].bitcast(F32),
                                          ALU.subtract).then_inc(s["xl_ok"], 1)

                def take_h(t, b):
                    done(dve, "hTh_ok", t)
                    dve.tensor_tensor(hTl[:, b], psH[:].rearrange("p (k t) -> p k t", k=KF), hTh[:, b].bitcast(F32),
                                      ALU.subtract).then_inc(s["hTl_ok"], 1)

                def tile(t, b):
                    done(dve, "sg_ok", t)
                    if later(t):
                        done(dve, "hh_ok", t - 1)
                    dve.tensor_tensor(gg[:], psG[:], sg[:], ALU.mult).then_inc(s["gg_ok"], 1)
                    if inside(t + 3):
                        index(t + 3, 1 - b)
                    if later(t):
                        slot = slot_of(dve, t - 1)
                        for n in range(8, NPC):
                            low(t, n, slot)
                    done(dve, "gg_ok", t)
                    multiplied(dve, t, 7)
                    if later(t):
                        done(dve, "hT_ps", t - 1)
                    dve.tensor_tensor(hh[:], psU[:], gg[:], ALU.mult).then_inc(s["hh_ok"], 1)
                    if inside(t + 1):
                        slot = slot_of(dve, t + 1)
                        low(t + 1, 0, slot)
                        take_x(t + 1, 1 - b)
                        for n in range(1, 6):
                            low(t + 1, n, slot)
                    take_h(t, b)
                    if inside(t + 1):
                        for n in range(6, 8):
                            low(t + 1, n, slot)

                index(0, 0)
                index(1, 1)
                index(2, 0)
                take_x(0, 0)
                slot = slot_of(dve, 0)
                for n in range(8):
                    low(0, n, slot)
                blocks_of(dve, tile)
                slot = slot_of(dve, NB - 1)
                for n in range(8, NPC):
                    low(NB, n, slot)

            @block.tensor
            def _(pe):
                pe.sem_inc(s["y_ps"], 1)
                pe.wait_ge(consts_in, 64)
                pe.wait_ge(rows_f_ok, 1)
                pe.transpose(psH[:, 0:NB], rows_f[:], ident[0:NB, 0:NB]).then_inc(rows_ps, 1)

                def transpose_x(t, b):
                    pe.wait_ge(x_in[b], (t - b + 2) * 8)
                    for i in range(2):
                        if later(t):
                            done(pe, "xl_ok", t - 1, i + 1, 2)
                        for j in range(4):
                            last = pe.transpose(psT[i][:, j], x[:, b, (i * 4 + j) * P:(i * 4 + j + 1) * P], ident[:])
                        last.then_inc(s["xT_ps"], 1)

                def three(out, left, b, k, r, j, start, stop):
                    hi, lo = left
                    pe.matmul(out, hi[:, b, k], wh[:, r, j], start=start, stop=False)
                    pe.matmul(out, hi[:, b, k], wl[:, r, j], start=False, stop=False)
                    return pe.matmul(out, lo[:, b, k], wh[:, r, j], start=False, stop=stop)

                def up(t, b):
                    done(pe, "xl_ok", t, 2, 2)
                    for m, (ps, free) in enumerate(((psG, "gg_ok"), (psU, "hh_ok"))):
                        if later(t):
                            done(pe, free, t - 1)
                        for i in range(4):
                            n = m * 4 + i
                            pe.wait_ge(wl_ok, piece(t, n) + 1)
                            for j in range(2):
                                k = i * 2 + j
                                last = three(ps[:], (xh, xl), b, k, ring(t, n), j, k == 0, k == KD - 1)
                            last.then_inc(w_used, 1)

                def down(t, b):
                    done(pe, "hTl_ok", t)
                    if later(t):
                        done(pe, "y_ok", t - 1)
                    for k in range(KF):
                        pe.wait_ge(wl_ok, piece(t + 1, 8 + k) + 1)
                        for j in range(2):
                            last = three(psY[:, j], (hTh, hTl), b, k, ring(t + 1, 8 + k), j, k == 0, k == KF - 1)
                        last.then_inc(s["y_ps"] if k == KF - 1 else w_used, 1)

                def turn_h(t, b):
                    done(pe, "hh_ok", t)
                    if later(t):
                        done(pe, "hTl_ok", t - 1)
                    for k in range(KF):
                        last = pe.transpose(psH[:, k * P:(k + 1) * P], hh[:, k * P:(k + 1) * P], ident[:])
                        if k == 0 and later(t):
                            last.then_inc(w_used, 1)
                    last.then_inc(s["hT_ps"], 1)

                def tile(t, b):
                    up(t, b)
                    if inside(t + 1):
                        transpose_x(t + 1, 1 - b)
                    if later(t):
                        down(t - 1, 1 - b)
                    turn_h(t, b)

                transpose_x(0, 0)
                blocks_of(pe, tile)
                down(NB - 1, (NB - 1) % 2)


PD = 256
KP = PD // P


def embed(nc, h1, y_rows, dest_in, wgt_in, p_in, ple_proj, ple_norm, ple_gate, ident_in, out):
    NW = KD + KP
    NS = 4
    with ExitStack() as stack:
        at = Place(nc, stack, "ple")
        ident = at.sb("ident", [P, P])
        gain = at.sb("gain", [P, D])
        eps = at.sb("eps", [P, 1])
        dest = at.sb("dest", [P, 2, NT], I32)
        wgt = at.sb("wgt", [P, 2, NT])
        idx = [[at.sb(f"idx{i}{a}", [P, 1], I32) for a in range(2)] for i in range(2)]
        wraw = at.sb("wraw", [P, NS, D])
        whi = at.sb("whi", [P, NW, D], F32R)
        wlo = at.sb("wlo", [P, NW, D], F32R)
        h = at.sb("h", [P, NS, D])
        y = at.sb("y", [P, 2, 2, D])
        pp = at.sb("pp", [P, NS, PD])
        ahi = at.sb("ahi", [P, 2, NW, P], F32R)
        alo = at.sb("alo", [P, 2, NW, P], F32R)
        sq = at.sb("sq", [P, D])
        ss, lnm, rs = (at.sb(n, [P, 2]) for n in ("ss", "lnm", "rs"))
        ple = at.sb("ple", [P, 2, D])
        sg = at.sb("sg", [P, 2, D])
        psT = [at.ps(f"psT{i}", (P, 4, P)) for i in range(2)]
        psP = at.ps("psP", (P, KP, P))
        psG = at.ps("psG", (P, 2, HALF))
        psE = at.ps("psE", (P, 2, HALF))
        consts_in, gain_in, eps_set = at.sem("consts_in"), at.sem("gain_in"), at.sem("eps_set")
        w_in = [at.sem(f"w_in{i}") for i in range(NS)]
        whi_ok, wlo_ok = at.sem("whi_ok"), at.sem("wlo_ok")
        h_in, p_sem, stored = ([at.sem(f"{n}{i}") for i in range(NS)] for n in ("h_in", "p_in", "stored"))
        y_in = [at.sem(f"y_in{i}") for i in range(2)]
        idx_ok = at.sem("idx_ok")
        ha_ok = at.sem("ha_ok")
        hb_ok = at.sem("hb_ok")
        pT_ps = at.sem("pT_ps")
        aT_ps = at.sem("aT_ps")
        phi_ok, plo_ok = at.sem("phi_ok"), at.sem("plo_ok")
        ahi_ok, alo_ok = at.sem("ahi_ok"), at.sem("alo_ok")
        e_ps = at.sem("e_ps")
        g_ps = at.sem("g_ps")
        sq_ok, lnm_ok, rs_ok = at.sem("sq_ok"), at.sem("lnm_ok"), at.sem("rs_ok")
        ple_ok = at.sem("ple_ok")
        sg_ok = at.sem("sg_ok")
        sp_ok = at.sem("sp_ok")
        o_ok = at.sem("o_ok")

        def later(t, n=1):
            return not isinstance(t, int) or t >= n

        def inside(t):
            return not isinstance(t, int) or t < NT

        def used(t, slots, u):
            return (t - u % slots + slots) * (16 // slots)

        def steps(eng, body):
            for u in range(4):
                body(u, u)
            with eng.Fori(1, NT // 4 - 1) as g:
                for u in range(4):
                    body(g * 4 + u, u)
            for u in range(4):
                body(NT - 4 + u, u)

        with nc.Block() as block:
            @block.sync
            def _(sp):
                sp.dma_start(ident[:], ident_in).then_inc(consts_in, 16)
                sp.dma_start(dest[:].rearrange("p a t -> p (a t)"), dest_in).then_inc(consts_in, 16)
                sp.dma_start(wgt[:].rearrange("p a t -> p (a t)"), wgt_in).then_inc(consts_in, 16)

                def load(t, u):
                    v = u % NS
                    if later(t, NS):
                        at.hold(sp, stored[v], used(t - NS, NS, v))
                        at.hold(sp, pT_ps, t - NS + 1)
                    sp.dma_start(pp[:, v], p_in[bass.ds(t * P, P), :]).then_inc(p_sem[v], 16)
                    sp.dma_start(h[:, v], h1[bass.ds(t * P, P), :]).then_inc(h_in[v], 16)

                load(0, 0)
                load(1, 1)
                for k in range(NW):
                    if k >= NS:
                        sp.wait_ge(whi_ok, k - NS + 1)
                        sp.wait_ge(wlo_ok, k - NS + 1)
                    src = ple_proj[k * P:(k + 1) * P] if k < KP else ple_gate[(k - KP) * P:(k - KP + 1) * P]
                    sp.dma_start(wraw[:, k % NS], src).then_inc(w_in[k % NS], 16)
                sp.dma_start(gain[:], ple_norm.broadcast_to([P, D])).then_inc(gain_in, 16)
                load(2, 2)

                def step(t, u):
                    if inside(t + 3):
                        load(t + 3, u + 3)
                    at.hold(sp, o_ok, t + 1)
                    sp.dma_start(out[bass.ds(t * P, P), :], h[:, u % NS]).then_inc(stored[u % NS], 16)

                steps(sp, step)
                for v in range(NS):
                    sp.wait_ge(stored[v], NT // NS * 16)

            @block.gpsimd
            def _(pool):
                pool.wait_ge(consts_in, 48)

                def gather(t, u):
                    b = u % 2
                    at.hold(pool, idx_ok, (t + 1) * 2)
                    if later(t, 2):
                        at.hold(pool, hb_ok, t - 1)
                    for a in range(2):
                        pool.indirect_dma_start(y[:, b, a], None, y_rows, bass.IndirectOffsetOnAxis(ap=idx[b][a][:], axis=0)).then_inc(y_in[b], 16)

                for t in range(3):
                    gather(t, t)

                def step(t, u):
                    b = u % 2
                    if inside(t + 3):
                        gather(t + 3, u + 3)
                    pool.wait_ge(ple_ok, t + 1)
                    pool.wait_ge(sg_ok, t + 1)
                    pool.tensor_tensor(ple[:, b], ple[:, b], sg[:, b], ALU.mult).then_inc(sp_ok, 1)

                steps(pool, step)

            @block.scalar
            def _(act):
                def split_w(k):
                    act.wait_ge(w_in[k % NS], 16 * (k // NS + 1))
                    act.activation(whi[:, k], wraw[:, k % NS], ACT.Copy).then_inc(whi_ok, 1)

                def front(t, u):
                    b = u % 2
                    act.wait_ge(pT_ps, t + 1)
                    if later(t, 2):
                        act.wait_ge(g_ps, t - 1)
                    act.activation(ahi[:, b, 0:KP], psP[:], ACT.Copy).then_inc(phi_ok, 1)
                    for i in range(2):
                        act.wait_ge(aT_ps, t * 2 + i + 1)
                        act.activation(ahi[:, b, KP + i * 4:KP + (i + 1) * 4], psT[i][:], ACT.Copy).then_inc(ahi_ok, 1)

                def step(t, u):
                    b = u % 2
                    if inside(t + 1):
                        front(t + 1, u + 1)
                    act.wait_ge(e_ps, t + 1)
                    if later(t, 2):
                        act.wait_ge(ple_ok, t - 1)
                    if later(t):
                        act.wait_ge(sq_ok, t)
                    act.activation(sq[:], psE[:].rearrange("p a n -> p (a n)"), ACT.Square, accum_out=ss[:, b:b + 1]).then_inc(sq_ok, 1)
                    act.wait_ge(sq_ok, t + 1)
                    act.activation(lnm[:, b:b + 1], ss[:, b:b + 1], ACT.Ln, bias=eps[:], scale=1.0 / D).then_inc(lnm_ok, 1)
                    act.wait_ge(lnm_ok, t + 1)
                    act.activation(rs[:, b:b + 1], lnm[:, b:b + 1], ACT.Exp, scale=-0.5).then_inc(rs_ok, 1)
                    act.wait_ge(g_ps, t + 1)
                    if later(t, 2):
                        act.wait_ge(sp_ok, t - 1)
                    act.activation(sg[:, b], psG[:].rearrange("p a n -> p (a n)"), ACT.Sigmoid).then_inc(sg_ok, 1)

                act.wait_ge(eps_set, 1)
                for k in range(NW):
                    split_w(k)
                    if k == 0:
                        front(0, 0)
                steps(act, step)

            @block.vector
            def _(dve):
                dve.memset(eps[:], EPS).then_inc(eps_set, 1)
                dve.wait_ge(consts_in, 48)

                def index(t, u):
                    if later(t, 2):
                        dve.wait_ge(y_in[u % 2], used(t - 2, 2, u) * 2)
                    for a in range(2):
                        dve.tensor_copy(idx[u % 2][a][:], dest[:, a, bass.ds(t, 1)]).then_inc(idx_ok, 1)

                def split_w(k):
                    dve.wait_ge(whi_ok, k + 1)
                    dve.tensor_tensor(wlo[:, k], wraw[:, k % NS], whi[:, k].bitcast(F32), ALU.subtract).then_inc(wlo_ok, 1)

                def add(t, u):
                    b, v = u % 2, u % NS
                    dve.wait_ge(h_in[v], used(t, NS, u))
                    dve.wait_ge(y_in[b], used(t, 2, u) * 2)
                    dve.scalar_tensor_tensor(h[:, v], y[:, b, 0], wgt[:, 0, bass.ds(t, 1)], h[:, v], ALU.mult, ALU.add).then_inc(ha_ok, 1)
                    dve.wait_ge(ha_ok, t + 1)
                    dve.scalar_tensor_tensor(h[:, v], y[:, b, 1], wgt[:, 1, bass.ds(t, 1)], h[:, v], ALU.mult, ALU.add).then_inc(hb_ok, 1)

                def split(t, u):
                    b = u % 2
                    dve.wait_ge(phi_ok, t + 1)
                    dve.tensor_tensor(alo[:, b, 0:KP], psP[:], ahi[:, b, 0:KP].bitcast(F32), ALU.subtract).then_inc(plo_ok, 1)
                    for i in range(2):
                        dve.wait_ge(ahi_ok, t * 2 + i + 1)
                        cut = slice(KP + i * 4, KP + (i + 1) * 4)
                        dve.tensor_tensor(alo[:, b, cut], psT[i][:], ahi[:, b, cut].bitcast(F32), ALU.subtract).then_inc(alo_ok, 1)

                def finish(t, u):
                    b, v = u % 2, u % NS
                    dve.wait_ge(sp_ok, t + 1)
                    dve.tensor_tensor(h[:, v], h[:, v], ple[:, b], ALU.add).then_inc(o_ok, 1)

                def step(t, u):
                    b = u % 2
                    if inside(t + 1):
                        split(t + 1, u + 1)
                    if inside(t + 2):
                        add(t + 2, u + 2)
                    if inside(t + 4):
                        index(t + 4, u + 4)
                    if later(t):
                        finish(t - 1, u + 3)
                    dve.wait_ge(rs_ok, t + 1)
                    if later(t, 2):
                        dve.wait_ge(o_ok, t - 1)
                    dve.scalar_tensor_tensor(ple[:, b], psE[:].rearrange("p a n -> p (a n)"), rs[:, b:b + 1], gain[:],
                                             ALU.mult, ALU.mult).then_inc(ple_ok, 1)

                index(0, 0)
                index(1, 1)
                add(0, 0)
                index(2, 2)
                split_w(0)
                split(0, 0)
                for k in range(1, NW):
                    split_w(k)
                    if k == 3:
                        add(1, 1)
                        index(3, 3)
                dve.wait_ge(gain_in, 16)
                steps(dve, step)
                finish(NT - 1, NT - 1)

            @block.tensor
            def _(pe):
                pe.wait_ge(consts_in, 48)

                def front(t, u):
                    pe.wait_ge(p_sem[u % NS], used(t, NS, u))
                    if later(t):
                        pe.wait_ge(plo_ok, t)
                    for j in range(KP):
                        last = pe.transpose(psP[:, j], pp[:, u % NS, j * P:(j + 1) * P], ident[:])
                    last.then_inc(pT_ps, 1)
                    pe.wait_ge(hb_ok, t + 1)
                    for i in range(2):
                        if later(t):
                            pe.wait_ge(alo_ok, t * 2 - 1 + i)
                        for j in range(4):
                            last = pe.transpose(psT[i][:, j], h[:, u % NS, (i * 4 + j) * P:(i * 4 + j + 1) * P], ident[:])
                        last.then_inc(aT_ps, 1)

                def step(t, u):
                    b = u % 2
                    first = isinstance(t, int) and t == 0
                    if inside(t + 1):
                        front(t + 1, u + 1)
                    pe.wait_ge(plo_ok, t + 1)
                    for ps, k0, k1, done, free in ((psE, 0, KP, e_ps, ple_ok), (psG, KP, NW, g_ps, sg_ok)):
                        if k0:
                            pe.wait_ge(alo_ok, t * 2 + 2)
                        if later(t):
                            pe.wait_ge(free, t)
                        for k in range(k0, k1):
                            if first:
                                pe.wait_ge(wlo_ok, k + 1)
                            for n in range(2):
                                cut = slice(n * HALF, (n + 1) * HALF)
                                for i, (l, r) in enumerate(((ahi, whi), (ahi, wlo), (alo, whi))):
                                    last = pe.matmul(ps[:, n], l[:, b, k], r[:, k, cut], start=(k == k0 and i == 0),
                                                     stop=(k == k1 - 1 and i == 2))
                        last.then_inc(done, 1)

                front(0, 0)
                steps(pe, step)


def build(nc, a, out):
    def scratch(name, shape, dt=F32):
        return nc.dram_tensor(name, list(shape), dt, kind="Internal").ap()

    hgrn_q, hgrn_f, hgrn_k = (scratch(f"hgrn_{n}", (HW, S)) for n in "qfk")
    tok = scratch("tok", (S, 5 * HW))
    mix = scratch("mix", (S, D))
    h1 = scratch("h1", (S, D))
    xn_rows = scratch("xn_rows", (S + 1, D))
    logits = scratch("logits", (P, NT * NE))
    row_tok = scratch("row_tok", (NROW, 1), I32)
    dest = scratch("dest", (P, 2 * NT), I32)
    wgt = scratch("wgt", (P, 2 * NT))
    plan = scratch("plan", (P, 2 * NB + NE), I32)
    y_rows = scratch("y_rows", (NROW, D))
    x, ident = a["x"].rearrange("a s d -> (a s) d"), a["ident"]

    project_in(nc, x, a["mix_norm"], a["w_in"][0], ident, hgrn_q, hgrn_f, hgrn_k, tok)
    recurrence(nc, hgrn_q, hgrn_f, hgrn_k, tok, a["hgrn_lb"], a["hgrn_out_norm"], ident, a["masks"], a["resets"], mix)
    attention(nc, tok, a["q_norm"], a["k_norm"], a["lam_q1"], a["lam_k1"], a["lam_q2"], a["lam_k2"], a["diff_subln"],
              ident, a["causal"], mix)
    project_out(nc, mix, x, a["w_out"][0], a["ffn_norm"], a["w_router"], ident, h1, xn_rows, logits)
    route(nc, logits, a["below"], a["upper"], a["firsts"], a["blocks"], row_tok, dest, wgt, plan)
    experts(nc, xn_rows, row_tok, plan, dest, a["tokens"], a["w_gate"], a["w_up"], a["w_down"], ident, y_rows)
    embed(nc, h1, y_rows, dest, wgt, a["p"].rearrange("a b s d -> (a b s) d"), a["ple_proj"][0], a["ple_norm"],
          a["ple_gate"][0], ident, out.rearrange("a s d -> (a s) d"))


def shape_constants():
    import numpy as np

    s, t = np.meshgrid(np.arange(P), np.arange(P), indexing="ij")
    masks = np.zeros((P, LV, P), np.int32)
    for i, half in enumerate((CH, *HALVES)):
        masks[:, i] = (s // (2 * half) == t // (2 * half)) & (s // half % 2 == 0) & (t // half % 2 == 1)
    base = HALVES[-1]
    masks[:, LV - 1] = (s // base == t // base) & (s <= t)
    resets = np.ones((P, NH * P // CH, CH), np.float32)
    resets[:, :, 0] = 0
    upper = np.stack([s < t, np.ones((P, P), bool)], 1).astype(np.float32)
    firsts = np.ones((P, NE, NT), np.float32)
    firsts[:, :, 0] = 0
    j = np.arange(GE)
    return {
        "ident": np.eye(P, dtype=np.float32),
        "causal": np.where(t > s, -1e30, 0.0).astype(np.float32),
        "masks": masks,
        "resets": resets.reshape(P, NH * P),
        "below": np.tile((j[None, :] < j[:, None]).astype(np.float32), (P, 1, 1)),
        "upper": upper,
        "firsts": firsts,
        "blocks": np.tile(np.arange(NB, dtype=np.float32), (P, 1)),
        "tokens": (np.arange(NT)[None, :] * P + np.arange(P)[:, None]).astype(np.int32),
    }


INPUTS = ("x p mix_norm w_in hgrn_lb hgrn_out_norm q_norm k_norm lam_q1 lam_k1 lam_q2 lam_k2 diff_subln w_out "
          "ffn_norm w_router w_gate w_up w_down ple_proj ple_norm ple_gate").split()


def kernel(**inputs):
    import numpy as np
    import concourse.bacc as bacc
    from concourse.bass_utils import run_bass_kernel_spmd

    nc = bacc.Bacc("TRN2", target_bir_lowering=False, num_devices=1)
    arrays = {n: np.ascontiguousarray(inputs[n]) for n in INPUTS} | shape_constants()
    aps = {n: nc.dram_tensor(n, v.shape, mybir.dt.from_np(v.dtype), kind="ExternalInput").ap() for n, v in arrays.items()}
    out = nc.dram_tensor("out", (1, S, D), F32, kind="ExternalOutput").ap()
    build(nc, aps, out)
    return run_bass_kernel_spmd(nc, [arrays], core_ids=[0]).results[0]["out"]
```
